# Optimizing a Trainium2 kernel written in Bass

```python
import jax, jax.numpy as jnp
from jax import lax
import numpy as np

D_MODEL = 1024
BATCH = 1
SEQ = 256
DEPTH = 2

CHUNK = 64
N_MIXERS = 2
N_A_LAYERS = (DEPTH + 1) // 2
N_B_LAYERS = DEPTH // 2
N_VRES = max(N_B_LAYERS - 1, 0)
PLE_DIM = 256
D_FF = 2816
RMS_EPS = 1e-6
GMLP_BLOCK = 128
GMLP_WIDTH = 2 * D_MODEL
GMLP_GROUPS = 8
GMLP_GROUP_DIM = GMLP_WIDTH // GMLP_GROUPS
LN_EPS = 1e-5
RWKV_HEAD_DIM = 64
RWKV_HEADS = D_MODEL // RWKV_HEAD_DIM
DECAY_LORA = 64
AAA_LORA = 64
MV_LORA = 32
GATE_LORA = 160
GN_EPS = 64e-5


def rms_norm(x, g):
    xf = x.astype(jnp.float32)
    y = xf * lax.rsqrt(jnp.mean(xf * xf, axis=-1, keepdims=True) + RMS_EPS)
    return (y * g.astype(jnp.float32)).astype(x.dtype)

def swiglu(x, w13, w2):
    gate, up = jnp.split(x @ w13, 2, axis=-1)
    return (jax.nn.silu(gate) * up) @ w2

def gmlp_mixer(h, w_in, b_in, v_gain, w_s, b_s, w_out):
    B, S, _ = h.shape
    z = jax.nn.gelu(h @ w_in + b_in)
    u, v = jnp.split(z, 2, axis=-1)
    vf = v.astype(jnp.float32)
    mean = jnp.mean(vf, axis=-1, keepdims=True)
    var = jnp.mean(jnp.square(vf - mean), axis=-1, keepdims=True)
    v = ((vf - mean) * lax.rsqrt(var + LN_EPS) * v_gain.astype(jnp.float32)).astype(h.dtype)
    nb = S // GMLP_BLOCK
    v = v.reshape(B, nb, GMLP_BLOCK, GMLP_GROUPS, GMLP_GROUP_DIM)
    u = u.reshape(B, nb, GMLP_BLOCK, GMLP_GROUPS, GMLP_GROUP_DIM)
    cidx = jnp.arange(GMLP_BLOCK) // CHUNK
    mask = cidx[None, :] <= cidx[:, None]
    ws = jnp.where(mask[None], w_s, jnp.zeros_like(w_s))
    s = jnp.einsum('gij,bcjgd->bcigd', ws, v) + b_s.T[None, None, :, :, None]
    y = (u * s).reshape(B, S, GMLP_WIDTH)
    return y @ w_out

def wkv7_scan(r, w, k, v, a, b):
    B, S, H, N = r.shape

    def step(state, inp):
        r_t, w_t, k_t, v_t, a_t, b_t = inp
        sa = jnp.einsum('bhij,bhj->bhi', state, a_t)
        state = (state * w_t[:, :, None, :] + sa[..., None] * b_t[:, :, None, :]
                 + v_t[..., None] * k_t[:, :, None, :])
        y_t = jnp.einsum('bhij,bhj->bhi', state, r_t)
        return state, y_t

    xs = tuple(jnp.moveaxis(t, 1, 0) for t in (r, w, k, v, a, b))
    state0 = jnp.zeros((B, H, N, N), jnp.float32)
    _, ys = lax.scan(step, state0, xs)
    return jnp.moveaxis(ys, 0, 1)

def rwkv7_mixer(h, v_first, vres, mu, w_in, w0, w1, w2, a0, a1, a2, g1, g2,
                k_k, k_a, r_k, lnx, w_out):
    B, S, D = h.shape
    H, N = RWKV_HEADS, RWKV_HEAD_DIM
    f32 = jnp.float32
    dx = jnp.pad(h, ((0, 0), (1, 0), (0, 0)))[:, :-1] - h
    x_rkv = h[:, :, None, :] + dx[:, :, None, :] * mu[:3]
    rkv = jnp.einsum('bsnd,nde->bsne', x_rkv, w_in)
    r, k, v = rkv[:, :, 0], rkv[:, :, 1], rkv[:, :, 2]
    xw = h + dx * mu[3]
    xa = h + dx * mu[4]
    xg = h + dx * mu[5]
    zw = (w0 + jnp.tanh(xw @ w1) @ w2).astype(f32)
    decay = jnp.exp(-jnp.exp(-jax.nn.softplus(-zw) - 0.5))
    a = jax.nn.sigmoid(a0 + (xa @ a1) @ a2)
    g = jax.nn.sigmoid(xg @ g1) @ g2

    def heads(t):
        return t.reshape(B, S, H, N).astype(f32)

    kk = heads(k * k_k)
    kk = kk / jnp.maximum(jnp.sqrt(jnp.sum(kk * kk, axis=-1, keepdims=True)), 1e-12)
    k = k * (1.0 + (a - 1.0) * k_a)
    if vres is None:
        v_first = v
    else:
        v0, v1, v2 = vres
        xv = h + dx * mu[2]
        v = v + (v_first - v) * jax.nn.sigmoid(v0 + (xv @ v1) @ v2)
    rh, kh, vh, ah = heads(r), heads(k), heads(v), heads(a)
    y = wkv7_scan(rh, heads(decay), kh, vh, -kk, kk * ah)
    mean = jnp.mean(y, axis=-1, keepdims=True)
    var = jnp.mean(jnp.square(y - mean), axis=-1, keepdims=True)
    yn = ((y - mean) * lax.rsqrt(var + GN_EPS)).reshape(B, S, D)
    yn = yn * lnx[0].astype(f32) + lnx[1].astype(f32)
    bonus = (jnp.sum(rh * kh * r_k.astype(f32), axis=-1, keepdims=True) * vh).reshape(B, S, D)
    out = ((yn + bonus).astype(h.dtype) * g) @ w_out
    return out, v_first

def first_inputs(seed: int = 0) -> dict:
    key = jax.random.key(seed)
    ks = iter(jax.random.split(key, 40))
    f32 = jnp.float32

    def nrm(shape, scale):
        return jax.random.normal(next(ks), shape, f32) * scale

    def gain(shape):
        return 1.0 + nrm(shape, 0.05)

    D, E2, E = D_MODEL, 2 * GMLP_WIDTH, GMLP_WIDTH
    NA, NB = N_A_LAYERS, N_B_LAYERS
    return {
        "x": nrm((BATCH, SEQ, D), 1.0),
        "p": nrm((DEPTH, BATCH, SEQ, PLE_DIM), 1.0),
        "norm_g": gain((DEPTH, 8, D)),
        "ffn_w13": nrm((DEPTH, 2, D, 2 * D_FF), D ** -0.5),
        "ffn_w2": nrm((DEPTH, 2, D_FF, D), D_FF ** -0.5),
        "ple_w_gate": nrm((DEPTH, D, D), D ** -0.5),
        "ple_w_proj": nrm((DEPTH, PLE_DIM, D), PLE_DIM ** -0.5),
        "a_w_in": nrm((NA, D, E2), D ** -0.5),
        "a_b_in": nrm((NA, E2), 0.02),
        "a_v_gain": gain((NA, E)),
        "a_w_s": nrm((NA, GMLP_GROUPS, GMLP_BLOCK, GMLP_BLOCK), GMLP_BLOCK ** -0.5),
        "a_b_s": gain((NA, GMLP_GROUPS, GMLP_BLOCK)),
        "a_w_out": nrm((NA, E, D), E ** -0.5),
        "b_mu": jax.random.uniform(next(ks), (NB, 6, D), f32),
        "b_w_in": nrm((NB, 3, D, D), D ** -0.5),
        "b_w0": nrm((NB, D), 0.5),
        "b_w1": nrm((NB, D, DECAY_LORA), D ** -0.5),
        "b_w2": nrm((NB, DECAY_LORA, D), DECAY_LORA ** -0.5),
        "b_a0": nrm((NB, D), 0.1),
        "b_a1": nrm((NB, D, AAA_LORA), D ** -0.5),
        "b_a2": nrm((NB, AAA_LORA, D), AAA_LORA ** -0.5),
        "b_g1": nrm((NB, D, GATE_LORA), D ** -0.5),
        "b_g2": nrm((NB, GATE_LORA, D), GATE_LORA ** -0.5),
        "b_k_k": 0.85 + nrm((NB, D), 0.05),
        "b_k_a": gain((NB, D)),
        "b_r_k": nrm((NB, RWKV_HEADS, RWKV_HEAD_DIM), 0.1),
        "b_lnx": jnp.stack([gain((NB, D)), nrm((NB, D), 0.02)], axis=1),
        "b_w_out": nrm((NB, D, D), D ** -0.5),
        "b_v0": nrm((N_VRES, D), 0.1),
        "b_v1": nrm((N_VRES, D, MV_LORA), D ** -0.5),
        "b_v2": nrm((N_VRES, MV_LORA, D), MV_LORA ** -0.5),
    }

def first_block(x, p, norm_g, ffn_w13, ffn_w2, ple_w_gate, ple_w_proj,
              a_w_in, a_b_in, a_v_gain, a_w_s, a_b_s, a_w_out,
              b_mu, b_w_in, b_w0, b_w1, b_w2, b_a0, b_a1, b_a2, b_g1, b_g2,
              b_k_k, b_k_a, b_r_k, b_lnx, b_w_out, b_v0, b_v1, b_v2):
    h = x
    v_first = None
    for i in range(DEPTH):
        g = norm_g[i]
        h = h + 0.5 * rms_norm(swiglu(rms_norm(h, g[0]), ffn_w13[i, 0], ffn_w2[i, 0]), g[1])
        hn = rms_norm(h, g[2])
        j = i // N_MIXERS
        if i % N_MIXERS == 0:
            m = gmlp_mixer(hn, a_w_in[j], a_b_in[j], a_v_gain[j], a_w_s[j], a_b_s[j], a_w_out[j])
        else:
            vres = None if v_first is None else (b_v0[j - 1], b_v1[j - 1], b_v2[j - 1])
            m, v_first = rwkv7_mixer(hn, v_first, vres, b_mu[j], b_w_in[j], b_w0[j], b_w1[j],
                                     b_w2[j], b_a0[j], b_a1[j], b_a2[j], b_g1[j], b_g2[j],
                                     b_k_k[j], b_k_a[j], b_r_k[j], b_lnx[j], b_w_out[j])
        h = h + rms_norm(m, g[3])
        h = h + 0.5 * rms_norm(swiglu(rms_norm(h, g[4]), ffn_w13[i, 1], ffn_w2[i, 1]), g[5])
        gate = jax.nn.sigmoid(rms_norm(h, g[6]) @ ple_w_gate[i])
        h = h + rms_norm(gate * (p[i] @ ple_w_proj[i]), g[7])
    return h


N_MIXERS_2 = 3
D_HEAD = 64
ROT_DIM = D_HEAD // 4
ROPE_THETA = 500000.0
NEG_INF = -1e30
N_NORMS = 8
A_PAIRS = ((128, 1), (512, 4), (2048, 16))
A_HEADS = 8
A_BLOCK = 64
B_HEADS = 16
B_KV_HEADS = 4
B_RADIUS = 128
B_BLOCK = 128
C_HEADS = 16
GRID_W = 64
NA_ROWS = 8
NA_COLS = 16
NA_QC = 16
NA_KC = 2 * NA_QC


def rms_norm_2(x, g):
    x32 = x.astype(jnp.float32)
    y = x32 * lax.rsqrt(jnp.mean(x32 * x32, axis=-1, keepdims=True) + RMS_EPS)
    return (y * g.astype(jnp.float32)).astype(x.dtype)

def swiglu_2(x, wi, wo):
    gate, up = jnp.split(x @ wi, 2, axis=-1)
    return (jax.nn.silu(gate) * up) @ wo

def rope_tables(seq):
    pos = jnp.arange(seq, dtype=jnp.float32)
    inv = ROPE_THETA ** (-jnp.arange(0, ROT_DIM, 2, dtype=jnp.float32) / ROT_DIM)
    ang = pos[:, None] * inv[None, :]
    return jnp.cos(ang), jnp.sin(ang)

def apply_rope(x, cos, sin):
    shape = (cos.shape[0],) + (1,) * (x.ndim - 3) + (cos.shape[1],)
    c = cos.reshape(shape).astype(x.dtype)
    s = sin.reshape(shape).astype(x.dtype)
    half = ROT_DIM // 2
    x1, x2, rest = x[..., :half], x[..., half:ROT_DIM], x[..., ROT_DIM:]
    return jnp.concatenate([x1 * c - x2 * s, x2 * c + x1 * s, rest], axis=-1)

def band_attention(q, k, v, radius, block, sink=None):
    n, length, hk, grp, dh = q.shape
    nb = -(-length // block)
    pad = nb * block - length
    qb = jnp.pad(q, ((0, 0), (0, pad), (0, 0), (0, 0), (0, 0))).reshape(n, nb, block, hk, grp, dh)

    def three_blocks(a):
        a = jnp.pad(a, ((0, 0), (block, pad + block), (0, 0), (0, 0))).reshape(n, nb + 2, block, hk, dh)
        return jnp.concatenate([a[:, :-2], a[:, 1:-1], a[:, 2:]], axis=2)

    kb, vb = three_blocks(k), three_blocks(v)
    qpos = jnp.arange(nb * block).reshape(nb, block)
    kpos = jnp.arange(nb)[:, None] * block - block + jnp.arange(3 * block)[None, :]
    rel = kpos[:, None, :] - qpos[:, :, None]
    valid = (jnp.abs(rel) <= radius) & (kpos[:, None, :] >= 0) & (kpos[:, None, :] < length)
    s = jnp.einsum('nbqhgd,nbkhd->nbhgqk', qb, kb).astype(jnp.float32) * (dh ** -0.5)
    s = jnp.where(valid[None, :, None, None], s, NEG_INF)
    m = jnp.max(s, axis=-1)
    if sink is not None:
        sk = sink.astype(jnp.float32)[None, None, :, :, None]
        m = jnp.maximum(m, sk)
    pr = jnp.exp(s - m[..., None])
    den = jnp.sum(pr, axis=-1)
    if sink is not None:
        den = den + jnp.exp(sk - m)
    o = jnp.einsum('nbhgqk,nbkhd->nbqhgd', pr.astype(v.dtype), vb)
    o = o / jnp.transpose(den, (0, 1, 4, 2, 3))[..., None]
    lse = jnp.transpose(m + jnp.log(den), (0, 1, 4, 2, 3))
    o = o.reshape(n, nb * block, hk, grp, dh)[:, :length].astype(q.dtype)
    lse = lse.reshape(n, nb * block, hk, grp)[:, :length]
    return o, lse

def dilated_mixer(h, wqkv, wo, cos, sin):
    b, s, _ = h.shape
    ng = len(A_PAIRS)
    qkv = (h @ wqkv).reshape(b, s, 3, ng, A_HEADS, D_HEAD)
    q = apply_rope(qkv[:, :, 0], cos, sin)
    k = apply_rope(qkv[:, :, 1], cos, sin)
    v = qkv[:, :, 2]
    outs, lses = [], []
    for g, (window, dil) in enumerate(A_PAIRS):
        sub = s // dil

        def to_sub(a):
            return a.reshape(b, sub, dil, A_HEADS, D_HEAD).transpose(0, 2, 1, 3, 4).reshape(b * dil, sub, A_HEADS, D_HEAD)

        o, lse = band_attention(to_sub(q[:, :, g])[:, :, :, None], to_sub(k[:, :, g]), to_sub(v[:, :, g]),
                                window // (2 * dil), A_BLOCK)
        o = o[:, :, :, 0].reshape(b, dil, sub, A_HEADS, D_HEAD).transpose(0, 2, 1, 3, 4).reshape(b, s, A_HEADS, D_HEAD)
        lse = lse[..., 0].reshape(b, dil, sub, A_HEADS).transpose(0, 2, 1, 3).reshape(b, s, A_HEADS)
        outs.append(o)
        lses.append(lse)
    wts = jax.nn.softmax(jnp.stack(lses, axis=0), axis=0)
    o = jnp.sum(wts[..., None] * jnp.stack(outs, axis=0).astype(jnp.float32), axis=0).astype(h.dtype)
    return o.reshape(b, s, A_HEADS * D_HEAD) @ wo

def window_gqa_mixer(h, wqkv, wo, sink, cos, sin):
    b, s, _ = h.shape
    grp = B_HEADS // B_KV_HEADS
    qkv = h @ wqkv
    q = qkv[..., :B_HEADS * D_HEAD].reshape(b, s, B_HEADS, D_HEAD)
    k = qkv[..., B_HEADS * D_HEAD:(B_HEADS + B_KV_HEADS) * D_HEAD].reshape(b, s, B_KV_HEADS, D_HEAD)
    v = qkv[..., (B_HEADS + B_KV_HEADS) * D_HEAD:].reshape(b, s, B_KV_HEADS, D_HEAD)
    q = apply_rope(q, cos, sin).reshape(b, s, B_KV_HEADS, grp, D_HEAD)
    k = apply_rope(k, cos, sin)
    o, _ = band_attention(q, k, v, B_RADIUS, B_BLOCK, sink.reshape(B_KV_HEADS, grp))
    return o.reshape(b, s, B_HEADS * D_HEAD) @ wo

def neighbourhood_mixer(h, wqkv, wo, rpb):
    b, s, _ = h.shape
    rows = s // GRID_W
    kh = min(NA_ROWS, rows)
    ncb = GRID_W // NA_QC
    qkv = (h @ wqkv).reshape(b, rows, GRID_W, 3, C_HEADS, D_HEAD)
    q = qkv[:, :, :, 0] * (D_HEAD ** -0.5)
    k, v = qkv[:, :, :, 1], qkv[:, :, :, 2]
    qcol = np.arange(GRID_W).reshape(ncb, NA_QC)
    kstart = np.clip(np.arange(ncb) * NA_QC - NA_COLS // 2, 0, GRID_W - NA_KC)
    kcol = kstart[:, None] + np.arange(NA_KC)[None, :]
    cstart = np.clip(qcol - NA_COLS // 2, 0, GRID_W - NA_COLS)
    col_valid = (kcol[:, None, :] >= cstart[..., None]) & (kcol[:, None, :] < cstart[..., None] + NA_COLS)
    dc_idx = np.clip(kcol[:, None, :] - qcol[:, :, None] + NA_COLS - 1, 0, 2 * NA_COLS - 2)
    kc = k[:, :, kcol]
    vc = v[:, :, kcol]

    def row_fn(r):
        rs = jnp.clip(r - kh // 2, 0, rows - kh)
        kw = lax.dynamic_slice_in_dim(kc, rs, kh, axis=1)
        vw = lax.dynamic_slice_in_dim(vc, rs, kh, axis=1)
        qr = lax.dynamic_index_in_dim(q, r, axis=1, keepdims=False).reshape(b, ncb, NA_QC, C_HEADS, D_HEAD)
        sc = jnp.einsum('bnqhd,bjnchd->bhnqjc', qr, kw).astype(jnp.float32)
        dr_idx = rs + jnp.arange(kh) - r + NA_ROWS - 1
        bias = rpb[:, dr_idx][:, :, dc_idx].transpose(0, 2, 3, 1, 4)
        sc = sc + bias.astype(jnp.float32)[None]
        sc = jnp.where(col_valid[None, None, :, :, None, :], sc, NEG_INF)
        pr = jax.nn.softmax(sc.reshape(b, C_HEADS, ncb, NA_QC, kh * NA_KC), axis=-1)
        pr = pr.reshape(b, C_HEADS, ncb, NA_QC, kh, NA_KC).astype(vw.dtype)
        o = jnp.einsum('bhnqjc,bjnchd->bnqhd', pr, vw)
        return o.reshape(b, GRID_W, C_HEADS * D_HEAD)

    out = lax.map(row_fn, jnp.arange(rows))
    return out.transpose(1, 0, 2, 3).reshape(b, s, C_HEADS * D_HEAD) @ wo

def second_inputs(seed: int = 0) -> dict:
    key = jax.random.key(seed)
    ks = jax.random.split(key, 16)
    f32 = jnp.float32

    def dense(k, shape, fan_in):
        return jax.random.normal(k, shape, f32) * (fan_in ** -0.5)

    n_a = len(range(0, DEPTH, N_MIXERS_2))
    n_b = len(range(1, DEPTH, N_MIXERS_2))
    n_c = len(range(2, DEPTH, N_MIXERS_2))
    ng = len(A_PAIRS)
    return {
        "x": jax.random.normal(ks[0], (BATCH, SEQ, D_MODEL), f32),
        "p": jax.random.normal(ks[1], (DEPTH, BATCH, SEQ, PLE_DIM), f32),
        "norm_g": 1.0 + 0.02 * jax.random.normal(ks[2], (DEPTH, N_NORMS, D_MODEL), f32),
        "ffn_wi": dense(ks[3], (DEPTH, 2, D_MODEL, 2 * D_FF), D_MODEL),
        "ffn_wo": dense(ks[4], (DEPTH, 2, D_FF, D_MODEL), D_FF),
        "ple_proj": dense(ks[5], (DEPTH, PLE_DIM, D_MODEL), PLE_DIM),
        "ple_gate": dense(ks[6], (DEPTH, D_MODEL, D_MODEL), D_MODEL),
        "a_wqkv": dense(ks[7], (n_a, D_MODEL, 3 * ng * A_HEADS * D_HEAD), D_MODEL),
        "a_wo": dense(ks[8], (n_a, A_HEADS * D_HEAD, D_MODEL), A_HEADS * D_HEAD),
        "b_wqkv": dense(ks[9], (n_b, D_MODEL, (B_HEADS + 2 * B_KV_HEADS) * D_HEAD), D_MODEL),
        "b_wo": dense(ks[10], (n_b, B_HEADS * D_HEAD, D_MODEL), B_HEADS * D_HEAD),
        "b_sink": 0.5 * jax.random.normal(ks[11], (n_b, B_HEADS), f32),
        "c_wqkv": dense(ks[12], (n_c, D_MODEL, 3 * C_HEADS * D_HEAD), D_MODEL),
        "c_wo": dense(ks[13], (n_c, C_HEADS * D_HEAD, D_MODEL), C_HEADS * D_HEAD),
        "c_rpb": 0.1 * jax.random.normal(ks[14], (n_c, C_HEADS, 2 * NA_ROWS - 1, 2 * NA_COLS - 1), f32),
    }

def second_block(x, p, norm_g, ffn_wi, ffn_wo, ple_proj, ple_gate, a_wqkv, a_wo,
              b_wqkv, b_wo, b_sink, c_wqkv, c_wo, c_rpb):
    cos, sin = rope_tables(x.shape[1])
    h = x
    for i in range(DEPTH):
        g = norm_g[i]
        h = h + 0.5 * rms_norm_2(swiglu_2(rms_norm_2(h, g[0]), ffn_wi[i, 0], ffn_wo[i, 0]), g[1])
        hn = rms_norm_2(h, g[2])
        mixer, j = i % N_MIXERS_2, i // N_MIXERS_2
        if mixer == 0:
            y = dilated_mixer(hn, a_wqkv[j], a_wo[j], cos, sin)
        elif mixer == 1:
            y = window_gqa_mixer(hn, b_wqkv[j], b_wo[j], b_sink[j], cos, sin)
        else:
            y = neighbourhood_mixer(hn, c_wqkv[j], c_wo[j], c_rpb[j])
        h = h + rms_norm_2(y, g[3])
        h = h + 0.5 * rms_norm_2(swiglu_2(rms_norm_2(h, g[4]), ffn_wi[i, 1], ffn_wo[i, 1]), g[5])
        e = p[i].astype(h.dtype) @ ple_proj[i]
        gate = jax.nn.sigmoid(rms_norm_2(h, g[6]) @ ple_gate[i])
        h = h + rms_norm_2(e * gate, g[7])
    return h


def setup_inputs(seed=0):
    out = dict(first_inputs(seed))
    for name, value in second_inputs(seed + 1).items():
        if name != "x":
            out[name + "_2"] = value
    return out


def reference(
    x, p, norm_g, ffn_w13, ffn_w2, ple_w_gate, ple_w_proj, a_w_in, a_b_in, a_v_gain, a_w_s,
    a_b_s, a_w_out, b_mu, b_w_in, b_w0, b_w1, b_w2, b_a0, b_a1, b_a2, b_g1, b_g2, b_k_k, b_k_a,
    b_r_k, b_lnx, b_w_out, b_v0, b_v1, b_v2, p_2, norm_g_2, ffn_wi_2, ffn_wo_2, ple_proj_2,
    ple_gate_2, a_wqkv_2, a_wo_2, b_wqkv_2, b_wo_2, b_sink_2, c_wqkv_2, c_wo_2, c_rpb_2,
):
    x = first_block(
        x, p, norm_g, ffn_w13, ffn_w2, ple_w_gate, ple_w_proj, a_w_in, a_b_in, a_v_gain, a_w_s,
        a_b_s, a_w_out, b_mu, b_w_in, b_w0, b_w1, b_w2, b_a0, b_a1, b_a2, b_g1, b_g2, b_k_k,
        b_k_a, b_r_k, b_lnx, b_w_out, b_v0, b_v1, b_v2,
    )
    return second_block(
        x, p_2, norm_g_2, ffn_wi_2, ffn_wo_2, ple_proj_2, ple_gate_2, a_wqkv_2, a_wo_2,
        b_wqkv_2, b_wo_2, b_sink_2, c_wqkv_2, c_wo_2, c_rpb_2,
    )


_drawn_inputs = setup_inputs


def setup_inputs(seed=0):
    import zlib

    import numpy as np

    out = dict(_drawn_inputs(seed))
    spreads = {}
    factors = {'b_a0': 2.72, 'b_k_k': 8.0, 'b_sink_2': 8.0}
    for name, (base, spread) in spreads.items():
        noise = np.random.default_rng([zlib.crc32(name.encode()), seed]).standard_normal(out[name].shape)
        drawn = base * np.exp(spread * noise) if base else spread * noise
        out[name] = __import__('jax').numpy.asarray(drawn.astype(out[name].dtype))
    for name, factor in factors.items():
        out[name] = (out[name] * factor).astype(out[name].dtype)
    return out
```

```python
from contextlib import ExitStack

import numpy as np

import concourse.bass as bass
from concourse import mybir

F32 = mybir.dt.float32
F32R = mybir.dt.float32r
BF16 = mybir.dt.bfloat16
ALU = mybir.AluOpType
ACT = mybir.ActivationFunctionType
AX = mybir.AxisListType.X

P = 128
T = 2
S = T * P
D = 1024
DK = D // P
FF = 2816
FB = 256
PD = 256
RMS_EPS = 1e-6
LN_EPS = 1e-5
GN_EPS = 64e-5
NH = 16
HD = 64
EXP_HALF = 0.6065306597126334

BASE = 16512
CHUNK = 2048
N_RAW = 4
N_W = 3


class Written:

    def matmul(self, *a, **k):
        return lambda e: e.matmul(*a, **k)

    def transpose(self, *a, **k):
        return lambda e: e.transpose(*a, **k)

    def activation(self, *a, **k):
        return lambda e: e.activation(*a, **k)

    def tensor_tensor(self, *a, **k):
        return lambda e: e.tensor_tensor(*a, **k)

    def tensor_scalar(self, *a, **k):
        return lambda e: e.tensor_scalar(*a, **k)

    def scalar_tensor_tensor(self, *a, **k):
        return lambda e: e.scalar_tensor_tensor(*a, **k)

    def tensor_reduce(self, *a, **k):
        return lambda e: e.tensor_reduce(*a, **k)

    def tensor_copy(self, *a, **k):
        return lambda e: e.tensor_copy(*a, **k)

    def reciprocal(self, *a, **k):
        return lambda e: e.reciprocal(*a, **k)

    def memset(self, *a, **k):
        return lambda e: e.memset(*a, **k)


class Queue:

    def __init__(self, sem):
        self.sem, self.count, self.ops, self.passed = sem, 0, [], {}

    def wait(self, *marks):
        for m in marks:
            if m is None:
                continue
            if isinstance(m, list):
                self.wait(*m)
                continue
            sem, value = m
            if self.passed.get(id(sem), 0) < value:
                self.passed[id(sem)] = value
                self.ops.append(lambda e, sem=sem, value=value: e.wait_ge(sem, value))

    def put(self, fn, *marks, mark=True):
        self.wait(*marks)
        fn = fn(Written())
        if not mark:
            self.ops.append(fn)
            return None
        self.count += 1
        self.ops.append(lambda e, sem=self.sem: fn(e).then_inc(sem, 1))
        return (self.sem, self.count)

    def run(self, e):
        for op in self.ops:
            op(e)


class Loads:

    def __init__(self, sem):
        self.sem, self.count = sem, 0

    def put(self, queue, out, in_, *marks):
        queue.wait(*marks)
        self.count += 16
        queue.ops.append(lambda e, sem=self.sem: e.dma_start(out, in_).then_inc(sem, 16))
        return (self.sem, self.count)


class Ring:

    def __init__(self, places):
        self.places, self.free, self.at, self.out = places, [[] for _ in places], 0, set()

    def take(self):
        n = self.at % len(self.places)
        self.at += 1
        assert n not in self.out
        self.out.add(n)
        return n, self.places[n], self.free[n]

    def give(self, n, *marks):
        self.free[n] = list(marks)
        self.out.discard(n)


def constants():
    i = np.arange(S)
    rel = i[None, :] - i[:, None]
    far = np.float32(-1e30)
    dil = np.stack([np.where(np.abs(rel) <= 64, 0, far), np.where(rel % 4 == 0, 0, far),
                    np.where(rel % 16 == 0, 0, far)], axis=1)
    dil = dil.reshape(T, P, 3 * S).transpose(1, 0, 2)
    gqa = np.where(np.abs(rel) <= 128, 0, far).reshape(T, P, S).transpose(1, 0, 2)
    inv = np.float32(500000.0) ** (-np.arange(0, 16, 2, dtype=np.float32) / np.float32(16))
    ang = np.arange(S, dtype=np.float32)[:, None] * inv[None, :].astype(np.float32)
    rope = np.stack([np.cos(ang), np.sin(ang)], axis=1).astype(np.float32)
    rope = rope.reshape(T, P, 2, 8).transpose(1, 2, 0, 3)
    a = np.arange(P)
    low = a[None, :] < a[:, None]
    up = a[:, None] < a[None, :]
    upi = a[:, None] <= a[None, :]
    masks = [low, up, upi]
    for k in range(7):
        b = 1 << k
        blk = a // b
        m = (blk[:, None] % 2 == 0) & (blk[None, :] == blk[:, None] + 1)
        masks.append(m | np.eye(P, dtype=bool))
    masks = np.stack(masks, axis=1).astype(np.float32)
    mid = (a[:, None] <= 63).astype(np.float32) * np.ones((1, P), np.float32)
    cum = np.stack([upi - mid, up - mid], axis=1).astype(np.float32)
    ends = np.stack([a >= 64, a <= 63], axis=1).astype(np.float32)
    bf = mybir.dt.np(BF16)
    return {
        "c_ident": np.eye(P, dtype=np.float32),
        "c_identb": np.eye(P, dtype=np.float32).astype(bf),
        "c_dil": dil.astype(bf), "c_gqa": gqa.astype(bf), "c_rope": np.ascontiguousarray(rope),
        "c_masks": masks.astype(bf), "c_cum": np.concatenate([cum.reshape(P, 2 * P), ends], axis=1),
    }


def program(nc, A, out, stages=99):
    ctx = ExitStack()
    plan = []
    with ctx:
        cache = {}

        def named_sem(name):
            if name not in cache:
                cache[name] = ctx.enter_context(nc.semaphore(name))
            return cache[name]

        tensors = {}

        def at(name, offset, shape, dt):
            if name not in tensors:
                tensors[name] = nc.alloc_sbuf_tensor_at(name, shape, dt, offset=BASE + offset)
            return tensors[name]

        banks_t = [ctx.enter_context(nc.psum_tensor(f"bank{i}", [P, 1024], F32)) for i in range(4)]
        queues = emit(nc, A, out, at, banks_t, named_sem, None, plan, stages)
        queues = emit(nc, A, out, at, banks_t, named_sem, list(plan), [], stages)
        block = ctx.enter_context(nc.Block())
        for name, q in queues.items():
            on = {"sp": block.sync, "pe": block.tensor, "v": block.vector,
                  "a": block.scalar, "g": block.gpsimd}[name]
            on(q.run)


def emit(nc, A, out, at, banks_t, sem, plan, listed, stages):
    PE, V, C, G, SP = (Queue(sem(n)) for n in ("s_pe", "s_v", "s_a", "s_g", "s_sp"))

    raw = [at(f"raw{i}", i * 8192, [P, CHUNK], F32) for i in range(N_RAW)]
    o = N_RAW * 8192
    wh = [at(f"wh{i}", o + i * 8192, [P, CHUNK], F32R) for i in range(N_W)]
    o += N_W * 8192
    wl = [at(f"wl{i}", o + i * 8192, [P, CHUNK], F32R) for i in range(N_W)]
    o += N_W * 8192
    XO = o
    XH = at("XH", o, [P, DK, S], F32R)
    XL = at("XL", o + 8192, [P, DK, S], F32R)
    o += 16384
    H = at("H", o, [P, T, D], F32)
    o += 8192
    TO = o
    TMP = at("TMP", o, [P, T, 2, D], F32)
    o += 16384
    BO = o
    bct = [at(f"bc{i}", o + i * 4096, [P, D], F32) for i in range(3)]
    o += 12288
    AO = o
    att = [at(f"att{i}", o + i * 2048, [P, 512], F32) for i in range(3)]
    o += 6144
    JUNK = at("JUNK", o, [P, 1024], BF16)
    o += 2048
    ST = at("ST", o, [P, 512], F32)
    o += 2048
    ident = at("ident", o, [P, P], F32)
    identb = at("identb", o + 512, [P, P], BF16)
    o += 768
    GT = at("GT", o, [P, 2, P], F32)
    o += 1024
    MT = at("MT", o, [P, 64], F32)
    o += 256
    PT = at("PT", o, [P, T, PD], F32)
    PH = at("PH", o + 2048, [P, PD // P, S], F32R)
    PL = at("PL", o + 4096, [P, PD // P, S], F32R)
    o += 6144
    NEG = at("NEG", o, [P, 32], F32)
    o += 128
    EO = o
    AH = at("AH", EO, [P, FF // P, S], F32R)
    AL = at("AL", EO + FF // P * S * 4, [P, FF // P, S], F32R)

    def bank(i):
        return banks_t[i // 2][:, (i % 2) * 512:(i % 2) * 512 + 512]

    pairs = Ring([(bank(0), bank(1)), (bank(2), bank(3)), (bank(4), bank(5))])
    tbanks = Ring([bank(6), bank(7)])
    bc = Ring(bct)
    atts = Ring(att)
    bc_loads = [Loads(sem(f"d_bc{i}")) for i in range(3)]
    raw_loads = [Loads(sem(f"d_raw{i}")) for i in range(N_RAW)]
    once = Loads(sem("d_once"))
    pload = Loads(sem("d_p"))
    stat = [0]
    singles = [0]

    def single(queue, out_, in_, *marks):
        singles[0] += 1
        return Loads(sem(f"d_s{singles[0]}")).put(queue, out_, in_, *marks)


    def cols(n):
        c = stat[0]
        stat[0] += n
        assert stat[0] <= 512
        return ST[:, c:c + n]

    n_used, n_ready = [0], [0]
    done, conv, landed = {}, {}, {}

    def load(j):
        src, shape, _ = plan[j]
        dst = raw[j % N_RAW][:, 0:shape[0] * shape[1]].rearrange("p (k n) -> p k n", k=shape[0])
        if len(src.shape) == 4:
            dst = dst.rearrange("p k (s n) -> p k s n", s=2)
            raw_loads[j % N_RAW].put(SP, dst[:, :, 0, :], src[:, :, 0, :], conv.get(j - N_RAW))
            dst, src = dst[:, :, 1, :], src[:, :, 1, :]
        landed[j] = raw_loads[j % N_RAW].put(SP, dst, src, conv.get(j - N_RAW))

    def convert(j):
        size = plan[j][1][0] * plan[j][1][1]
        r, hi, lo = raw[j % N_RAW], wh[j % N_W], wl[j % N_W]
        a = C.put(lambda e: e.activation(hi[:, 0:size], r[:, 0:size], ACT.Copy),
                  landed[j], done.get(j - N_W))
        v = V.put(lambda e: e.tensor_tensor(lo[:, 0:size], r[:, 0:size], hi[:, 0:size].bitcast(F32),
                                            ALU.subtract), a, landed[j])
        conv[j] = [a, v]
        if j + N_RAW < len(plan):
            load(j + N_RAW)

    def use(src, kc, n):
        j = n_used[0]
        n_used[0] += 1
        listed.append((src, (kc, n), None))
        if plan is None:
            conv[j] = []
        else:
            if j == 0:
                for i in range(min(N_RAW, len(plan))):
                    load(i)
            while n_ready[0] < min(j + N_W, len(plan)):
                convert(n_ready[0])
                n_ready[0] += 1
        hi = wh[j % N_W][:, 0:kc * n].rearrange("p (k n) -> p k n", k=kc)
        lo = wl[j % N_W][:, 0:kc * n].rearrange("p (k n) -> p k n", k=kc)
        return j, hi, lo, conv[j]

    pending = []

    def flush():
        while pending:
            pending.pop(0)()

    def linear(xh, xl, nk, blocks, consume, ready, kc=4):
        tok = None
        for b, (n, src) in enumerate(blocks):
            slot, pair, free = pairs.take()
            for k0 in range(0, nk, kc):
                kn = min(kc, nk - k0)
                j, hi, lo, conv_done = use(src(k0, k0 + kn), kn, n)
                PE.wait(conv_done, free)
                for k in range(k0, k0 + kn):
                    PE.wait(ready[k])
                    for t in range(T):
                        last = k == nk - 1
                        o_ = pair[t][:, 0:n]
                        a_, b_ = xh[:, k, t * P:(t + 1) * P], xl[:, k, t * P:(t + 1) * P]
                        h_, l_ = hi[:, k - k0, :], lo[:, k - k0, :]
                        PE.put(lambda e, o_=o_, a_=a_, h_=h_, s=(k == 0): e.matmul(
                            o_, a_, h_, start=s, stop=False), mark=False)
                        PE.put(lambda e, o_=o_, a_=a_, l_=l_: e.matmul(
                            o_, a_, l_, start=False, stop=False), mark=False)
                        tok = PE.put(lambda e, o_=o_, b_=b_, h_=h_, s=last: e.matmul(
                            o_, b_, h_, start=False, stop=s), mark=(k == k0 + kn - 1 and t == T - 1))
                done[j] = tok
                if k0 == 0:
                    flush()
            later = consume(b, slot, pair, tok)
            if later is not None:
                pending.append(later)
        return tok

    def spread(src, nk, xh, xl, gain, src_done, free):
        ready = []
        for k in range(0, nk, 2):
            slot, b, bfree = tbanks.take()
            n = min(2, nk - k)
            for i in range(n):
                for t in range(T):
                    tok = PE.put(lambda e, i=i, t=t, k=k, b=b: e.transpose(
                        b[:, i * S + t * P:i * S + (t + 1) * P], src(k + i, t), ident[:, :]),
                        bfree, src_done(k + i, t), mark=(i == n - 1 and t == T - 1))
            v = []
            if gain is None:
                bb = b[:, 0:n * S].rearrange("p (k s) -> p k s", k=n)
                a = C.put(lambda e, k=k, n=n, bb=bb: e.activation(xh[:, k:k + n, :], bb, ACT.Copy),
                          tok, free)
                v = V.put(lambda e, k=k, n=n, bb=bb: e.tensor_tensor(
                    xl[:, k:k + n, :], bb, xh[:, k:k + n, :].bitcast(F32), ALU.subtract), a, tok, free)
                ready += [[a, v]] * n
                tbanks.give(slot, a, v)
            else:
                for i in range(n):
                    g = gain[:, k + i:k + i + 1]
                    bb = b[:, i * S:(i + 1) * S]
                    a = C.put(lambda e, k=k + i, g=g, bb=bb: e.activation(
                        xh[:, k, :], bb, ACT.Copy, scale=g), tok, free)
                for i in range(n):
                    g = gain[:, k + i:k + i + 1]
                    bb = b[:, i * S:(i + 1) * S]
                    v = V.put(lambda e, k=k + i, g=g, bb=bb: e.scalar_tensor_tensor(
                        xl[:, k, :], bb, g, xh[:, k, :].bitcast(F32), ALU.mult, ALU.subtract), a, tok, free)
                    ready.append([a, v])
                tbanks.give(slot, a, v)
        return ready

    def rsqrt(x, scale, eps, *marks):
        n = x.shape[-1]
        m = G.put(lambda e: e.tensor_scalar(x, x, scale, eps, ALU.mult, ALU.add), *marks)
        return G.put(lambda e: e.tensor_tensor(x, x, NEG[:, 0:n], ALU.pow), m, neg_done)

    def broadcast(src, n=D):
        slot, b, free = bc.take()
        tok = bc_loads[slot].put(G, b[:, 0:n], src.partition_broadcast(P), free)
        return slot, b, tok

    h_done = [None, None]
    hload = [Loads(sem(f"d_h{t}")) for t in range(T)]
    for t in range(T):
        h_done[t] = hload[t].put(C, H[:, t, :], A["x"][0, t * P:(t + 1) * P, :])
    i_done = once.put(C, ident[:, :], A["c_ident"])
    i_done = once.put(C, identb[:, :], A["c_identb"])
    gs = TMP[:, 0, :, :]
    g_in = once.put(C, gs[:, 0, 0:P], A["norm_g"].rearrange("l n (k p) -> (l n k) p", p=P))
    g_in = once.put(C, gs[:, 0, P:2 * P], A["norm_g_2"].rearrange("l n (k p) -> (l n k) p", p=P))
    g_in = once.put(C, gs[0:48, 0, 2 * P:3 * P], A["b_mu"].rearrange("l n (k p) -> (l n k) p", p=P))
    g_in = once.put(C, gs[48:56, 0, 2 * P:3 * P], A["a_b_s"].rearrange("l g p -> (l g) p"))
    neg_done = V.put(lambda e: e.memset(NEG[:, :], -0.5))
    slot, b, free = tbanks.take()
    for i in range(2):
        PE.put(lambda e, i=i, b=b: e.transpose(b[:, i * P:(i + 1) * P], gs[:, 0, i * P:(i + 1) * P],
                                               ident[:, :]), g_in, mark=False)
    tok = PE.put(lambda e, b=b: e.transpose(b[:, 2 * P:2 * P + 56], gs[0:56, 0, 2 * P:3 * P],
                                            ident[0:56, 0:56]))
    a = C.put(lambda e, b=b: e.activation(GT[:, :, :], b[:, 0:2 * P].rearrange("p (i n) -> p i n", i=2),
                                          ACT.Copy), tok)
    a2 = C.put(lambda e, b=b: e.activation(MT[:, 0:56], b[:, 2 * P:2 * P + 56], ACT.Copy), tok)
    tbanks.give(slot, a2)
    const_done = a2
    V.wait(const_done)
    G.wait(neg_done)

    x_used = [None]
    a_used = [None]
    tmp_used = [tok]

    def gain_cols(block, layer, n):
        c = (layer * 8 + n) * DK
        return GT[:, block, c:c + DK]

    def prenorm(block, layer, n, fine=True):
        ss = cols(T)
        m = [C.put(lambda e, t=t: e.activation(JUNK[:, :], H[:, t, :], ACT.Square,
                                               accum_out=ss[:, t:t + 1]),
                   h_done[t], (C.sem, C.count) if C.count else None) for t in range(T)]
        rs_done = rsqrt(ss, 1.0 / D, RMS_EPS, m[-1])
        ready = spread(lambda k, t: H[:, t, k * P:(k + 1) * P], DK, XH, XL,
                       gain_cols(block, layer, n), lambda k, t: [h_done[t], i_done], x_used[0])
        return ss, rs_done, ready

    def squares(y, ss, *marks):
        return C.put(lambda e: e.activation(JUNK[:, 0:y.shape[-1]], y, ACT.Square, accum_out=ss),
                     *marks, (C.sem, C.count))

    def residual(y, ss, sq, gb, factor, pre, slots):
        slot_b, gbt, gb_done = gb
        sm = cols(T)
        m = V.put(lambda e: e.tensor_tensor(sm, ss[:, 0:T], ss[:, T:2 * T], ALU.add), sq)
        m = rsqrt(sm, pre * pre / D, RMS_EPS, m)
        if pre * factor != 1.0:
            m = G.put(lambda e: e.tensor_scalar(sm, sm, pre * factor, None, ALU.mult), m)
        last = []
        for t in range(T):
            for b in range(2):
                part = H[:, t, b * 512:(b + 1) * 512]
                tmp = TMP[:, t, b, 512:1024]
                v = V.put(lambda e, t=t, b=b, tmp=tmp: e.scalar_tensor_tensor(
                    tmp, y[b][t], sm[:, t:t + 1], gbt[:, b * 512:(b + 1) * 512], ALU.mult, ALU.mult),
                    m, gb_done, tmp_used[0])
                v = V.put(lambda e, part=part, tmp=tmp: e.tensor_tensor(part, part, tmp, ALU.add),
                          v, h_done[t])
                last.append(v)
            h_done[t] = v
        bc.give(slot_b, last[-1])
        for s in slots:
            pairs.give(s, last[-1])
        tmp_used[0] = last[-1]

    def project(xh, xl, nk, w, gain, factor, ready):
        gb = broadcast(gain)
        ss = cols(2 * T)
        y, slots, sq = [None, None], [], []

        def consume(b, slot, pair, tok):
            y[b] = pair
            slots.append(slot)
            for t in range(T):
                sq.append(squares(pair[t], ss[:, b * T + t:b * T + t + 1], tok))

        wv = w.rearrange("(k p) n -> p k n", p=P)
        blocks = [(512, lambda k0, k1, b=b: wv[:, k0:k1, b * 512:(b + 1) * 512]) for b in range(2)]
        last = linear(xh, xl, nk, blocks, consume, ready)
        flush()
        residual(y, ss, sq[-1], gb, factor, 1.0, slots)
        return last

    def ffn(block, layer, i, w13, w2, norm_g):
        rs, rs_done, ready = prenorm(block, layer, 4 * i)
        sc = cols(2 * T)
        m = G.put(lambda e: e.tensor_scalar(sc[:, 0:T], rs, 0.5, None, ALU.mult), rs_done)
        sc_done = G.put(lambda e: e.tensor_tensor(sc[:, T:2 * T], sc[:, 0:T], rs, ALU.mult), m)
        wv = w13.rearrange("(k p) (s n) -> p k s n", p=P, s=2)
        blocks = [(512, lambda k0, k1, b=b: wv[:, k0:k1, :, b * FB:(b + 1) * FB])
                  for b in range(FF // FB)]
        aready = {}

        def consume(b, slot, pair, tok):
            n, th, free = atts.take()
            for t in range(T):
                tt = th[:, t * FB:(t + 1) * FB]
                g_, u_ = pair[t][:, 0:FB], pair[t][:, FB:2 * FB]
                a = C.put(lambda e, tt=tt, g_=g_, t=t: e.activation(
                    tt, g_, ACT.Tanh, scale=sc[:, t:t + 1]), tok, sc_done, free)
                v = V.put(lambda e, tt=tt, g_=g_: e.scalar_tensor_tensor(
                    tt, tt, 1.0, g_, ALU.add, ALU.mult), a, tok)
                v = V.put(lambda e, tt=tt, u_=u_, t=t: e.scalar_tensor_tensor(
                    tt, tt, sc[:, T + t:T + t + 1], u_, ALU.mult, ALU.mult), v, sc_done)
            pairs.give(slot, v)

            def later():
                r = spread(lambda k, t: th[:, t * FB + k * P:t * FB + (k + 1) * P], 2,
                           AH[:, 2 * b:2 * b + 2, :], AL[:, 2 * b:2 * b + 2, :], None,
                           lambda k, t: v, a_used[0])
                atts.give(n, (PE.sem, PE.count))
                aready[2 * b], aready[2 * b + 1] = r

            return later

        x_used[0] = linear(XH, XL, DK, blocks, consume, ready)
        flush()
        a_used[0] = project(AH, AL, FF // P, w2, norm_g[layer, 4 * i + 1], 0.5,
                            [aready[k] for k in range(FF // P)])

    def ple(block, layer, p, w_gate, w_proj, norm_g):
        gb = broadcast(norm_g[layer, 7])
        p_in = pload.put(G, PT[:, :, :], p[layer, 0].rearrange("(t p) n -> p t n", p=P), p_used[0])
        rs, rs_done, ready = prenorm(block, layer, 6)
        hr = cols(T)
        hr_done = G.put(lambda e: e.tensor_scalar(hr, rs, 0.5, None, ALU.mult), rs_done)
        pready = spread(lambda k, t: PT[:, t, k * P:(k + 1) * P], PD // P, PH, PL, None,
                        lambda k, t: [p_in, i_done], p_used[0])
        ss = cols(2 * T)
        y = [[TMP[:, t, b, 0:512] for t in range(T)] for b in range(2)]
        sq = []
        gate = {}
        wg = w_gate[layer].rearrange("(k p) n -> p k n", p=P)
        wp = w_proj[layer].rearrange("(k p) n -> p k n", p=P)

        def consume_gate(b):
            def f(_, slot, pair, tok):
                a = [C.put(lambda e, t=t: e.activation(y[b][t], pair[t], ACT.Tanh,
                                                       scale=hr[:, t:t + 1]), tok, hr_done, tmp_used[0])
                     for t in range(T)]
                pairs.give(slot, a[-1])
                gate[b] = a
            return f

        def consume_e(b):
            def f(_, slot, pair, tok):
                for t in range(T):
                    v = V.put(lambda e, t=t: e.scalar_tensor_tensor(
                        y[b][t], y[b][t], 1.0, pair[t], ALU.add, ALU.mult), tok, gate[b][t])
                    sq.append(squares(y[b][t], ss[:, b * T + t:b * T + t + 1], v))
                pairs.give(slot, v)
            return f

        for b in range(2):
            x_used[0] = linear(XH, XL, DK, [(512, lambda k0, k1: wg[:, k0:k1, b * 512:(b + 1) * 512])],
                               consume_gate(b), ready)
            p_used[0] = linear(PH, PL, PD // P,
                               [(512, lambda k0, k1: wp[:, k0:k1, b * 512:(b + 1) * 512])],
                               consume_e(b), pready)
        residual(y, ss, sq[-1], gb, 1.0, 0.5, [])

    p_used = [None]

    def gmlp():
        bs = MT[:, 48:56]
        U = at("gU", EO + 32768, [P, T, 2048], F32)
        W = at("gW", EO + 32768 + 16384, [P, 8, P], F32)
        yh = at("gYH", EO, [P, 16, S], F32R)
        yl = at("gYL", EO + 16384, [P, 16, S], F32R)
        w_in_done = single(G, U[:, 0, 0:1024].rearrange("p (g j) -> p g j", g=8),
                              A["a_w_s"][0].rearrange("g i j -> i g j"), a_used[0])
        rs, rs_done, ready = prenorm(0, 0, 2)
        for q in range(2):
            slot, b, free = tbanks.take()
            for i in range(4):
                g = 4 * q + i
                tok = PE.put(lambda e, g=g, i=i, b=b: e.transpose(
                    b[:, i * P:(i + 1) * P], U[:, 0, g * P:(g + 1) * P], ident[:, :]),
                    free, w_in_done, mark=(i == 3))
            a = C.put(lambda e, q=q, b=b: e.activation(
                W[:, 4 * q:4 * q + 4, :], b.rearrange("p (g i) -> p g i", g=4), ACT.Copy), tok, a_used[0])
            tbanks.give(slot, a)
        w_done = V.put(lambda e: e.memset(W[64:128, :, 0:64], 0.0), a)
        w_read = tok
        bsrc = A["a_b_in"][0]
        order = [4, 5, 6, 7, 0, 1, 2, 3]
        bcs = {}

        def bias(i):
            c = order[2 * i]
            bcs[i] = broadcast(bsrc[c * 512:c * 512 + 1024])

        bias(0)
        sums = cols(T * 4)
        wv = A["a_w_in"][0].rearrange("(k p) n -> p k n", p=P)
        blocks = [(512, lambda k0, k1, c=c: wv[:, k0:k1, c * 512:(c + 1) * 512]) for c in order]
        vdone, udone = [None] * T, {}
        v_norm = [None] * T

        def layer_norm():
            g0 = broadcast(A["a_v_gain"][0, 0:1024])
            mean = cols(T)
            nmean = cols(T)
            var = cols(2 * T)
            m = V.put(lambda e: e.tensor_reduce(mean, sums.rearrange("p (t b) -> p t b", t=T), AX, ALU.add),
                      vdone[0], vdone[1])
            m = V.put(lambda e: e.tensor_scalar(nmean, mean, -1.0 / 2048, None, ALU.mult), m)
            for t in range(T):
                for a_ in range(2):
                    s_ = C.put(lambda e, t=t, a_=a_: e.activation(
                        JUNK[:, :], TMP[:, t, a_, :], ACT.Square, bias=nmean[:, t:t + 1],
                        accum_out=var[:, a_ * T + t:a_ * T + t + 1]), m, (C.sem, C.count))
            r = cols(T)
            v = V.put(lambda e: e.tensor_tensor(r, var[:, 0:T], var[:, T:2 * T], ALU.add), s_)
            r_done = rsqrt(r, 1.0 / 2048, LN_EPS, v)
            for a_ in range(2):
                gg = g0 if a_ == 0 else broadcast(A["a_v_gain"][0, 1024:2048])
                for t in range(T):
                    x = TMP[:, t, a_, :]
                    v = V.put(lambda e, x=x, t=t: e.tensor_scalar(
                        x, x, nmean[:, t:t + 1], r[:, t:t + 1], ALU.add, ALU.mult), r_done, s_, m)
                    v = V.put(lambda e, x=x, gg=gg: e.tensor_tensor(x, x, gg[1][:, :], ALU.mult), v, gg[2])
                    v_norm[t] = v
                bc.give(gg[0], v)

        def consume(b, slot, pair, tok):
            c = order[b]
            i = b // 2
            bslot, bb, b_done = bcs[i]
            v = None
            for t in range(T):
                n, z, free = atts.take()
                v = V.put(lambda e, t=t, z=z: e.scalar_tensor_tensor(
                    z[:, :], pair[t], rs[:, t:t + 1], bb[:, (b % 2) * 512:(b % 2) * 512 + 512],
                    ALU.mult, ALU.add), tok, rs_done, b_done, free)
                if c >= 4:
                    dst = TMP[:, t, (c - 4) // 2, (c % 2) * 512:(c % 2) * 512 + 512]
                    a = C.put(lambda e, z=z, dst=dst, t=t: e.activation(
                        dst, z[:, :], ACT.Gelu_apprx_tanh, accum_out=sums[:, t * 4 + c - 4:t * 4 + c - 3]),
                        v, tmp_used[0])
                    vdone[t] = a
                else:
                    dst = U[:, t, c * 512:(c + 1) * 512]
                    a = C.put(lambda e, z=z, dst=dst: e.activation(
                        dst, z[:, :], ACT.Gelu_apprx_tanh), v, w_read, a_used[0])
                    udone[(t, c)] = a
                atts.give(n, a)
            pairs.give(slot, v)
            if b % 2 == 1:
                bc.give(bslot, v)
                if i < 3:
                    bias(i + 1)
            if b == 3:
                layer_norm()

        x_used[0] = linear(XH, XL, DK, blocks, consume, ready)
        ydone = {}
        for g2 in range(4):
            slot, pair, free = pairs.take()
            for t in range(T):
                for i in range(2):
                    g = 2 * g2 + i
                    tok = PE.put(lambda e, t=t, g=g, i=i, pair=pair: e.matmul(
                        pair[t][:, i * 256:(i + 1) * 256], W[:, g, :],
                        TMP[:, t, g // 4, (g % 4) * 256:(g % 4) * 256 + 256], start=True, stop=True),
                        free, w_done, v_norm[t])
                for i in range(2):
                    g = 2 * g2 + i
                    u = U[:, t, g * 256:(g + 1) * 256]
                    v = V.put(lambda e, t=t, g=g, i=i, u=u, pair=pair: e.scalar_tensor_tensor(
                        u, pair[t][:, i * 256:(i + 1) * 256], bs[:, g:g + 1], u, ALU.add, ALU.mult),
                        tok, udone[(t, g // 2)])
                    ydone[(t, g)] = v
            pairs.give(slot, v)
        tmp_used[0] = tok
        ready = spread(lambda k, t: U[:, t, k * P:(k + 1) * P], 16, yh, yl, None,
                       lambda k, t: ydone[(t, k // 2)], a_used[0])
        a_used[0] = project(yh, yl, 16, A["a_w_out"][0], A["norm_g"][0, 3], 1.0, ready)


    def rwkv():
        wide = [P, T, D]
        R = at("rR", EO, wide, F32)
        K = at("rK", EO + 8192, wide, F32)
        VV = at("rV", EO + 16384, wide, F32)
        LW = at("rLW", EO + 24576, wide, F32)
        AA = at("rAA", EO + 32768, wide, F32)
        GG = at("rGG", EO + 40960, wide, F32)
        MK = at("rMK", EO + 49152, [P, 10, P], BF16)
        CU = at("rCU", EO + 49152 + 2560, [P, 2 * P + 2], F32)
        SM = at("rSM", EO + 49152 + 2560 + 1056, [P, 256], F32)
        W2 = at("rW2", EO + 49152 + 2560 + 1056 + 1024, [P, D], F32)
        HT = at("rHT", TO, [P, DK, S], F32)
        DX = at("rDX", TO + 8192, [P, DK, S], F32)
        KK = at("rKK", TO, wide, F32)
        TB = at("rTB", TO + 8192, wide, F32)
        nr = A["norm_g"]
        e0 = a_used[0]
        mk_in = single(G, MK[:, :, :], A["c_masks"], e0)
        cu_in = single(G, CU[:, :], A["c_cum"], e0)
        ss = cols(T)
        m = [squares(H[:, t, :], ss[:, t:t + 1], h_done[t]) for t in range(T)]
        rs_done = rsqrt(ss, 1.0 / D, RMS_EPS, m[-1])
        hn = [V.put(lambda e, t=t: e.tensor_scalar(R[:, t, :], H[:, t, :], ss[:, t:t + 1], None, ALU.mult),
                    rs_done, h_done[t], e0) for t in range(T)]
        gain = gain_cols(0, 1, 2)
        hdone = []
        for k in range(0, DK, 2):
            slot, b, free = tbanks.take()
            for i in range(2):
                for t in range(T):
                    tok = PE.put(lambda e, k=k, i=i, t=t, b=b: e.transpose(
                        b[:, i * S + t * P:i * S + (t + 1) * P], R[:, t, (k + i) * P:(k + i + 1) * P],
                        ident[:, :]), free, hn[t], mark=(i == 1 and t == 1))
            for i in range(2):
                a = C.put(lambda e, k=k + i, i=i, b=b: e.activation(
                    HT[:, k, :], b[:, i * S:(i + 1) * S], ACT.Copy, scale=gain[:, k:k + 1]),
                    tok, tmp_used[0])
                hdone.append(a)
            tbanks.give(slot, a)
        ht_read = tok
        v = V.put(lambda e: e.tensor_scalar(DX[:, :, 0:1], HT[:, :, 0:1], -1.0, None, ALU.mult),
                  hdone[-1], tmp_used[0])
        dx = V.put(lambda e: e.tensor_tensor(DX[:, :, 1:S], HT[:, :, 0:S - 1], HT[:, :, 1:S], ALU.subtract),
                   hdone[-1], v)
        LO = at("rLO", EO + 24576, [P, DK, S], F32)
        W1 = at("rW1", EO + 32768, [P, DK, 160], F32)
        lora = {}

        def mix(n, dst, *marks):
            out_ = []
            for k in range(DK):
                out_.append(V.put(lambda e, k=k: e.scalar_tensor_tensor(
                    dst[:, k, :], DX[:, k, :], MT[:, n * DK + k:n * DK + k + 1], HT[:, k, :],
                    ALU.mult, ALU.add), dx, const_done, *marks))
            return out_

        lread, w1read = e0, e0
        TH = at("rTH", AO, [P, 4, S], F32)
        th_done = {}
        att_free = [f for f in atts.free]
        for n, name, width in ((5, "b_g1", 160), (4, "b_a1", 64), (3, "b_w1", 64)):
            w_in = single(G, W1[:, :, 0:width], A[name][0].rearrange("(k p) n -> p k n", p=P), w1read)
            xs = mix(n, LO, lread)
            slot, pair, free = pairs.take()
            for part in range((width + P - 1) // P):
                c0, c1 = part * P, min(width, part * P + P)
                for k in range(DK):
                    tok = PE.put(lambda e, k=k, c0=c0, c1=c1, part=part, pair=pair: e.matmul(
                        pair[part][0:c1 - c0, 0:S], W1[:, k, c0:c1], LO[:, k, :],
                        start=(k == 0), stop=(k == DK - 1)), free, w_in, xs[k], mark=(k == DK - 1))
            lread, w1read = tok, tok
            if n == 5:
                a = C.put(lambda e, pair=pair: e.activation(TH[:, 0, 0:S], pair[0][:, 0:S], ACT.Tanh,
                                                            scale=0.5), tok, *att_free)
                a = C.put(lambda e, pair=pair: e.activation(TH[0:32, 1, 0:S], pair[1][0:32, 0:S], ACT.Tanh,
                                                            scale=0.5), tok)
                v = V.put(lambda e: e.tensor_scalar(TH[:, 0, 0:S], TH[:, 0, 0:S], 1.0, 0.5, ALU.add,
                                                    ALU.mult), a)
                v = V.put(lambda e: e.tensor_scalar(TH[0:32, 1, 0:S], TH[0:32, 1, 0:S], 1.0, 0.5, ALU.add,
                                                    ALU.mult), a)
                th_done[n] = v
            elif n == 4:
                a = C.put(lambda e, pair=pair: e.activation(TH[0:64, 2, 0:S], pair[0][0:64, 0:S], ACT.Copy),
                          tok)
                th_done[n] = a
            else:
                a = C.put(lambda e, pair=pair: e.activation(TH[64:128, 2, 0:S], pair[0][0:64, 0:S], ACT.Tanh),
                          tok)
                th_done[n] = a
            pairs.give(slot, a)

        w2read = e0
        gdone, adone, wdone = {}, {}, {}

        def second(name, parts, evac):
            nonlocal w2read
            w_ins = []
            for i, (p0, p1, blk, r0, r1) in enumerate(parts):
                assert i == 0 or p1 - p0 <= 32
                dst = W2[p0:p1, :] if i == 0 else bc3[p0:p1, :]
                w_ins.append(single(G, dst, A[name][0][r0:r1, :], w2read))
            for b in range(2):
                slot, pair, free = pairs.take()
                for t in range(T):
                    for i, (p0, p1, blk, r0, r1) in enumerate(parts):
                        w_ = W2[p0:p1, b * 512:(b + 1) * 512] if i == 0 else bc3[p0:p1, b * 512:(b + 1) * 512]
                        tok = PE.put(lambda e, t=t, w_=w_, p0=p0, p1=p1, blk=blk, i=i, pair=pair: e.matmul(
                            pair[t], TH[p0:p1, blk, t * P:(t + 1) * P], w_,
                            start=(i == 0), stop=(i == len(parts) - 1)), free, w_ins, list(th_done.values()))
                evac(b, slot, pair, tok)
            w2read = tok

        n3, bc3, free3 = bc.take()
        G.wait(free3)

        def g_evac(b, slot, pair, tok):
            for t in range(T):
                a = C.put(lambda e, t=t, pair=pair: e.activation(GG[:, t, b * 512:(b + 1) * 512], pair[t],
                                                                 ACT.Copy), tok, e0)
            pairs.give(slot, a)
            gdone[0] = a

        second("b_g2", [(0, 128, 0, 0, 128), (0, 32, 1, 128, 160)], g_evac)
        a0b = broadcast(A["b_a0"][0])

        def a_evac(b, slot, pair, tok):
            for t in range(T):
                dst = AA[:, t, b * 512:(b + 1) * 512]
                v = V.put(lambda e, t=t, dst=dst, pair=pair: e.tensor_tensor(
                    dst, pair[t], a0b[1][:, b * 512:(b + 1) * 512], ALU.add), tok, a0b[2], w1read)
                a = C.put(lambda e, dst=dst: e.activation(dst, dst, ACT.Tanh, scale=0.5), v)
                v2 = V.put(lambda e, dst=dst: e.tensor_scalar(dst, dst, 1.0, 0.5, ALU.add, ALU.mult), a)
            pairs.give(slot, v)
            adone[0] = v2

        second("b_a2", [(0, 64, 2, 0, 64)], a_evac)
        bc.give(a0b[0], adone[0])
        w0b = broadcast(A["b_w0"][0])

        def w_evac(b, slot, pair, tok):
            for t in range(T):
                dst = LW[:, t, b * 512:(b + 1) * 512]
                v = V.put(lambda e, t=t, dst=dst, pair=pair: e.tensor_tensor(
                    dst, pair[t], w0b[1][:, b * 512:(b + 1) * 512], ALU.add), tok, w0b[2], lread)
                a = C.put(lambda e, dst=dst: e.activation(dst, dst, ACT.Tanh, scale=0.5), v)
                v2 = V.put(lambda e, dst=dst: e.tensor_scalar(dst, dst, 1.0, -0.5 * EXP_HALF, ALU.add,
                                                              ALU.mult), a)
            pairs.give(slot, v)
            wdone[0] = v2

        second("b_w2", [(64, 128, 2, 0, 64)], w_evac)
        bc.give(w0b[0], wdone[0])
        bc.give(n3, w2read)
        for i in range(3):
            atts.free[i] = [w2read]

        wv = A["b_w_in"][0].rearrange("n (k p) e -> n p k e", p=P)
        rkv_done = {}
        for n, dst in enumerate((R, K, VV)):
            rdy = []
            for k in range(DK):
                s_, x, free = atts.take()
                v0 = V.put(lambda e, k=k, x=x: e.scalar_tensor_tensor(
                    x[:, 0:S], DX[:, k, :], MT[:, n * DK + k:n * DK + k + 1], HT[:, k, :],
                    ALU.mult, ALU.add), dx, free)
                a = C.put(lambda e, k=k, x=x: e.activation(XH[:, k, :], x[:, 0:S], ACT.Copy), v0, x_used[0])
                v = V.put(lambda e, k=k, x=x: e.tensor_tensor(
                    XL[:, k, :], x[:, 0:S], XH[:, k, :].bitcast(F32), ALU.subtract), a, x_used[0])
                atts.give(s_, v)
                rdy.append([a, v])

            def consume(b, slot, pair, tok, dst=dst, n=n):
                for t in range(T):
                    a = C.put(lambda e, t=t: e.activation(dst[:, t, b * 512:(b + 1) * 512], pair[t],
                                                          ACT.Copy), tok, ht_read, e0)
                    rkv_done[(n, b, t)] = a
                pairs.give(slot, a)

            blocks = [(512, lambda k0, k1, b=b, n=n: wv[n][:, k0:k1, b * 512:(b + 1) * 512])
                      for b in range(2)]
            x_used[0] = linear(XH, XL, DK, blocks, consume, rdy)
        rkv = rkv_done[(2, 1, 1)]
        fl = lambda x: x.rearrange("p t (h n) -> p (t h) n", n=HD)

        b1 = broadcast(A["b_k_k"][0])
        b2 = broadcast(A["b_k_a"][0])
        n2, inv = SM[:, 0:32], SM[:, 32:64]
        kkd = []
        for t in range(T):
            v = V.put(lambda e, t=t: e.tensor_tensor(KK[:, t, :], K[:, t, :], b1[1][:, :], ALU.mult),
                      b1[2], rkv, dx, [(V.sem, V.count)])
            v = V.put(lambda e, t=t: e.tensor_tensor(TB[:, t, :], KK[:, t, :], KK[:, t, :], ALU.mult), v)
        v = V.put(lambda e: e.tensor_reduce(n2, fl(TB[:, :, :]), AX, ALU.add), v)
        v = V.put(lambda e: e.tensor_scalar(n2, n2, 1e-24, None, ALU.max), v)
        g = G.put(lambda e: e.tensor_tensor(inv, n2, NEG[:, 0:32], ALU.pow), v)
        kk = V.put(lambda e: e.tensor_tensor(fl(KK[:, :, :]), fl(KK[:, :, :]),
                                             inv.unsqueeze(2).broadcast_to([P, 32, HD]), ALU.mult), g)
        for t in range(T):
            v = V.put(lambda e, t=t: e.scalar_tensor_tensor(
                TB[:, t, :], AA[:, t, :], -1.0, b2[1][:, :], ALU.add, ALU.mult), b2[2], adone[0], kk)
            v = V.put(lambda e, t=t: e.scalar_tensor_tensor(
                K[:, t, :], TB[:, t, :], 1.0, K[:, t, :], ALU.add, ALU.mult), v)
        bc.give(b1[0], v)
        bc.give(b2[0], v)
        kd = v
        bb = V.put(lambda e: e.tensor_tensor(AA[:, :, :], KK[:, :, :], AA[:, :, :], ALU.mult), kd, kk)
        b3 = broadcast(A["b_r_k"][0].rearrange("h n -> (h n)"))
        v = V.put(lambda e: e.tensor_tensor(TB[:, :, :], R[:, :, :], K[:, :, :], ALU.mult), kd)
        for t in range(T):
            v = V.put(lambda e, t=t: e.tensor_tensor(TB[:, t, :], TB[:, t, :], b3[1][:, :], ALU.mult),
                      v, b3[2])
        bon = SM[:, 64:96]
        bon_done = V.put(lambda e: e.tensor_reduce(bon, fl(TB[:, :, :]), AX, ALU.add), v)
        bc.give(b3[0], v)
        tin, tex = CU[:, 0:P], CU[:, P:2 * P]
        scan_in = {}
        for t in range(T):
            for b in range(2):
                slot, pair, free = pairs.take()
                c = slice(b * 512, (b + 1) * 512)
                tok = PE.put(lambda e, t=t, c=c, pair=pair: e.matmul(
                    pair[0], tin, LW[:, t, c], start=True, stop=True), free, cu_in, wdone[0])
                tok2 = PE.put(lambda e, t=t, c=c, pair=pair: e.matmul(
                    pair[1], tex, LW[:, t, c], start=True, stop=True))
                s1, e1, f1 = atts.take()
                s2, e2, f2 = atts.take()
                s3, e3, f3 = atts.take()
                a1 = C.put(lambda e, e1=e1, pair=pair: e.activation(e1[:, :], pair[0], ACT.Exp), tok, f1)
                a2 = C.put(lambda e, e2=e2, pair=pair: e.activation(e2[:, :], pair[0], ACT.Exp, scale=-1.0),
                           tok, f2)
                a3 = C.put(lambda e, e3=e3, pair=pair: e.activation(e3[:, :], pair[1], ACT.Exp), tok2, f3)
                pairs.give(slot, a3)
                v1 = V.put(lambda e, e1=e1, t=t, c=c: e.tensor_tensor(R[:, t, c], R[:, t, c], e1[:, :],
                                                                      ALU.mult), a1, bon_done)
                v2 = V.put(lambda e, e2=e2, t=t, c=c: e.tensor_tensor(K[:, t, c], K[:, t, c], e2[:, :],
                                                                      ALU.mult), a2)
                v3 = V.put(lambda e, e2=e2, t=t, c=c: e.tensor_tensor(AA[:, t, c], AA[:, t, c], e2[:, :],
                                                                      ALU.mult), bb)
                v4 = V.put(lambda e, e3=e3, t=t, c=c: e.scalar_tensor_tensor(
                    KK[:, t, c], KK[:, t, c], -1.0, e3[:, :], ALU.mult, ALU.mult), a3, bb)
                atts.give(s1, v1)
                atts.give(s2, v3)
                atts.give(s3, v4)
                scan_in[(t, b)] = v4
        slot, pair, free = pairs.take()
        for t in range(T):
            for p in range(8):
                tok = PE.put(lambda e, t=t, p=p, pair=pair: e.matmul(
                    pair[0][:, p:p + 1], LW[:, t, p * P:(p + 1) * P], CU[:, 2 * P + t:2 * P + t + 1],
                    start=(t == 0 and p == 0), stop=(t == 1 and p == 7), skip_group_check=True), free)
        scl = SM[:, 96:104]
        scl_done = C.put(lambda e, pair=pair: e.activation(scl, pair[0][:, 0:8], ACT.Exp), tok)
        pairs.give(slot, scl_done)

        allbanks = Ring([bank(i) for i in range(8)])
        for i in range(3):
            allbanks.free[2 * i] = list(pairs.free[i])
            allbanks.free[2 * i + 1] = list(pairs.free[i])
        for i in range(2):
            allbanks.free[6 + i] = list(tbanks.free[i])
        maps = []
        before = [x_used[0], [f for f in atts.free], scl_done, tok, scan_in[(1, 1)], bc.free[0], bc.free[1],
                  bc.free[2]]
        for s_, spots in enumerate((
                [XO, XO + 4096, XO + 8192, XO + 10240, XO + 12288, XO + 14336, AO, AO + 2048, AO + 3072],
                [TO + 8192, TO + 12288, EO + 24576, EO + 26624, EO + 28672, EO + 30720, BO, BO + 2048,
                 BO + 3072])):
            TT = at(f"sTT{s_}", spots[0], [P, 4, 2, P], F32)
            KR = at(f"sKR{s_}", spots[1], [P, 4, 2, P], F32)
            MR = at(f"sMR{s_}", spots[2], [P, 2, 2, 2, P], F32)
            XX = at(f"sXX{s_}", spots[4], [P, 4, P], F32)
            YY = at(f"sYY{s_}", spots[5], [P, 4, P], F32)
            WW = at(f"sWW{s_}", spots[6], [P, 4, P], F32)
            RH = at(f"sRH{s_}", spots[7], [P, 4, HD], F32)
            SA = at(f"sSA{s_}", spots[8], [P, 4, HD], F32)
            maps.append((TT, KR, MR, XX, YY, WW, RH, SA))
        S0 = at("sS0", BO + 4096, [P, 8, HD], F32)
        set_free = [before, before]
        s0_done = {}
        y_done = {}
        s0_free = before

        def mask(i, n):
            return MK[:, i, :].unsqueeze(1).broadcast_to([P, n, P])

        def group(c, q, s_):
            TT, KR, MR, XX, YY, WW, RH, SA = maps[s_]
            f0 = set_free[s_]
            srcs = (KK, R, AA, K)
            b4 = lambda b: b.rearrange("p (u n) -> p u n", u=4)
            for half in range(2):
                n, b, free = allbanks.take()
                for i in range(2):
                    for pr in range(2):
                        x = srcs[2 * half + i][:, c, (2 * q + pr) * P:(2 * q + pr + 1) * P]
                        tok = PE.put(lambda e, i=i, pr=pr, x=x, b=b: e.transpose(
                            b[:, (2 * i + pr) * P:(2 * i + pr + 1) * P], x, ident[:, :]),
                            free, scan_in[(c, q // 2)], mark=(i == 1 and pr == 1))
                dst = TT[:, 2 * half:2 * half + 2, :, :].rearrange("p a b n -> p (a b) n")
                if half == 0:
                    tt0 = C.put(lambda e, b=b, dst=dst: e.activation(dst, b4(b), ACT.Copy), tok, f0)
                    allbanks.give(n, tt0)
                else:
                    tt1 = V.put(lambda e, b=b, dst=dst: e.tensor_copy(dst, b4(b)), tok, f0)
                    allbanks.give(n, tt1)
            yield
            un = [(u, 2 * q + u // 2, slice((u % 2) * HD, (u % 2) * HD + HD)) for u in range(4)]
            for h2 in range(2):
                n, b, free = allbanks.take()
                for i, (l_, r_) in enumerate(((0, 2), (2, 1))):
                    for u, pr, hs in un[h2::2]:
                        tok = PE.put(lambda e: e.matmul(
                            b[:, (2 * i + u // 2) * P:(2 * i + u // 2 + 1) * P], TT[hs, l_, u // 2, :],
                            TT[hs, r_, u // 2, :], start=True, stop=True),
                            free, tt0, tt1, mark=(i == 1 and u >= 2))
                m02 = MK[:, 0:3:2, :].unsqueeze(2).broadcast_to([P, 2, 2, P])
                ma = V.put(lambda e: e.tensor_tensor(
                    MR[:, h2, :, :, :], b.rearrange("p (i u n) -> p i u n", i=2, u=2), m02, ALU.mult),
                    tok, f0, mk_in)
                allbanks.give(n, ma)
                n, b, free = allbanks.take()
                for u, pr, hs in un[h2::2]:
                    tok = PE.put(lambda e: e.matmul(
                        b[:, (u // 2) * 256:(u // 2) * 256 + 256].rearrange("p (i n) -> p i n", i=2),
                        TT[hs, 3, u // 2, :], TT[hs, 0:2, u // 2, :], start=True, stop=True),
                        free, mark=(u >= 2))
                m12 = MK[:, 1:3, :].rearrange("p a n -> p (a n)").unsqueeze(1).broadcast_to([P, 2, 2 * P])
                kr = V.put(lambda e: e.tensor_tensor(
                    KR[:, h2:4:2, :, :].rearrange("p u a n -> p u (a n)"),
                    b.rearrange("p (u n) -> p u n", u=2), m12, ALU.mult), tok, f0)
                allbanks.give(n, kr)
            rb = ma
            yield
            x_done = i_done
            y_done_ = i_done
            for lv in range(7):
                n, b, free = allbanks.take()
                for u in range(4):
                    y_ = ident[:, :] if lv == 0 else YY[:, u, :]
                    PE.put(lambda e, u=u, b=b, y_=y_: e.matmul(
                        b[:, u * P:(u + 1) * P], MR[:, u % 2, 0, u // 2, :], y_, start=True, stop=False),
                        free, ma, y_done_, mark=False)
                    tok = PE.put(lambda e, u=u, b=b: e.matmul(
                        b[:, u * P:(u + 1) * P], identb[:, :], identb[:, :], start=False, stop=True),
                        mark=(u == 3))
                W_ = YY if lv == 0 else WW
                w = V.put(lambda e, b=b, W_=W_, lv=lv: e.tensor_tensor(
                    W_[:, :, :], b4(b), mask(3 + lv, 4), ALU.mult), tok, f0)
                allbanks.give(n, w)
                yield
                if lv > 0:
                    n, b, free = allbanks.take()
                    for u in range(4):
                        tok = PE.put(lambda e, u=u, b=b: e.matmul(
                            b[:, u * P:(u + 1) * P], XX[:, u, :], WW[:, u, :], start=True, stop=True),
                            free, w, x_done, mark=(u == 3))
                    y_done_ = C.put(lambda e, b=b: e.activation(YY[:, :, :], b4(b), ACT.Copy), tok)
                    allbanks.give(n, y_done_)
                else:
                    y_done_ = w
                if lv < 6:
                    n, b, free = allbanks.take()
                    for u in range(4):
                        x_ = ident[:, :] if lv == 0 else XX[:, u, :]
                        tok = PE.put(lambda e, u=u, b=b, W_=W_, x_=x_: e.matmul(
                            b[:, u * P:(u + 1) * P], W_[:, u, :], x_, start=True, stop=True),
                            free, w, x_done, mark=(u == 3))
                    x_done = C.put(lambda e, b=b: e.activation(XX[:, :, :], b4(b), ACT.Copy), tok, f0)
                    allbanks.give(n, x_done)
                yield
            b64 = lambda b, k: b[:, 0:k * HD].rearrange("p (u n) -> p u n", u=k)
            vs = lambda pr, hs: VV[:, c, pr * P + hs.start:pr * P + hs.start + HD]
            for h2 in range(2):
                n, b, free = allbanks.take()
                for u, pr, hs in un[h2::2]:
                    o_ = b[:, (u // 2) * HD:(u // 2 + 1) * HD]
                    tok = PE.put(lambda e: e.matmul(
                        o_, KR[:, u, 0, :], vs(pr, hs), start=True, stop=(c == 0)), free, kr, rkv)
                    if c == 1:
                        tok = PE.put(lambda e: e.matmul(
                            o_, TT[hs, 0, u // 2, :], S0[hs, pr, :], start=False, stop=True), s0_done[q])
                a = C.put(lambda e: e.activation(RH[:, h2:4:2, :], b64(b, 2), ACT.Copy), tok, f0)
                allbanks.give(n, a)
            yield
            n, b, free = allbanks.take()
            for u in range(4):
                tok = PE.put(lambda e: e.matmul(
                    b[:, u * HD:(u + 1) * HD], YY[:, u, :], RH[:, u, :], start=True, stop=True),
                    free, a, y_done_, mark=(u == 3))
            a = C.put(lambda e: e.activation(SA[:, :, :], b64(b, 4), ACT.Copy), tok, f0)
            allbanks.give(n, a)
            yield
            for h2 in range(2):
                n, b, free = allbanks.take()
                for u, pr, hs in un[h2::2]:
                    o_ = b[:, (u // 2) * HD:(u // 2 + 1) * HD]
                    PE.put(lambda e: e.matmul(
                        o_, KR[:, u, 1, :], vs(pr, hs), start=True, stop=False), free, mark=False)
                    if c == 1:
                        PE.put(lambda e: e.matmul(
                            o_, TT[hs, 1, u // 2, :], S0[hs, pr, :], start=False, stop=False), mark=False)
                    tok = PE.put(lambda e: e.matmul(
                        o_, MR[:, u % 2, 1, u // 2, :], SA[:, u, :], start=False, stop=True), a, rb)
                yo = R[:, c, q * 256:(q + 1) * 256].rearrange("p (u h n) -> p h u n", h=2, n=HD)[:, h2, :, :]
                y = C.put(lambda e: e.activation(yo, b64(b, 2), ACT.Copy), tok)
                allbanks.give(n, y)
            y_done[(c, q)] = y
            if c == 0:
                n, b, free = allbanks.take()
                for u, pr, hs in un:
                    o_ = b[hs, (u // 2) * HD:(u // 2) * HD + HD]
                    ch = slice(pr * P + hs.start, pr * P + hs.start + HD)
                    PE.put(lambda e, u=u, o_=o_, ch=ch: e.matmul(
                        o_, AA[:, 0, ch], SA[:, u, :], start=True, stop=False), free, mark=False)
                    tok = PE.put(lambda e, o_=o_, ch=ch: e.matmul(
                        o_, K[:, 0, ch], VV[:, 0, ch], start=False, stop=True))
                for i in range(2):
                    s0_done[q] = V.put(lambda e, i=i, b=b: e.tensor_scalar(
                        S0[:, 2 * q + i, :], b[:, i * HD:(i + 1) * HD], scl[:, 2 * q + i:2 * q + i + 1], None,
                        ALU.mult), tok, s0_free, scl_done)
                allbanks.give(n, s0_done[q])
            set_free[s_] = [tok, y, (V.sem, V.count)]

        for c in range(2):
            for q in (0, 2):
                gens = [group(c, q, 0), group(c, q + 1, 1)]
                while gens:
                    for g_ in list(gens):
                        try:
                            next(g_)
                        except StopIteration:
                            gens.remove(g_)
        for i in range(3):
            pairs.free[i] = allbanks.free[2 * i] + allbanks.free[2 * i + 1]
        for i in range(2):
            tbanks.free[i] = allbanks.free[6 + i]
        over = [set_free[0], set_free[1]]
        for i in range(3):
            atts.free[i] = over
            bc.free[i] = over
        l0 = broadcast(A["b_lnx"][0, 0])
        l1 = broadcast(A["b_lnx"][0, 1])
        mean, var = SM[:, 128:160], SM[:, 160:192]
        x3 = fl(R[:, :, :])
        t3 = fl(TB[:, :, :])
        v = V.put(lambda e: e.tensor_reduce(mean, x3, AX, ALU.add), list(y_done.values()))
        v = V.put(lambda e: e.tensor_scalar(mean, mean, 1.0 / HD, None, ALU.mult), v)
        v = V.put(lambda e: e.tensor_tensor(x3, x3, mean.unsqueeze(2).broadcast_to([P, 32, HD]),
                                            ALU.subtract), v)
        v = V.put(lambda e: e.tensor_tensor(t3, x3, x3, ALU.mult), v, over)
        v = V.put(lambda e: e.tensor_reduce(var, t3, AX, ALU.add), v)
        g = rsqrt(var, 1.0 / HD, GN_EPS, v)
        v = V.put(lambda e: e.tensor_tensor(x3, x3, var.unsqueeze(2).broadcast_to([P, 32, HD]),
                                            ALU.mult), g)
        w = V.put(lambda e: e.tensor_tensor(t3, fl(VV[:, :, :]), bon.unsqueeze(2).broadcast_to([P, 32, HD]),
                                            ALU.mult), over)
        yd = []
        for t in range(T):
            v = V.put(lambda e, t=t: e.tensor_tensor(R[:, t, :], R[:, t, :], l0[1][:, :], ALU.mult), v, l0[2])
            v = V.put(lambda e, t=t: e.tensor_tensor(TB[:, t, :], TB[:, t, :], l1[1][:, :], ALU.add), w, l1[2])
            v = V.put(lambda e, t=t: e.tensor_tensor(R[:, t, :], R[:, t, :], TB[:, t, :], ALU.add), v)
            v = V.put(lambda e, t=t: e.tensor_tensor(R[:, t, :], R[:, t, :], GG[:, t, :], ALU.mult), v, gdone[0])
            yd.append(v)
        bc.give(l0[0], v)
        bc.give(l1[0], v)
        tmp_used[0] = v
        ready = spread(lambda k, t: R[:, t, k * P:(k + 1) * P], DK, XH, XL, None,
                       lambda k, t: yd[t], over)
        x_used[0] = project(XH, XL, DK, A["b_w_out"][0], nr[1, 3], 1.0, ready)
        a_used[0] = [x_used[0], (V.sem, V.count)]

    def rope(x, nh, RP, TR, *marks):
        for t in range(T):
            x4 = x[:, t, :].rearrange("p (h n) -> p h n", n=HD)
            a, b = x4[:, :, 0:8], x4[:, :, 8:16]
            cs, sn = (RP[:, i, t, :].unsqueeze(1).broadcast_to([P, nh, 8]) for i in range(2))
            tr = [TR[:, i, t, 0:nh * 8].rearrange("p (h n) -> p h n", n=8) for i in range(4)]
            m = [V.put(lambda e, i=i, y=y, z=z: e.tensor_tensor(tr[i], y, z, ALU.mult), *marks,
                       (V.sem, V.count)) for i, (y, z) in enumerate(((a, cs), (b, sn), (b, cs), (a, sn)))]
            V.put(lambda e: e.tensor_tensor(a, tr[0], tr[1], ALU.subtract), m[3])
            v = V.put(lambda e: e.tensor_tensor(b, tr[2], tr[3], ALU.add), m[3])
        return v

    def dilated():
        QT = at("dQT", EO, [P, 12, S], F32)
        KT = at("dKT", EO + 12288, [P, 12, S], F32)
        VD = at("dVD", EO + 24576, [P, T, 3, 512], F32)
        MK = at("dMK", EO + 36864, [P, T, 3 * S], BF16)
        RP = at("dRP", EO + 39936, [P, 2, T, 8], F32)
        TR = at("dTR", EO + 40064, [P, 4, T, 64], F32)
        PS = [at(f"dPS{i}", EO + 42112 + i * 3072, [P, 3 * S], F32) for i in range(2)]
        PTs = [at(f"dPT{i}", EO + 48256 + i * 3072, [P, 6, P], F32) for i in range(2)]
        SM = at("dSM", EO + 54400, [P, 64], F32)
        QS = [TMP[:, :, i, 0:512] for i in range(2)]
        OO = at("dOO", EO + 54656, [P, T, 512], F32)
        e0 = a_used[0]
        in1 = [single(G, MK[:, :, :], A["c_dil"], e0), single(G, RP[:, :, :, :], A["c_rope"], e0)]
        rs, rs_done, ready = prenorm(1, 0, 2)
        wv = A["a_wqkv_2"][0].rearrange("(k p) n -> p k n", p=P)
        blocks = [(512, lambda k0, k1, c=c: wv[:, k0:k1, c * 512:(c + 1) * 512]) for c in range(9)]
        qs = Ring(QS)
        qs.free = [[tmp_used[0]], [tmp_used[0]]]
        kt_done, vd_done = [], []

        def consume(b, slot, pair, tok):
            if b >= 6:
                for t in range(T):
                    a = C.put(lambda e, t=t: e.activation(VD[:, t, b - 6, :], pair[t], ACT.Copy,
                                                          scale=rs[:, t:t + 1]), tok, rs_done, e0)
                vd_done.append(a)
                pairs.give(slot, a)
                return None
            n, x, free = qs.take()
            for t in range(T):
                a = C.put(lambda e, t=t: e.activation(x[:, t, :], pair[t], ACT.Copy, scale=rs[:, t:t + 1]),
                          tok, rs_done, free)
            pairs.give(slot, a)
            v = rope(x, 8, RP, TR, a, in1, e0)

            def later():
                dst, g = (QT, b) if b < 3 else (KT, b - 3)
                for p in range(0, 4, 2):
                    tslot, bk, tfree = tbanks.take()
                    for i in range(2):
                        for t in range(T):
                            tok = PE.put(lambda e, p=p, i=i, t=t, bk=bk: e.transpose(
                                bk[:, i * S + t * P:i * S + (t + 1) * P],
                                x[:, t, (p + i) * P:(p + i + 1) * P], ident[:, :]),
                                tfree, v, a, mark=(i == 1 and t == 1))
                    w = V.put(lambda e, p=p, bk=bk: e.tensor_copy(
                        dst[:, 4 * g + p:4 * g + p + 2, :], bk.rearrange("p (i s) -> p i s", i=2)), tok, e0)
                    tbanks.give(tslot, w)
                    kt_done.append(w)
                qs.give(n, tok)

            return later

        x_used[0] = linear(XH, XL, DK, blocks, consume, ready)
        flush()
        sc = Ring([0, 1])
        sc.free = [pairs.free[0] + pairs.free[2], pairs.free[1] + pairs.free[2]]
        ob = Ring([bank(4), bank(5)])
        ob.free = [pairs.free[2], pairs.free[2]]
        pr_ring, pt_ring = Ring(PS), Ring(PTs)
        pr_ring.free = pt_ring.free = [[e0], [e0]]
        pt_ring.free = [[e0], [e0]]
        odone = {}
        steps = [(hd, t) for hd in range(8) for t in range(T)]
        state = {}

        def first(i):
            hd, t = steps[i]
            pr, hs = hd // 2, slice((hd % 2) * HD, (hd % 2) * HD + HD)
            n, s_, free = sc.take()
            for g in range(3):
                o_ = banks_t[s_][:, g * S:(g + 1) * S]
                PE.put(lambda e, g=g, o_=o_: e.matmul(
                    o_, QT[hs, 4 * g + pr, t * P:(t + 1) * P], KT[hs, 4 * g + pr, :],
                    start=True, stop=False), free, kt_done[-1], mark=False)
                tok = PE.put(lambda e, g=g, o_=o_: e.matmul(
                    o_, identb[:, :], MK[:, t, g * S:(g + 1) * S], start=False, stop=True),
                    in1, mark=(g == 2))
            c = 4 * (i % 4)
            mx, nm, den = SM[:, c:c + 1], SM[:, c + 1:c + 2], SM[:, c + 2:c + 3]
            rd = SM[:, c + 3:c + 4]
            old = state.get(i - 4)
            v = V.put(lambda e: e.tensor_reduce(mx, banks_t[s_][:, 0:3 * S], AX, ALU.max), tok, e0,
                      old[-1] if old else None)
            v = V.put(lambda e: e.tensor_scalar(nm, mx, -0.125, None, ALU.mult), v)
            m, pp, pfree = pr_ring.take()
            a = C.put(lambda e: e.activation(pp[:, :], banks_t[s_][:, 0:3 * S], ACT.Exp, bias=nm, scale=0.125,
                                             accum_out=den), v, pfree)
            sc.give(n, a)
            v = V.put(lambda e: e.reciprocal(rd, den), a)
            state[i] = [m, pp, a, rd, v]

        def second(i):
            hd, t = steps[i]
            m, pp, a, rd, rdone = state[i]
            k, pt, tfree = pt_ring.take()
            ev = []
            for h2, (j0, j1) in enumerate(((0, 4), (4, 6))):
                slot, bk, free = tbanks.take()
                for j in range(j0, j1):
                    tok = PE.put(lambda e, j=j, bk=bk: e.transpose(
                        bk[:, (j - j0) * P:(j - j0 + 1) * P], pp[:, j * P:(j + 1) * P], ident[:, :]),
                        free, a, mark=(j == j1 - 1))
                src = bk[:, 0:(j1 - j0) * P].rearrange("p (j n) -> p j n", n=P)
                if h2 == 0:
                    w = V.put(lambda e, src=src: e.tensor_copy(pt[:, 0:4, :], src), tok, tfree)
                else:
                    w = C.put(lambda e, src=src: e.activation(pt[:, 4:6, :], src, ACT.Copy), tok, tfree)
                tbanks.give(slot, w)
                ev.append(w)
            pr_ring.give(m, tok)
            n, b, free = ob.take()
            for j in range(6):
                tok = PE.put(lambda e, j=j, b=b: e.matmul(
                    b[:, 0:HD], pt[:, j, :], VD[:, j % 2, j // 2, hd * HD:(hd + 1) * HD],
                    start=(j == 0), stop=(j == 5)), free, ev, vd_done[-1], mark=(j == 5))
            pt_ring.give(k, tok)
            v = V.put(lambda e, b=b: e.tensor_scalar(OO[:, t, hd * HD:(hd + 1) * HD], b[:, 0:HD], rd, None,
                                                     ALU.mult), tok, rdone, e0)
            ob.give(n, v)
            state[i].append(v)
            odone[(hd, t)] = v

        first(0)
        for i in range(16):
            if i + 1 < 16:
                first(i + 1)
            second(i)
        pairs.free = [sc.free[0], sc.free[1], [ob.free[0], ob.free[1]]]
        ready = spread(lambda k, t: OO[:, t, k * P:(k + 1) * P], 4, XH, XL, None,
                       lambda k, t: odone[(2 * k + 1, t)], x_used[0])
        tmp_used[0] = (PE.sem, PE.count)
        x_used[0] = project(XH, XL, 4, A["a_wo_2"][0], A["norm_g_2"][0, 3], 1.0, ready)
        a_used[0] = [x_used[0], (V.sem, V.count)]

    def gqa():
        QT = at("qQT", EO, [P, 8, S], F32)
        KT = at("qKT", EO + 8192, [P, 4, S], F32)
        QS = at("qQS", EO + 12288, [P, T, 1536], F32)
        KD = at("qKD", EO + 24576, [P, T, 4, P], F32)
        MK = at("qMK", EO + 28672, [P, T, S], BF16)
        RP = at("qRP", EO + 29696, [P, 2, T, 8], F32)
        TR = at("qTR", EO + 29824, [P, 4, T, 160], F32)
        OO = at("qOO", EO + 34944, [P, T, D], F32)
        PTs = [at(f"qPT{i}", EO + 43136 + 4096 * i, [P, 2, 4, P], F32) for i in range(2)]
        SK = at("qSK", EO + 51328, [P, NH], F32)
        SM = at("qSM", EO + 51392, [P, 8, 20], F32)
        PS = [at(f"qPS{i}", TO + 4096 * i, [P, 4, S], F32) for i in range(2)]
        e0 = a_used[0]
        in1 = [single(G, MK[:, :, :], A["c_gqa"], e0), single(G, RP[:, :, :, :], A["c_rope"], e0),
               single(G, SK[:, :], A["b_sink_2"][0].partition_broadcast(P), e0)]
        rs, rs_done, ready = prenorm(1, 1, 2)
        wv = A["b_wqkv_2"][0].rearrange("(k p) n -> p k n", p=P)
        blocks = [(512, lambda k0, k1, c=c: wv[:, k0:k1, c * 512:(c + 1) * 512]) for c in range(3)]
        ev = []

        def consume(b, slot, pair, tok):
            for t in range(T):
                a = C.put(lambda e, t=t: e.activation(QS[:, t, b * 512:(b + 1) * 512], pair[t], ACT.Copy,
                                                      scale=rs[:, t:t + 1]), tok, rs_done, e0)
            ev.append(a)
            pairs.give(slot, a)

        x_used[0] = linear(XH, XL, DK, blocks, consume, ready)
        v = rope(QS[:, :, 0:1280], 20, RP, TR, ev[-1], in1, e0)
        for t in range(T):
            for i in range(2):
                kd = V.put(lambda e, t=t, i=i: e.tensor_copy(
                    KD[:, t, :, i * HD:(i + 1) * HD],
                    QS[:, t, 1024:1280].rearrange("p (k n) -> p k n", n=HD)), v, e0)
        kt_done = None
        for p in range(0, 12, 2):
            slot, bk, free = tbanks.take()
            for i in range(2):
                for t in range(T):
                    src = QS[:, t, (p + i) * P:(p + i + 1) * P] if p < 8 else KD[:, t, p + i - 8, :]
                    tok = PE.put(lambda e, i=i, t=t, bk=bk, src=src: e.transpose(
                        bk[:, i * S + t * P:i * S + (t + 1) * P], src, ident[:, :]),
                        free, v if p < 8 else kd, mark=(i == 1 and t == 1))
            dst = QT[:, p:p + 2, :] if p < 8 else KT[:, p - 8:p - 6, :]
            src = bk.rearrange("p (i s) -> p i s", i=2)
            kt_done = C.put(lambda e, dst=dst, src=src: e.activation(dst, src, ACT.Copy), tok, e0)
            tbanks.give(slot, kt_done)
        sc = Ring([0, 1])
        sc.free = [pairs.free[0], pairs.free[1]]
        ob = Ring([bank(4), bank(5)])
        ob.free = [pairs.free[2], pairs.free[2]]
        pr_ring, pt_ring = Ring(PS), Ring(PTs)
        pr_ring.free = [[tmp_used[0]], [tmp_used[0]]]
        pt_ring.free = [[e0], [e0]]
        steps = [(kv, t) for kv in range(4) for t in range(T)]
        state, odone = {}, {}

        def first(i):
            kv, t = steps[i]
            n, s_, free = sc.take()
            for j in range(4):
                hd = 4 * kv + j
                hs = slice((hd % 2) * HD, (hd % 2) * HD + HD)
                at_ = (j % 2) * 2 + j // 2
                o_ = banks_t[s_][:, at_ * S:(at_ + 1) * S]
                PE.put(lambda e, hd=hd, hs=hs, o_=o_: e.matmul(
                    o_, QT[hs, hd // 2, t * P:(t + 1) * P], KT[hs, kv, :], start=True, stop=False),
                    free, kt_done, mark=False)
                tok = PE.put(lambda e, o_=o_: e.matmul(
                    o_, identb[:, :], MK[:, t, :], start=False, stop=True), in1, mark=(j == 3))
            mx, nm, den, es, rd = (SM[:, i, 4 * c:4 * c + 4] for c in range(5))
            sk = SK[:, 4 * kv:4 * kv + 4].rearrange("p (a b) -> p b a", b=2)
            ba = lambda x: x.rearrange("p (b a) -> p b a", b=2)
            v = V.put(lambda e: e.tensor_reduce(mx, banks_t[s_][:, :].rearrange("p (j s) -> p j s", j=4),
                                                AX, ALU.max), tok, e0)
            v = V.put(lambda e: e.scalar_tensor_tensor(ba(mx), ba(mx), 0.125, sk, ALU.mult, ALU.max), v, in1)
            v0 = V.put(lambda e: e.tensor_scalar(nm, mx, -1.0, None, ALU.mult), v)
            v = V.put(lambda e: e.tensor_tensor(ba(es), sk, ba(nm), ALU.add), v0)
            m, pp, pfree = pr_ring.take()
            for j in range(4):
                a = C.put(lambda e, j=j: e.activation(
                    pp[:, j, :], banks_t[s_][:, j * S:(j + 1) * S], ACT.Exp, bias=nm[:, j:j + 1], scale=0.125,
                    accum_out=den[:, j:j + 1]), v0, pfree)
            sc.give(n, a)
            a2 = C.put(lambda e: e.activation(es, es, ACT.Exp), v)
            v = V.put(lambda e: e.tensor_tensor(den, den, es, ALU.add), a2, a)
            v = V.put(lambda e: e.reciprocal(rd, den), v)
            state[i] = [m, pp, a, rd, v]

        def second(i):
            kv, t = steps[i]
            m, pp, a, rd, rdone = state[i]
            k, pt, tfree = pt_ring.take()
            ev = []
            for kt in range(2):
                slot, bk, free = tbanks.take()
                for j in range(4):
                    tok = PE.put(lambda e, j=j, bk=bk: e.transpose(
                        bk[:, j * P:(j + 1) * P], pp[:, j, kt * P:(kt + 1) * P], ident[:, :]),
                        free, a, mark=(j == 3))
                src = bk.rearrange("p (j n) -> p j n", n=P)
                if kt == 0:
                    w = V.put(lambda e, src=src: e.tensor_copy(pt[:, 0, :, :], src), tok, tfree)
                else:
                    w = C.put(lambda e, src=src: e.activation(pt[:, 1, :, :], src, ACT.Copy), tok, tfree)
                tbanks.give(slot, w)
                ev.append(w)
            pr_ring.give(m, tok)
            n, b, free = ob.take()
            for j in range(4):
                for kt in range(2):
                    tok = PE.put(lambda e, j=j, kt=kt, b=b: e.matmul(
                        b[:, j * HD:(j + 1) * HD], pt[:, kt, (j % 2) * 2 + j // 2, :],
                        QS[:, kt, 1280 + kv * HD:1280 + (kv + 1) * HD], start=(kt == 0), stop=(kt == 1)),
                        free, ev, mark=(j == 3 and kt == 1))
            pt_ring.give(k, tok)
            v = V.put(lambda e, b=b: e.tensor_tensor(
                OO[:, t, kv * 256:(kv + 1) * 256].rearrange("p (a b n) -> p a b n", n=HD, b=2),
                b[:, 0:256].rearrange("p (a b n) -> p a b n", n=HD, b=2),
                rd.rearrange("p (b a) -> p a b", b=2).unsqueeze(3).broadcast_to([P, 2, 2, HD]), ALU.mult), tok, rdone, e0)
            ob.give(n, v)
            odone[(kv, t)] = v

        first(0)
        for i in range(8):
            if i + 1 < 8:
                first(i + 1)
            second(i)
        pairs.free = [sc.free[0], sc.free[1], [ob.free[0], ob.free[1]]]
        ready = spread(lambda k, t: OO[:, t, k * P:(k + 1) * P], DK, XH, XL, None,
                       lambda k, t: odone[(k // 2, t)], x_used[0])
        tmp_used[0] = (PE.sem, PE.count)
        x_used[0] = project(XH, XL, DK, A["b_wo_2"][0], A["norm_g_2"][1, 3], 1.0, ready)
        a_used[0] = [x_used[0], (V.sem, V.count)]

    todo = []
    for block, names, mixers in (
            (0, ("ffn_w13", "ffn_w2", "norm_g", "p", "ple_w_gate", "ple_w_proj"), (gmlp, rwkv)),
            (1, ("ffn_wi_2", "ffn_wo_2", "norm_g_2", "p_2", "ple_gate_2", "ple_proj_2"), (dilated, gqa))):
        w13, w2, ng, p, wg, wp = (A[n] for n in names)
        for layer in range(2):
            todo.append(lambda b=block, l=layer, w13=w13, w2=w2, ng=ng: ffn(b, l, 0, w13[l, 0], w2[l, 0], ng))
            todo.append(mixers[layer])
            todo.append(lambda b=block, l=layer, w13=w13, w2=w2, ng=ng: ffn(b, l, 1, w13[l, 1], w2[l, 1], ng))
            todo.append(lambda b=block, l=layer, p=p, wg=wg, wp=wp, ng=ng: ple(b, l, p, wg, wp, ng))
    which = range(stages) if isinstance(stages, int) else stages
    for n in which:
        if n < len(todo):
            todo[n]()

    s_out = sem("d_out")
    for t in range(T):
        SP.wait(h_done[t])
        SP.ops.append(lambda e, t=t: e.dma_start(out[0, t * P:(t + 1) * P, :], H[:, t, :]).then_inc(s_out, 16))
    SP.ops.append(lambda e: e.wait_ge(s_out, 16 * T))
    return {"sp": SP, "pe": PE, "v": V, "a": C, "g": G}


_INS = ["x", "p", "norm_g", "ffn_w13", "ffn_w2", "ple_w_gate", "ple_w_proj", "a_w_in", "a_b_in", "a_v_gain",
        "a_w_s", "a_b_s", "a_w_out", "b_mu", "b_w_in", "b_w0", "b_w1", "b_w2", "b_a0", "b_a1", "b_a2", "b_g1",
        "b_g2", "b_k_k", "b_k_a", "b_r_k", "b_lnx", "b_w_out", "p_2", "norm_g_2", "ffn_wi_2", "ffn_wo_2",
        "ple_proj_2", "ple_gate_2", "a_wqkv_2", "a_wo_2", "b_wqkv_2", "b_wo_2", "b_sink_2"]


def kernel(**inputs):
    import numpy as _np
    import concourse.bacc as _bacc
    from concourse import mybir as _mybir
    from concourse.bass_utils import run_bass_kernel_spmd as _run

    nc = _bacc.Bacc("TRN2", target_bir_lowering=False, num_devices=1)
    given = {name: _np.ascontiguousarray(inputs[name]) for name in _INS}
    given.update(constants())
    arrays, args = {}, {}
    for name, a in given.items():
        arrays[f"in_{name}_dram"] = a
        args[name] = nc.dram_tensor(f"in_{name}_dram", a.shape, _mybir.dt.from_np(a.dtype),
                                    kind="ExternalInput").ap()
    out = nc.dram_tensor("out_0_dram", (1, S, D), F32, kind="ExternalOutput").ap()
    program(nc, args, out)
    r = _run(nc, [arrays], core_ids=[0])
    return r.results[0]["out_0_dram"]
```

```python
from contextlib import ExitStack

import numpy as np

import concourse.bass as bass
from concourse import mybir

F32 = mybir.dt.float32
F32R = mybir.dt.float32r
BF16 = mybir.dt.bfloat16
ALU = mybir.AluOpType
ACT = mybir.ActivationFunctionType
AX = mybir.AxisListType.X

P = 128
T = 2
S = T * P
D = 1024
DK = D // P
FF = 2816
FB = 256
PD = 256
RMS_EPS = 1e-6
LN_EPS = 1e-5
GN_EPS = 64e-5
NH = 16
HD = 64
EXP_HALF = 0.6065306597126334

BASE = 16512
CHUNK = 2048
PART = 1024
N_RAW = 3
N_W = 7
HEAD, TAIL = 5, 6
TURN0, TURN1, NORMS = 5, 6, 14


class Written:

    def matmul(self, *a, **k):
        return lambda e: e.matmul(*a, **k)

    def transpose(self, *a, **k):
        return lambda e: e.transpose(*a, **k)

    def activation(self, *a, **k):
        return lambda e: e.activation(*a, **k)

    def tensor_tensor(self, *a, **k):
        return lambda e: e.tensor_tensor(*a, **k)

    def tensor_scalar(self, *a, **k):
        return lambda e: e.tensor_scalar(*a, **k)

    def scalar_tensor_tensor(self, *a, **k):
        return lambda e: e.scalar_tensor_tensor(*a, **k)

    def tensor_reduce(self, *a, **k):
        return lambda e: e.tensor_reduce(*a, **k)

    def tensor_copy(self, *a, **k):
        return lambda e: e.tensor_copy(*a, **k)

    def reciprocal(self, *a, **k):
        return lambda e: e.reciprocal(*a, **k)

    def memset(self, *a, **k):
        return lambda e: e.memset(*a, **k)


class Queue:

    def __init__(self, sem):
        self.sem, self.count, self.ops, self.passed = sem, 0, [], {}

    def wait(self, *marks):
        for m in marks:
            if m is None:
                continue
            if isinstance(m, list):
                self.wait(*m)
                continue
            sem, value = m
            if self.passed.get(id(sem), 0) < value:
                self.passed[id(sem)] = value
                self.ops.append(lambda e, sem=sem, value=value: e.wait_ge(sem, value))

    def put(self, fn, *marks, mark=True):
        self.wait(*marks)
        fn = fn(Written())
        if not mark:
            self.ops.append(fn)
            return None
        self.count += 1
        self.ops.append(lambda e, sem=self.sem: fn(e).then_inc(sem, 1))
        return (self.sem, self.count)

    def run(self, e):
        for op in self.ops:
            op(e)


class Loads:

    def __init__(self, sem):
        self.sem, self.count = sem, 0

    def put(self, queue, out, in_, *marks):
        queue.wait(*marks)
        self.count += 16
        queue.ops.append(lambda e, sem=self.sem: e.dma_start(out, in_).then_inc(sem, 16))
        return (self.sem, self.count)


class Ring:

    def __init__(self, places):
        self.places, self.free, self.at, self.out = places, [[] for _ in places], 0, set()

    def take(self):
        n = self.at % len(self.places)
        self.at += 1
        assert n not in self.out
        self.out.add(n)
        return n, self.places[n], self.free[n]

    def give(self, n, *marks):
        self.free[n] = list(marks)
        self.out.discard(n)


def constants():
    i = np.arange(S)
    rel = i[None, :] - i[:, None]
    far = np.float32(-1e30)
    dil = np.stack([np.where(np.abs(rel) <= 64, 0, far), np.where(rel % 4 == 0, 0, far),
                    np.where(rel % 16 == 0, 0, far)], axis=1)
    dil = dil.reshape(T, P, 3 * S).transpose(1, 0, 2)
    gqa = np.where(np.abs(rel) <= 128, 0, far).reshape(T, P, S).transpose(1, 0, 2)
    inv = np.float32(500000.0) ** (-np.arange(0, 16, 2, dtype=np.float32) / np.float32(16))
    ang = np.arange(S, dtype=np.float32)[:, None] * inv[None, :].astype(np.float32)
    rope = np.stack([np.cos(ang), np.sin(ang)], axis=1).astype(np.float32)
    rope = rope.reshape(T, P, 2, 8).transpose(1, 2, 0, 3)
    a = np.arange(P)
    low = a[None, :] < a[:, None]
    up = a[:, None] < a[None, :]
    upi = a[:, None] <= a[None, :]
    masks = [low, up, upi]
    for k in range(7):
        b = 1 << k
        blk = a // b
        m = (blk[:, None] % 2 == 0) & (blk[None, :] == blk[:, None] + 1)
        masks.append(m | np.eye(P, dtype=bool))
    masks = np.stack(masks, axis=1).astype(np.float32)
    mid = (a[:, None] <= 63).astype(np.float32) * np.ones((1, P), np.float32)
    cum = np.stack([upi - mid, up - mid], axis=1).astype(np.float32)
    ends = np.stack([a >= 64, a <= 63], axis=1).astype(np.float32)
    bf = mybir.dt.np(BF16)
    return {
        "c_ident": np.eye(P, dtype=np.float32),
        "c_identb": np.eye(P, dtype=np.float32).astype(bf),
        "c_dil": dil.astype(bf), "c_gqa": gqa.astype(bf), "c_rope": np.ascontiguousarray(rope),
        "c_masks": masks.astype(bf), "c_cum": np.concatenate([cum.reshape(P, 2 * P), ends], axis=1),
    }


def program(nc, A, out, stages=99):
    ctx = ExitStack()
    plan = []
    with ctx:
        cache = {}

        def named_sem(name):
            if name not in cache:
                cache[name] = ctx.enter_context(nc.semaphore(name))
            return cache[name]

        tensors = {}

        def at(name, offset, shape, dt):
            if name not in tensors:
                tensors[name] = nc.alloc_sbuf_tensor_at(name, shape, dt, offset=BASE + offset)
            return tensors[name]

        banks_t = [ctx.enter_context(nc.psum_tensor(f"bank{i}", [P, 1024], F32)) for i in range(4)]
        queues = emit(nc, A, out, at, banks_t, named_sem, None, plan, stages)
        queues = emit(nc, A, out, at, banks_t, named_sem, list(plan), [], stages)
        block = ctx.enter_context(nc.Block())
        for name, q in queues.items():
            on = {"sp": block.sync, "pe": block.tensor, "v": block.vector,
                  "a": block.scalar, "g": block.gpsimd}[name]
            on(q.run)


def emit(nc, A, out, at, banks_t, sem, plan, listed, stages):
    PE, V, C, G, SP = (Queue(sem(n)) for n in ("s_pe", "s_v", "s_a", "s_g", "s_sp"))

    raw = [at(f"raw{i}", i * 8192, [P, CHUNK], F32) for i in range(N_RAW)]
    o = N_RAW * 8192
    wh = [at(f"wh{i}", o + i * 4096, [P, PART], F32R) for i in range(N_W)]
    o += N_W * 4096
    wl = [at(f"wl{i}", o + i * 4096, [P, PART], F32R) for i in range(N_W)]
    o += N_W * 4096
    XO = o
    XH = at("XH", o, [P, DK, S], F32R)
    XL = at("XL", o + 8192, [P, DK, S], F32R)
    o += 16384
    H = at("H", o, [P, T, D], F32)
    o += 8192
    TO = o
    TMP = at("TMP", o, [P, T, 2, D], F32)
    o += 16384
    BO = o
    bct = [at(f"bc{i}", o + i * 4096, [P, D], F32) for i in range(3)]
    o += 12288
    AO = o
    att = [at(f"att{i}", o + i * 2048, [P, 512], F32) for i in range(3)]
    o += 6144
    JUNK = at("JUNK", o, [P, 1024], BF16)
    o += 2048
    ST = at("ST", o, [P, 512], F32)
    o += 2048
    ident = at("ident", o, [P, P], F32)
    identb = at("identb", o + 512, [P, P], BF16)
    o += 768
    GT = at("GT", o, [P, 2, P], F32)
    o += 1024
    MT = at("MT", o, [P, 64], F32)
    o += 256
    PT = at("PT", o, [P, T, PD], F32)
    PH = at("PH", o + 2048, [P, PD // P, S], F32R)
    PL = at("PL", o + 4096, [P, PD // P, S], F32R)
    o += 6144
    NEG = at("NEG", o, [P, 32], F32)
    o += 128
    EO = o
    AH = at("AH", EO, [P, FF // P, S], F32R)
    AL = at("AL", EO + FF // P * S * 4, [P, FF // P, S], F32R)

    def bank(i):
        return banks_t[i // 2][:, (i % 2) * 512:(i % 2) * 512 + 512]

    pairs = Ring([(bank(0), bank(1)), (bank(2), bank(3)), (bank(4), bank(5))])
    tbanks = Ring([bank(6), bank(7)])
    bc = Ring(bct)
    atts = Ring(att)
    bc_loads = [Loads(sem(f"d_bc{i}")) for i in range(3)]
    raw_loads = [Loads(sem(f"d_raw{i}")) for i in range(N_RAW)]
    once = Loads(sem("d_once"))
    pload = Loads(sem("d_p"))
    stat = [0]
    singles = [0]

    def single(queue, out_, in_, *marks):
        singles[0] += 1
        return Loads(sem(f"d_s{singles[0]}")).put(queue, out_, in_, *marks)


    def cols(n):
        c = stat[0]
        stat[0] += n
        assert stat[0] <= 512
        return ST[:, c:c + n]

    pending, deferred = [], []

    def flush():
        while pending:
            pending.pop(0)()

    def defer(steps, fn, first=False):
        deferred.append([steps, fn, first])

    def hurry():
        d = min(deferred, key=lambda d: d[0])
        deferred.remove(d)
        d[1]()

    def tick():
        for d in deferred:
            d[0] -= 1
        while deferred and min(d[0] for d in deferred) <= 0:
            hurry()

    n_used, n_ready, n_loads = [0], [0], [0]
    done, conv, landed, freed = {}, {}, {}, {}

    def load(c):
        src, shape = chunks[c]
        place = raw[c % N_RAW]
        dst = place[:, 0:shape[0] * shape[1]].rearrange("p (k n) -> p k n", k=shape[0])
        if len(src.shape) == 4:
            dst = dst.rearrange("p k (s n) -> p k s n", s=2)
            raw_loads[c % N_RAW].put(SP, dst[:, :, 0, :], src[:, :, 0, :], freed.get(c - N_RAW))
            dst, src = dst[:, :, 1, :], src[:, :, 1, :]
        landed[c] = raw_loads[c % N_RAW].put(SP, dst, src, freed.get(c - N_RAW))

    chunks, parts_left, parts_over = {}, {}, {}
    for c, src, shape, _, _ in plan or []:
        chunks[c] = (src, shape)
        parts_left[c] = parts_left.get(c, 0) + 1
        parts_over[c] = []

    def convert(j):
        c, _, _, at_, size = plan[j]
        while c not in landed:
            hurry()
        r, hi, lo = raw[c % N_RAW][:, at_:at_ + size], wh[j % N_W], wl[j % N_W]
        a = C.put(lambda e: e.activation(hi[:, 0:size], r, ACT.Copy), landed[c], done.get(j - N_W))

        def low():
            v = V.put(lambda e: e.tensor_tensor(lo[:, 0:size], r, hi[:, 0:size].bitcast(F32),
                                                ALU.subtract), a, landed[c])
            conv[j] = [a, v]
            parts_left[c] -= 1
            parts_over[c] += [a, v]
            if not parts_left[c]:
                freed[c] = parts_over[c]
                if c + N_RAW in chunks:
                    load(c + N_RAW)

        steps = [d[0] for d in deferred if d[2]]
        if steps:
            defer(max(steps) + 2, low)
        else:
            low()

    def use(src, k0, k1, r0, r1, n):
        j = n_used[0]
        n_used[0] += 1
        if k0 == r0:
            n_loads[0] += 1
        listed.append((n_loads[0] - 1, src(r0, r1), (r1 - r0, n), (k0 - r0) * n, (k1 - k0) * n))
        if plan is None:
            conv[j] = []
        else:
            if j == 0:
                for i in range(min(N_RAW, len(chunks))):
                    load(i)
                while any(d[2] for d in deferred):
                    hurry()
            while n_ready[0] < min(j + 1 if j else N_W, len(plan)):
                n_ready[0] += 1
                convert(n_ready[0] - 1)
            while j not in conv:
                hurry()
        hi = wh[j % N_W][:, 0:(k1 - k0) * n].rearrange("p (k n) -> p k n", n=n)
        lo = wl[j % N_W][:, 0:(k1 - k0) * n].rearrange("p (k n) -> p k n", n=n)
        return j, hi, lo, conv[j]

    def used(j, tok):
        done[j] = tok
        if plan is not None and n_ready[0] == j + N_W and n_ready[0] < len(plan):
            convert(n_ready[0])
            n_ready[0] += 1

    def linear(xh, xl, nk, blocks, consume, ready, kc=4, pc=2, head=1, tail=1, early=None):
        chunks = []
        for b in range(len(blocks)):
            cuts = list(range(0, nk, kc)) + [nk]
            if tail > 1 and b == len(blocks) - 1 and nk % kc:
                cuts = [0] + list(range(nk % kc, nk + 1, kc))
            chunks += [(b, k0, min(k0 + pc, r1), r0, r1) for r0, r1 in zip(cuts, cuts[1:])
                       for k0 in range(r0, r1, pc)]
        head = min(head, len(chunks))
        tail = min(tail, len(chunks) - head)
        groups = [chunks[:head]] + [[c] for c in chunks[head:len(chunks) - tail]]
        if tail:
            groups.append(chunks[len(chunks) - tail:])
        held, toks = {}, {}
        for group in groups:
            got = []
            for b, k0, k1, r0, r1 in group:
                if b not in held:
                    held[b] = pairs.take()
                    toks[b] = [None] * T
                n, src = blocks[b]
                got.append(use(src, k0, k1, r0, r1, n))
            for t in range(T):
                for (b, k0, k1, _, _), (j, hi, lo, conv_done) in zip(group, got):
                    slot, pair, free = held[b]
                    n = blocks[b][0]
                    PE.wait(conv_done, free[t] if len(free) == T else free)
                    for k in range(k0, k1):
                        tick()
                        PE.wait(ready(k, t))
                        o_ = pair[t][:, 0:n]
                        a_, b_ = xh[:, k, t * P:(t + 1) * P], xl[:, k, t * P:(t + 1) * P]
                        h_, l_ = hi[:, k - k0, :], lo[:, k - k0, :]
                        PE.put(lambda e: e.matmul(o_, a_, h_, start=(k == 0), stop=False), mark=False)
                        PE.put(lambda e: e.matmul(o_, a_, l_, start=False, stop=False), mark=False)
                        tok = PE.put(lambda e: e.matmul(o_, b_, h_, start=False, stop=(k == nk - 1)),
                                     mark=(k == k1 - 1))
                    toks[b][t] = tok
                    if k1 == nk and early is not None:
                        early(b, t, slot, pair, tok)
                    if t == T - 1:
                        used(j, tok)
                    if t == T - 1 and k1 == min(kc, nk):
                        flush()
                    if t == T - 1 and k1 == nk and consume is not None:
                        later = consume(b, slot, pair, toks[b])
                        if later is not None:
                            pending.append(later)
        return tok

    def same(ready):
        return lambda k, t: ready[k]

    def spread(src, nk, xh, xl, gain, src_done, free):
        ready = []
        for k in range(0, nk, 2):
            slot, b, bfree = tbanks.take()
            n = min(2, nk - k)
            for i in range(n):
                for t in range(T):
                    tok = PE.put(lambda e, i=i, t=t, k=k, b=b: e.transpose(
                        b[:, i * S + t * P:i * S + (t + 1) * P], src(k + i, t), ident[:, :]),
                        bfree, src_done(k + i, t), mark=(i == n - 1 and t == T - 1))
            v = []
            if gain is None:
                bb = b[:, 0:n * S].rearrange("p (k s) -> p k s", k=n)
                a = C.put(lambda e, k=k, n=n, bb=bb: e.activation(xh[:, k:k + n, :], bb, ACT.Copy),
                          tok, free)
                v = V.put(lambda e, k=k, n=n, bb=bb: e.tensor_tensor(
                    xl[:, k:k + n, :], bb, xh[:, k:k + n, :].bitcast(F32), ALU.subtract), a, tok, free)
                ready += [[a, v]] * n
                tbanks.give(slot, a, v)
            else:
                for i in range(n):
                    g = gain[:, k + i:k + i + 1]
                    bb = b[:, i * S:(i + 1) * S]
                    a = C.put(lambda e, k=k + i, g=g, bb=bb: e.activation(
                        xh[:, k, :], bb, ACT.Copy, scale=g), tok, free)
                for i in range(n):
                    g = gain[:, k + i:k + i + 1]
                    bb = b[:, i * S:(i + 1) * S]
                    v = V.put(lambda e, k=k + i, g=g, bb=bb: e.scalar_tensor_tensor(
                        xl[:, k, :], bb, g, xh[:, k, :].bitcast(F32), ALU.mult, ALU.subtract), a, tok, free)
                    ready.append([a, v])
                tbanks.give(slot, a, v)
        return ready

    def rsqrt(x, scale, eps, *marks):
        n = x.shape[-1]
        m = G.put(lambda e: e.tensor_scalar(x, x, scale, eps, ALU.mult, ALU.add), *marks)
        return G.put(lambda e: e.tensor_tensor(x, x, NEG[:, 0:n], ALU.pow), m, neg_done)

    def broadcast(src, n=D):
        slot, b, free = bc.take()
        tok = bc_loads[slot].put(G, b[:, 0:n], src.partition_broadcast(P), free)
        return slot, b, tok

    gs = TMP[:, 0, :, :]
    g_in = Loads(sem("d_g")).put(SP, gs[:, 0, 0:P], A["norm_g"].rearrange("l n (k p) -> (l n k) p", p=P))
    hload = [Loads(sem(f"d_h{t}")) for t in range(T)]
    h_done = [hload[t].put(SP, H[:, t, :], A["x"][0, t * P:(t + 1) * P, :]) for t in range(T)]
    i_done = Loads(sem("d_i")).put(C, ident[:, :], A["c_ident"])
    neg_done = V.put(lambda e: e.memset(NEG[:, :], -0.5))
    G.wait(neg_done)
    once.put(G, gs[:, 0, P:2 * P], A["norm_g_2"].rearrange("l n (k p) -> (l n k) p", p=P))
    once.put(G, gs[0:48, 0, 2 * P:3 * P], A["b_mu"].rearrange("l n (k p) -> (l n k) p", p=P))
    once.put(G, identb[:, :], A["c_identb"])
    late_in = once.put(G, gs[48:56, 0, 2 * P:3 * P], A["a_b_s"].rearrange("l g p -> (l g) p"))
    slot, b, free = tbanks.take()
    tok = PE.put(lambda e: e.transpose(b[:, 0:P], gs[:, 0, 0:P], ident[:, :]), g_in, i_done)
    gt_done = C.put(lambda e: e.activation(GT[:, 0, :], b[:, 0:P], ACT.Copy), tok)
    tbanks.give(slot, gt_done)
    V.wait(gt_done)
    PE.wait(i_done)
    C.wait(i_done)

    def late_constants():
        slot, b, free = tbanks.take()
        PE.put(lambda e: e.transpose(b[:, 0:P], gs[:, 0, P:2 * P], ident[:, :]), late_in, free, mark=False)
        tok = PE.put(lambda e: e.transpose(b[:, P:P + 56], gs[0:56, 0, 2 * P:3 * P], ident[0:56, 0:56]))
        C.put(lambda e: e.activation(GT[:, 1, :], b[:, 0:P], ACT.Copy), tok)
        a = C.put(lambda e: e.activation(MT[:, 0:56], b[:, P:P + 56], ACT.Copy), tok)
        tbanks.give(slot, a)
        V.wait(a)
        tmp_used[0] = tok

    defer(30, late_constants)

    x_used = [None]
    a_used = [None]
    tmp_used = [None]

    def gain_cols(block, layer, n):
        c = (layer * 8 + n) * DK
        return GT[:, block, c:c + DK]

    def prenorm(block, layer, n):
        if carry[0] is None:
            cr = carry_on((block, layer, n))
            for t in range(T):
                carry_tile(cr, t, [h_done[t], h_done[t]], x_used[0])
            carry[0] = cr
        cr, carry[0] = carry[0], None
        assert cr["next"] == (block, layer, n)
        return cr["rs"], cr["rs_done"], cr["ready"]

    carry = [None]

    def carry_on(nxt):
        got = {}

        def ready(k, t):
            while (k, t) not in got:
                hurry()
            return got[(k, t)]

        done_ = [None] * T

        def rs_done():
            while None in done_:
                hurry()
            return done_

        return {"next": nxt, "rs": cols(T), "done": done_, "rs_done": rs_done, "ready": ready, "got": got}

    def carry_tile(cr, t, halves, free):
        ss = cols(2)
        block, layer, n = cr["next"]
        x = cr["rs"][:, t:t + 1]

        def norms():
            m = [C.put(lambda e: e.activation(JUNK[:, 0:512], H[:, t, b * 512:(b + 1) * 512], ACT.Square,
                                              accum_out=ss[:, b:b + 1]), halves[b], (C.sem, C.count))
                 for b in range(2)]
            m = G.put(lambda e: e.tensor_tensor(x, ss[:, 0:1], ss[:, 1:2], ALU.add), m)
            cr["done"][t] = rsqrt(x, 1.0 / D, RMS_EPS, m)

        def turn(b):
            slot, bk, bfree = tbanks.take()
            for i in range(4):
                tok = PE.put(lambda e: e.transpose(
                    bk[:, i * P:(i + 1) * P], H[:, t, (4 * b + i) * P:(4 * b + i + 1) * P], ident[:, :]),
                    bfree, halves[b], mark=(i == 3))
            c = (layer * 8 + n) * DK + 4 * b
            g = GT[:, block, c:c + 4].unsqueeze(2).broadcast_to([P, 4, P])
            s_, tmp, tfree = atts.take()
            t4 = tmp.rearrange("p (k s) -> p k s", k=4)
            v = V.put(lambda e: e.tensor_tensor(t4, bk.rearrange("p (k s) -> p k s", k=4), g, ALU.mult),
                      tok, tfree)
            tbanks.give(slot, v)
            hi, lo = XH[:, 4 * b:4 * b + 4, t * P:(t + 1) * P], XL[:, 4 * b:4 * b + 4, t * P:(t + 1) * P]
            a = C.put(lambda e: e.activation(hi, t4, ACT.Copy), v, free)

            def low():
                w = V.put(lambda e: e.tensor_tensor(lo, t4, hi.bitcast(F32), ALU.subtract), a, free)
                atts.give(s_, w)
                for i in range(4):
                    cr["got"][(4 * b + i, t)] = [a, w]

            defer(1, low, True)

        defer(TURN0, lambda: turn(0), True)
        defer(TURN1, lambda: turn(1), True)
        defer(NORMS, norms)

    def squares(y, ss, *marks):
        return C.put(lambda e: e.activation(JUNK[:, 0:y.shape[-1]], y, ACT.Square, accum_out=ss),
                     *marks, (C.sem, C.count))

    def residual(gb, factor, pre, cr):
        slot_b, gbt, gb_done = gb
        ss, sm = cols(2 * T), cols(T)
        f2 = (pre * factor) ** 2
        half = {}

        def weigh(t, b, y, *marks):
            part, tmp = gbt[:, b * 512:(b + 1) * 512], TMP[:, t, b, 512:1024]
            return V.put(lambda e: e.tensor_tensor(tmp, y, part, ALU.mult), *marks, gb_done, tmp_used[0])

        def first(t, y, tok, sq):
            half[t] = [G.put(lambda e: e.tensor_scalar(sm[:, t:t + 1], ss[:, t:t + 1], pre * pre / D / f2,
                                                       RMS_EPS / f2, ALU.mult, ALU.add), sq),
                       weigh(t, 0, y, tok, sq)]

        def second(t, y, free, tok, sq):
            x = sm[:, t:t + 1]
            v0 = weigh(t, 1, y, tok, sq)
            m = V.put(lambda e: e.scalar_tensor_tensor(x, ss[:, T + t:T + t + 1], pre * pre / D / f2, x,
                                                       ALU.mult, ALU.add), half[t], sq)
            m = G.put(lambda e: e.tensor_tensor(x, x, NEG[:, 0:1], ALU.pow), m)
            halves = []
            for b in range(2):
                part = H[:, t, b * 512:(b + 1) * 512]
                tmp = TMP[:, t, b, 512:1024]
                v = V.put(lambda e: e.scalar_tensor_tensor(part, tmp, x, part, ALU.mult, ALU.add),
                          m, v0, h_done[t])
                halves.append(v)
            h_done[t] = v
            if cr is not None:
                carry_tile(cr, t, halves, free)
            if t == T - 1:
                bc.give(slot_b, v)
                tmp_used[0] = v
                carry[0] = cr
            return v0

        return ss, first, second

    def project(xh, xl, nk, w, gain, factor, ready, nxt):
        cr = carry_on(nxt) if nxt else None
        ss, first, second = residual(broadcast(gain), factor, 1.0, cr)
        slots = {}
        over = [None] * T

        def early(b, t, slot, pair, tok):
            slots[b] = slot
            sq = squares(pair[t], ss[:, b * T + t:b * T + t + 1], tok)
            if b == 0:
                first(t, pair[t], tok, sq)
            else:
                over[t] = second(t, pair[t], tok, tok, sq)
                if t == T - 1:
                    for s_ in slots.values():
                        pairs.give(s_, *over)

        wv = w.rearrange("(k p) n -> p k n", p=P)
        blocks = [(512, lambda k0, k1, b=b: wv[:, k0:k1, b * 512:(b + 1) * 512]) for b in range(2)]
        last = linear(xh, xl, nk, blocks, None, ready, tail=TAIL, early=early)
        flush()
        return last

    def ffn(block, layer, i, w13, w2, norm_g, nxt):
        rs, rs_done, ready = prenorm(block, layer, 4 * i)
        sc = cols(2 * T)
        sc_done = []
        wv = w13.rearrange("(k p) (s n) -> p k s n", p=P, s=2)
        blocks = [(512, lambda k0, k1, b=b: wv[:, k0:k1, :, b * FB:(b + 1) * FB])
                  for b in range(FF // FB)]
        aready = {}

        def consume(b, slot, pair, toks):
            if not sc_done:
                m = G.put(lambda e: e.tensor_scalar(sc[:, 0:T], rs, 0.5, None, ALU.mult), rs_done())
                sc_done.append(G.put(lambda e: e.tensor_tensor(sc[:, T:2 * T], sc[:, 0:T], rs, ALU.mult), m))
            n, th, free = atts.take()
            over = []
            for t in range(T):
                tt = th[:, t * FB:(t + 1) * FB]
                g_, u_ = pair[t][:, 0:FB], pair[t][:, FB:2 * FB]
                a = C.put(lambda e: e.activation(tt, g_, ACT.Tanh, scale=sc[:, t:t + 1]),
                          toks[t], sc_done, free)
                v = V.put(lambda e: e.scalar_tensor_tensor(tt, tt, 1.0, g_, ALU.add, ALU.mult), a)
                v = V.put(lambda e: e.scalar_tensor_tensor(
                    tt, tt, sc[:, T + t:T + t + 1], u_, ALU.mult, ALU.mult), v, sc_done)
                over.append(v)
            pairs.give(slot, *over)

            def later():
                r = spread(lambda k, t: th[:, t * FB + k * P:t * FB + (k + 1) * P], 2,
                           AH[:, 2 * b:2 * b + 2, :], AL[:, 2 * b:2 * b + 2, :], None,
                           lambda k, t: over[t], a_used[0])
                atts.give(n, (PE.sem, PE.count))
                aready[2 * b], aready[2 * b + 1] = r

            return later

        x_used[0] = linear(XH, XL, DK, blocks, consume, ready, head=HEAD)
        a_used[0] = project(AH, AL, FF // P, w2, norm_g[layer, 4 * i + 1], 0.5, same(aready), nxt)

    p_used, p_got = [None], [None]

    def ple_input(layer, p):
        p_in = pload.put(G, PT[:, :, :], p[layer, 0].rearrange("(t p) n -> p t n", p=P), p_used[0])

        def turn():
            p_got[0] = spread(lambda k, t: PT[:, t, k * P:(k + 1) * P], PD // P, PH, PL, None,
                              lambda k, t: [p_in, i_done], p_used[0])

        return turn

    def ple(block, layer, p, w_gate, w_proj, norm_g, nxt):
        if p_got[0] is None:
            ple_input(layer, p)()
        cr = carry_on(nxt) if nxt else None
        rs, rs_done, ready = prenorm(block, layer, 6)
        ss, first, second = residual(broadcast(norm_g[layer, 7]), 1.0, 0.5, cr)
        hr = cols(T)
        hr_done = []
        y = [[TMP[:, t, b, 0:512] for t in range(T)] for b in range(2)]
        wg = w_gate[layer].rearrange("(k p) n -> p k n", p=P)
        wp = w_proj[layer].rearrange("(k p) n -> p k n", p=P)
        em = {}

        def gate(b, t, slot, pair, tok):
            if not hr_done:
                hr_done.append(G.put(lambda e: e.tensor_scalar(hr, rs, 0.5, None, ALU.mult), rs_done()))
            n, th, free = atts.take()
            a = C.put(lambda e: e.activation(th[:, :], pair[t], ACT.Tanh, scale=hr[:, t:t + 1]),
                      tok, hr_done, free)
            over[t] = a
            v = V.put(lambda e: e.scalar_tensor_tensor(y[b][t], th[:, :], 1.0, y[b][t], ALU.add, ALU.mult),
                      a, em[(b, t)])
            atts.give(n, v)
            sq = squares(y[b][t], ss[:, b * T + t:b * T + t + 1], v)
            if t == T - 1:
                pairs.give(slot, *over)
            if b == 0:
                first(t, y[0][t], v, sq)
            else:
                second(t, y[1][t], tok, v, sq)

        over = [None] * T
        cut = lambda w: [(512, lambda k0, k1, b=b: w[:, k0:k1, b * 512:(b + 1) * 512]) for b in range(2)]
        def embed(b, t, slot, pair, tok):
            em[(b, t)] = C.put(lambda e: e.activation(y[b][t], pair[t], ACT.Copy), tok, tmp_used[0])
            if t == T - 1:
                pairs.give(slot, em[(b, 0)], em[(b, 1)])

        p_used[0] = linear(PH, PL, PD // P, cut(wp), None, same(p_got[0]), early=embed)
        x_used[0] = linear(XH, XL, DK, cut(wg), None, ready, tail=TAIL, early=gate)
        p_got[0] = None

    def gmlp():
        bs = MT[:, 48:56]
        U = at("gU", EO + 32768, [P, T, 2048], F32)
        W = at("gW", EO + 32768 + 16384, [P, 8, P], F32)
        yh = at("gYH", EO, [P, 16, S], F32R)
        yl = at("gYL", EO + 16384, [P, 16, S], F32R)
        e0 = a_used[0]
        w_in_done = single(G, U[:, 0, 0:1024].rearrange("p (g j) -> p g j", g=8),
                              A["a_w_s"][0].rearrange("g i j -> i g j"), a_used[0])
        rs, rs_done, ready = prenorm(0, 0, 2)
        mix = {}

        def turn_mix():
            for q in range(2):
                slot, b, free = tbanks.take()
                for i in range(4):
                    g = 4 * q + i
                    tok = PE.put(lambda e: e.transpose(
                        b[:, i * P:(i + 1) * P], U[:, 0, g * P:(g + 1) * P], ident[:, :]),
                        free, w_in_done, mark=(i == 3))
                a = C.put(lambda e: e.activation(
                    W[:, 4 * q:4 * q + 4, :], b.rearrange("p (g i) -> p g i", g=4), ACT.Copy),
                    tok, e0)
                tbanks.give(slot, a)
            mix["done"] = V.put(lambda e: e.memset(W[64:128, :, 0:64], 0.0), a)
            mix["read"] = tok

        defer(24, turn_mix)
        bsrc = A["a_b_in"][0]
        order = [4, 5, 6, 7, 0, 1, 2, 3]
        bcs = {}

        def bias(i):
            c = order[2 * i]
            bcs[i] = broadcast(bsrc[c * 512:c * 512 + 1024])

        bias(0)
        sums = cols(T * 4)
        wv = A["a_w_in"][0].rearrange("(k p) n -> p k n", p=P)
        blocks = [(512, lambda k0, k1, c=c: wv[:, k0:k1, c * 512:(c + 1) * 512]) for c in order]
        vdone, udone = [None] * T, {}
        v_norm = [None] * T

        def layer_norm():
            g0 = broadcast(A["a_v_gain"][0, 0:1024])
            mean = cols(T)
            nmean = cols(T)
            var = cols(2 * T)
            m = V.put(lambda e: e.tensor_reduce(mean, sums.rearrange("p (t b) -> p t b", t=T), AX, ALU.add),
                      vdone[0], vdone[1])
            m = V.put(lambda e: e.tensor_scalar(nmean, mean, -1.0 / 2048, None, ALU.mult), m)
            for t in range(T):
                for a_ in range(2):
                    s_ = C.put(lambda e, t=t, a_=a_: e.activation(
                        JUNK[:, :], TMP[:, t, a_, :], ACT.Square, bias=nmean[:, t:t + 1],
                        accum_out=var[:, a_ * T + t:a_ * T + t + 1]), m, (C.sem, C.count))
            r = cols(T)
            v = V.put(lambda e: e.tensor_tensor(r, var[:, 0:T], var[:, T:2 * T], ALU.add), s_)
            r_done = rsqrt(r, 1.0 / 2048, LN_EPS, v)
            for a_ in range(2):
                gg = g0 if a_ == 0 else broadcast(A["a_v_gain"][0, 1024:2048])
                for t in range(T):
                    x = TMP[:, t, a_, :]
                    v = V.put(lambda e, x=x, t=t: e.tensor_scalar(
                        x, x, nmean[:, t:t + 1], r[:, t:t + 1], ALU.add, ALU.mult), r_done, s_, m)
                    v = V.put(lambda e, x=x, gg=gg: e.tensor_tensor(x, x, gg[1][:, :], ALU.mult), v, gg[2])
                    v_norm[t] = v
                bc.give(gg[0], v)

        def consume(b, slot, pair, tok):
            c = order[b]
            i = b // 2
            bslot, bb, b_done = bcs[i]
            v = None
            for t in range(T):
                n, z, free = atts.take()
                v = V.put(lambda e, t=t, z=z: e.scalar_tensor_tensor(
                    z[:, :], pair[t], rs[:, t:t + 1], bb[:, (b % 2) * 512:(b % 2) * 512 + 512],
                    ALU.mult, ALU.add), tok, rs_done(), b_done, free)
                if c >= 4:
                    dst = TMP[:, t, (c - 4) // 2, (c % 2) * 512:(c % 2) * 512 + 512]
                    a = C.put(lambda e, z=z, dst=dst, t=t: e.activation(
                        dst, z[:, :], ACT.Gelu_apprx_tanh, accum_out=sums[:, t * 4 + c - 4:t * 4 + c - 3]),
                        v, tmp_used[0])
                    vdone[t] = a
                else:
                    dst = U[:, t, c * 512:(c + 1) * 512]
                    a = C.put(lambda e, z=z, dst=dst: e.activation(
                        dst, z[:, :], ACT.Gelu_apprx_tanh), v, mix["read"], e0)
                    udone[(t, c)] = a
                atts.give(n, a)
            pairs.give(slot, v)
            if b % 2 == 1:
                bc.give(bslot, v)
                if i < 3:
                    bias(i + 1)
            if b == 3:
                layer_norm()

        x_used[0] = linear(XH, XL, DK, blocks, consume, ready, head=HEAD)
        ydone = {}
        for g2 in range(4):
            slot, pair, free = pairs.take()
            for t in range(T):
                for i in range(2):
                    g = 2 * g2 + i
                    tok = PE.put(lambda e, t=t, g=g, i=i, pair=pair: e.matmul(
                        pair[t][:, i * 256:(i + 1) * 256], W[:, g, :],
                        TMP[:, t, g // 4, (g % 4) * 256:(g % 4) * 256 + 256], start=True, stop=True),
                        free, mix["done"], v_norm[t])
                for i in range(2):
                    g = 2 * g2 + i
                    u = U[:, t, g * 256:(g + 1) * 256]
                    v = V.put(lambda e, t=t, g=g, i=i, u=u, pair=pair: e.scalar_tensor_tensor(
                        u, pair[t][:, i * 256:(i + 1) * 256], bs[:, g:g + 1], u, ALU.add, ALU.mult),
                        tok, udone[(t, g // 2)])
                    ydone[(t, g)] = v
            pairs.give(slot, v)
        tmp_used[0] = tok
        ready = spread(lambda k, t: U[:, t, k * P:(k + 1) * P], 16, yh, yl, None,
                       lambda k, t: ydone[(t, k // 2)], a_used[0])
        a_used[0] = project(yh, yl, 16, A["a_w_out"][0], A["norm_g"][0, 3], 1.0, same(ready), (0, 0, 4))


    def rwkv():
        wide = [P, T, D]
        R = at("rR", EO, wide, F32)
        K = at("rK", EO + 8192, wide, F32)
        VV = at("rV", EO + 16384, wide, F32)
        LW = at("rLW", EO + 24576, wide, F32)
        AA = at("rAA", EO + 32768, wide, F32)
        GG = at("rGG", EO + 40960, wide, F32)
        MK = at("rMK", EO + 49152, [P, 10, P], BF16)
        CU = at("rCU", EO + 49152 + 2560, [P, 2 * P + 2], F32)
        SM = at("rSM", EO + 49152 + 2560 + 1056, [P, 256], F32)
        W2 = at("rW2", EO + 49152 + 2560 + 1056 + 1024, [P, D], F32)
        HT = at("rHT", TO, [P, DK, S], F32)
        DX = at("rDX", TO + 8192, [P, DK, S], F32)
        KK = at("rKK", TO, wide, F32)
        TB = at("rTB", TO + 8192, wide, F32)
        nr = A["norm_g"]
        e0 = a_used[0]
        mk_in = single(G, MK[:, :, :], A["c_masks"], e0)
        cu_in = single(G, CU[:, :], A["c_cum"], e0)
        ss = cols(T)
        m = [squares(H[:, t, :], ss[:, t:t + 1], h_done[t]) for t in range(T)]
        rs_done = rsqrt(ss, 1.0 / D, RMS_EPS, m[-1])
        hn = [V.put(lambda e, t=t: e.tensor_scalar(R[:, t, :], H[:, t, :], ss[:, t:t + 1], None, ALU.mult),
                    rs_done, h_done[t], e0) for t in range(T)]
        gain = gain_cols(0, 1, 2)
        hdone = []
        for k in range(0, DK, 2):
            slot, b, free = tbanks.take()
            for i in range(2):
                for t in range(T):
                    tok = PE.put(lambda e, k=k, i=i, t=t, b=b: e.transpose(
                        b[:, i * S + t * P:i * S + (t + 1) * P], R[:, t, (k + i) * P:(k + i + 1) * P],
                        ident[:, :]), free, hn[t], mark=(i == 1 and t == 1))
            for i in range(2):
                a = C.put(lambda e, k=k + i, i=i, b=b: e.activation(
                    HT[:, k, :], b[:, i * S:(i + 1) * S], ACT.Copy, scale=gain[:, k:k + 1]),
                    tok, tmp_used[0])
                hdone.append(a)
            tbanks.give(slot, a)
        ht_read = tok
        v = V.put(lambda e: e.tensor_scalar(DX[:, :, 0:1], HT[:, :, 0:1], -1.0, None, ALU.mult),
                  hdone[-1], tmp_used[0])
        dx = V.put(lambda e: e.tensor_tensor(DX[:, :, 1:S], HT[:, :, 0:S - 1], HT[:, :, 1:S], ALU.subtract),
                   hdone[-1], v)
        LO = at("rLO", EO + 24576, [P, DK, S], F32)
        W1 = at("rW1", EO + 32768, [P, DK, 160], F32)
        lora = {}

        def mix(n, dst, *marks):
            out_ = []
            for k in range(DK):
                out_.append(V.put(lambda e, k=k: e.scalar_tensor_tensor(
                    dst[:, k, :], DX[:, k, :], MT[:, n * DK + k:n * DK + k + 1], HT[:, k, :],
                    ALU.mult, ALU.add), dx, *marks))
            return out_

        lread, w1read = e0, e0
        TH = at("rTH", AO, [P, 4, S], F32)
        th_done = {}
        att_free = [f for f in atts.free]
        for n, name, width in ((5, "b_g1", 160), (4, "b_a1", 64), (3, "b_w1", 64)):
            w_in = single(G, W1[:, :, 0:width], A[name][0].rearrange("(k p) n -> p k n", p=P), w1read)
            xs = mix(n, LO, lread)
            slot, pair, free = pairs.take()
            for part in range((width + P - 1) // P):
                c0, c1 = part * P, min(width, part * P + P)
                for k in range(DK):
                    tok = PE.put(lambda e, k=k, c0=c0, c1=c1, part=part, pair=pair: e.matmul(
                        pair[part][0:c1 - c0, 0:S], W1[:, k, c0:c1], LO[:, k, :],
                        start=(k == 0), stop=(k == DK - 1)), free, w_in, xs[k], mark=(k == DK - 1))
            lread, w1read = tok, tok
            if n == 5:
                a = C.put(lambda e, pair=pair: e.activation(TH[:, 0, 0:S], pair[0][:, 0:S], ACT.Tanh,
                                                            scale=0.5), tok, *att_free)
                a = C.put(lambda e, pair=pair: e.activation(TH[0:32, 1, 0:S], pair[1][0:32, 0:S], ACT.Tanh,
                                                            scale=0.5), tok)
                v = V.put(lambda e: e.tensor_scalar(TH[:, 0, 0:S], TH[:, 0, 0:S], 1.0, 0.5, ALU.add,
                                                    ALU.mult), a)
                v = V.put(lambda e: e.tensor_scalar(TH[0:32, 1, 0:S], TH[0:32, 1, 0:S], 1.0, 0.5, ALU.add,
                                                    ALU.mult), a)
                th_done[n] = v
            elif n == 4:
                a = C.put(lambda e, pair=pair: e.activation(TH[0:64, 2, 0:S], pair[0][0:64, 0:S], ACT.Copy),
                          tok)
                th_done[n] = a
            else:
                a = C.put(lambda e, pair=pair: e.activation(TH[64:128, 2, 0:S], pair[0][0:64, 0:S], ACT.Tanh),
                          tok)
                th_done[n] = a
            pairs.give(slot, a)

        w2read = e0
        gdone, adone, wdone = {}, {}, {}

        def second(name, parts, evac):
            nonlocal w2read
            w_ins = []
            for i, (p0, p1, blk, r0, r1) in enumerate(parts):
                assert i == 0 or p1 - p0 <= 32
                dst = W2[p0:p1, :] if i == 0 else bc3[p0:p1, :]
                w_ins.append(single(G, dst, A[name][0][r0:r1, :], w2read))
            for b in range(2):
                slot, pair, free = pairs.take()
                for t in range(T):
                    for i, (p0, p1, blk, r0, r1) in enumerate(parts):
                        w_ = W2[p0:p1, b * 512:(b + 1) * 512] if i == 0 else bc3[p0:p1, b * 512:(b + 1) * 512]
                        tok = PE.put(lambda e, t=t, w_=w_, p0=p0, p1=p1, blk=blk, i=i, pair=pair: e.matmul(
                            pair[t], TH[p0:p1, blk, t * P:(t + 1) * P], w_,
                            start=(i == 0), stop=(i == len(parts) - 1)), free, w_ins, list(th_done.values()))
                evac(b, slot, pair, tok)
            w2read = tok

        n3, bc3, free3 = bc.take()
        G.wait(free3)

        def g_evac(b, slot, pair, tok):
            for t in range(T):
                a = C.put(lambda e, t=t, pair=pair: e.activation(GG[:, t, b * 512:(b + 1) * 512], pair[t],
                                                                 ACT.Copy), tok, e0)
            pairs.give(slot, a)
            gdone[0] = a

        second("b_g2", [(0, 128, 0, 0, 128), (0, 32, 1, 128, 160)], g_evac)
        a0b = broadcast(A["b_a0"][0])

        def a_evac(b, slot, pair, tok):
            for t in range(T):
                dst = AA[:, t, b * 512:(b + 1) * 512]
                v = V.put(lambda e, t=t, dst=dst, pair=pair: e.tensor_tensor(
                    dst, pair[t], a0b[1][:, b * 512:(b + 1) * 512], ALU.add), tok, a0b[2], w1read)
                a = C.put(lambda e, dst=dst: e.activation(dst, dst, ACT.Tanh, scale=0.5), v)
                v2 = V.put(lambda e, dst=dst: e.tensor_scalar(dst, dst, 1.0, 0.5, ALU.add, ALU.mult), a)
            pairs.give(slot, v)
            adone[0] = v2

        second("b_a2", [(0, 64, 2, 0, 64)], a_evac)
        bc.give(a0b[0], adone[0])
        w0b = broadcast(A["b_w0"][0])

        def w_evac(b, slot, pair, tok):
            for t in range(T):
                dst = LW[:, t, b * 512:(b + 1) * 512]
                v = V.put(lambda e, t=t, dst=dst, pair=pair: e.tensor_tensor(
                    dst, pair[t], w0b[1][:, b * 512:(b + 1) * 512], ALU.add), tok, w0b[2], lread)
                a = C.put(lambda e, dst=dst: e.activation(dst, dst, ACT.Tanh, scale=0.5), v)
                v2 = V.put(lambda e, dst=dst: e.tensor_scalar(dst, dst, 1.0, -0.5 * EXP_HALF, ALU.add,
                                                              ALU.mult), a)
            pairs.give(slot, v)
            wdone[0] = v2

        second("b_w2", [(64, 128, 2, 0, 64)], w_evac)
        bc.give(w0b[0], wdone[0])
        bc.give(n3, w2read)
        for i in range(3):
            atts.free[i] = [w2read]

        wv = A["b_w_in"][0].rearrange("n (k p) e -> n p k e", p=P)
        rkv_done = {}
        for n, dst in enumerate((R, K, VV)):
            rdy = []
            for k in range(DK):
                s_, x, free = atts.take()
                v0 = V.put(lambda e, k=k, x=x: e.scalar_tensor_tensor(
                    x[:, 0:S], DX[:, k, :], MT[:, n * DK + k:n * DK + k + 1], HT[:, k, :],
                    ALU.mult, ALU.add), dx, free)
                a = C.put(lambda e, k=k, x=x: e.activation(XH[:, k, :], x[:, 0:S], ACT.Copy), v0, x_used[0])
                v = V.put(lambda e, k=k, x=x: e.tensor_tensor(
                    XL[:, k, :], x[:, 0:S], XH[:, k, :].bitcast(F32), ALU.subtract), a, x_used[0])
                atts.give(s_, v)
                rdy.append([a, v])

            def consume(b, slot, pair, tok, dst=dst, n=n):
                for t in range(T):
                    a = C.put(lambda e, t=t: e.activation(dst[:, t, b * 512:(b + 1) * 512], pair[t],
                                                          ACT.Copy), tok, ht_read, e0)
                    rkv_done[(n, b, t)] = a
                pairs.give(slot, a)

            blocks = [(512, lambda k0, k1, b=b, n=n: wv[n][:, k0:k1, b * 512:(b + 1) * 512])
                      for b in range(2)]
            x_used[0] = linear(XH, XL, DK, blocks, consume, same(rdy))
        rkv = rkv_done[(2, 1, 1)]
        fl = lambda x: x.rearrange("p t (h n) -> p (t h) n", n=HD)

        b1 = broadcast(A["b_k_k"][0])
        b2 = broadcast(A["b_k_a"][0])
        n2, inv = SM[:, 0:32], SM[:, 32:64]
        kkd = []
        for t in range(T):
            v = V.put(lambda e, t=t: e.tensor_tensor(KK[:, t, :], K[:, t, :], b1[1][:, :], ALU.mult),
                      b1[2], rkv, dx, [(V.sem, V.count)])
            v = V.put(lambda e, t=t: e.tensor_tensor(TB[:, t, :], KK[:, t, :], KK[:, t, :], ALU.mult), v)
        v = V.put(lambda e: e.tensor_reduce(n2, fl(TB[:, :, :]), AX, ALU.add), v)
        v = V.put(lambda e: e.tensor_scalar(n2, n2, 1e-24, None, ALU.max), v)
        g = G.put(lambda e: e.tensor_tensor(inv, n2, NEG[:, 0:32], ALU.pow), v)
        kk = V.put(lambda e: e.tensor_tensor(fl(KK[:, :, :]), fl(KK[:, :, :]),
                                             inv.unsqueeze(2).broadcast_to([P, 32, HD]), ALU.mult), g)
        for t in range(T):
            v = V.put(lambda e, t=t: e.scalar_tensor_tensor(
                TB[:, t, :], AA[:, t, :], -1.0, b2[1][:, :], ALU.add, ALU.mult), b2[2], adone[0], kk)
            v = V.put(lambda e, t=t: e.scalar_tensor_tensor(
                K[:, t, :], TB[:, t, :], 1.0, K[:, t, :], ALU.add, ALU.mult), v)
        bc.give(b1[0], v)
        bc.give(b2[0], v)
        kd = v
        bb = V.put(lambda e: e.tensor_tensor(AA[:, :, :], KK[:, :, :], AA[:, :, :], ALU.mult), kd, kk)
        b3 = broadcast(A["b_r_k"][0].rearrange("h n -> (h n)"))
        v = V.put(lambda e: e.tensor_tensor(TB[:, :, :], R[:, :, :], K[:, :, :], ALU.mult), kd)
        for t in range(T):
            v = V.put(lambda e, t=t: e.tensor_tensor(TB[:, t, :], TB[:, t, :], b3[1][:, :], ALU.mult),
                      v, b3[2])
        bon = SM[:, 64:96]
        bon_done = V.put(lambda e: e.tensor_reduce(bon, fl(TB[:, :, :]), AX, ALU.add), v)
        bc.give(b3[0], v)
        tin, tex = CU[:, 0:P], CU[:, P:2 * P]
        scan_in = {}
        for t in range(T):
            for b in range(2):
                slot, pair, free = pairs.take()
                c = slice(b * 512, (b + 1) * 512)
                tok = PE.put(lambda e, t=t, c=c, pair=pair: e.matmul(
                    pair[0], tin, LW[:, t, c], start=True, stop=True), free, cu_in, wdone[0])
                tok2 = PE.put(lambda e, t=t, c=c, pair=pair: e.matmul(
                    pair[1], tex, LW[:, t, c], start=True, stop=True))
                s1, e1, f1 = atts.take()
                s2, e2, f2 = atts.take()
                s3, e3, f3 = atts.take()
                a1 = C.put(lambda e, e1=e1, pair=pair: e.activation(e1[:, :], pair[0], ACT.Exp), tok, f1)
                a2 = C.put(lambda e, e2=e2, pair=pair: e.activation(e2[:, :], pair[0], ACT.Exp, scale=-1.0),
                           tok, f2)
                a3 = C.put(lambda e, e3=e3, pair=pair: e.activation(e3[:, :], pair[1], ACT.Exp), tok2, f3)
                pairs.give(slot, a3)
                v1 = V.put(lambda e, e1=e1, t=t, c=c: e.tensor_tensor(R[:, t, c], R[:, t, c], e1[:, :],
                                                                      ALU.mult), a1, bon_done)
                v2 = V.put(lambda e, e2=e2, t=t, c=c: e.tensor_tensor(K[:, t, c], K[:, t, c], e2[:, :],
                                                                      ALU.mult), a2)
                v3 = V.put(lambda e, e2=e2, t=t, c=c: e.tensor_tensor(AA[:, t, c], AA[:, t, c], e2[:, :],
                                                                      ALU.mult), bb)
                v4 = V.put(lambda e, e3=e3, t=t, c=c: e.scalar_tensor_tensor(
                    KK[:, t, c], KK[:, t, c], -1.0, e3[:, :], ALU.mult, ALU.mult), a3, bb)
                atts.give(s1, v1)
                atts.give(s2, v3)
                atts.give(s3, v4)
                scan_in[(t, b)] = v4
        slot, pair, free = pairs.take()
        for t in range(T):
            for p in range(8):
                tok = PE.put(lambda e, t=t, p=p, pair=pair: e.matmul(
                    pair[0][:, p:p + 1], LW[:, t, p * P:(p + 1) * P], CU[:, 2 * P + t:2 * P + t + 1],
                    start=(t == 0 and p == 0), stop=(t == 1 and p == 7), skip_group_check=True), free)
        scl = SM[:, 96:104]
        scl_done = C.put(lambda e, pair=pair: e.activation(scl, pair[0][:, 0:8], ACT.Exp), tok)
        pairs.give(slot, scl_done)

        allbanks = Ring([bank(i) for i in range(8)])
        for i in range(3):
            allbanks.free[2 * i] = list(pairs.free[i])
            allbanks.free[2 * i + 1] = list(pairs.free[i])
        for i in range(2):
            allbanks.free[6 + i] = list(tbanks.free[i])
        maps = []
        before = [x_used[0], [f for f in atts.free], scl_done, tok, scan_in[(1, 1)], bc.free[0], bc.free[1],
                  bc.free[2]]
        for s_, spots in enumerate((
                [XO, XO + 4096, XO + 8192, XO + 10240, XO + 12288, XO + 14336, AO, AO + 2048, AO + 3072],
                [TO + 8192, TO + 12288, EO + 24576, EO + 26624, EO + 28672, EO + 30720, BO, BO + 2048,
                 BO + 3072])):
            TT = at(f"sTT{s_}", spots[0], [P, 4, 2, P], F32)
            KR = at(f"sKR{s_}", spots[1], [P, 4, 2, P], F32)
            MR = at(f"sMR{s_}", spots[2], [P, 2, 2, 2, P], F32)
            XX = at(f"sXX{s_}", spots[4], [P, 4, P], F32)
            YY = at(f"sYY{s_}", spots[5], [P, 4, P], F32)
            WW = at(f"sWW{s_}", spots[6], [P, 4, P], F32)
            RH = at(f"sRH{s_}", spots[7], [P, 4, HD], F32)
            SA = at(f"sSA{s_}", spots[8], [P, 4, HD], F32)
            maps.append((TT, KR, MR, XX, YY, WW, RH, SA))
        S0 = at("sS0", BO + 4096, [P, 8, HD], F32)
        set_free = [before, before]
        s0_done = {}
        y_done = {}
        s0_free = before

        def mask(i, n):
            return MK[:, i, :].unsqueeze(1).broadcast_to([P, n, P])

        def group(c, q, s_):
            TT, KR, MR, XX, YY, WW, RH, SA = maps[s_]
            f0 = set_free[s_]
            srcs = (KK, R, AA, K)
            b4 = lambda b: b.rearrange("p (u n) -> p u n", u=4)
            for half in range(2):
                n, b, free = allbanks.take()
                for i in range(2):
                    for pr in range(2):
                        x = srcs[2 * half + i][:, c, (2 * q + pr) * P:(2 * q + pr + 1) * P]
                        tok = PE.put(lambda e, i=i, pr=pr, x=x, b=b: e.transpose(
                            b[:, (2 * i + pr) * P:(2 * i + pr + 1) * P], x, ident[:, :]),
                            free, scan_in[(c, q // 2)], mark=(i == 1 and pr == 1))
                dst = TT[:, 2 * half:2 * half + 2, :, :].rearrange("p a b n -> p (a b) n")
                if half == 0:
                    tt0 = C.put(lambda e, b=b, dst=dst: e.activation(dst, b4(b), ACT.Copy), tok, f0)
                    allbanks.give(n, tt0)
                else:
                    tt1 = V.put(lambda e, b=b, dst=dst: e.tensor_copy(dst, b4(b)), tok, f0)
                    allbanks.give(n, tt1)
            yield
            un = [(u, 2 * q + u // 2, slice((u % 2) * HD, (u % 2) * HD + HD)) for u in range(4)]
            for h2 in range(2):
                n, b, free = allbanks.take()
                for i, (l_, r_) in enumerate(((0, 2), (2, 1))):
                    for u, pr, hs in un[h2::2]:
                        tok = PE.put(lambda e: e.matmul(
                            b[:, (2 * i + u // 2) * P:(2 * i + u // 2 + 1) * P], TT[hs, l_, u // 2, :],
                            TT[hs, r_, u // 2, :], start=True, stop=True),
                            free, tt0, tt1, mark=(i == 1 and u >= 2))
                m02 = MK[:, 0:3:2, :].unsqueeze(2).broadcast_to([P, 2, 2, P])
                ma = V.put(lambda e: e.tensor_tensor(
                    MR[:, h2, :, :, :], b.rearrange("p (i u n) -> p i u n", i=2, u=2), m02, ALU.mult),
                    tok, f0, mk_in)
                allbanks.give(n, ma)
                n, b, free = allbanks.take()
                for u, pr, hs in un[h2::2]:
                    tok = PE.put(lambda e: e.matmul(
                        b[:, (u // 2) * 256:(u // 2) * 256 + 256].rearrange("p (i n) -> p i n", i=2),
                        TT[hs, 3, u // 2, :], TT[hs, 0:2, u // 2, :], start=True, stop=True),
                        free, mark=(u >= 2))
                m12 = MK[:, 1:3, :].rearrange("p a n -> p (a n)").unsqueeze(1).broadcast_to([P, 2, 2 * P])
                kr = V.put(lambda e: e.tensor_tensor(
                    KR[:, h2:4:2, :, :].rearrange("p u a n -> p u (a n)"),
                    b.rearrange("p (u n) -> p u n", u=2), m12, ALU.mult), tok, f0)
                allbanks.give(n, kr)
            rb = ma
            yield
            x_done = i_done
            y_done_ = i_done
            for lv in range(7):
                n, b, free = allbanks.take()
                for u in range(4):
                    y_ = ident[:, :] if lv == 0 else YY[:, u, :]
                    PE.put(lambda e, u=u, b=b, y_=y_: e.matmul(
                        b[:, u * P:(u + 1) * P], MR[:, u % 2, 0, u // 2, :], y_, start=True, stop=False),
                        free, ma, y_done_, mark=False)
                    tok = PE.put(lambda e, u=u, b=b: e.matmul(
                        b[:, u * P:(u + 1) * P], identb[:, :], identb[:, :], start=False, stop=True),
                        mark=(u == 3))
                W_ = YY if lv == 0 else WW
                w = V.put(lambda e, b=b, W_=W_, lv=lv: e.tensor_tensor(
                    W_[:, :, :], b4(b), mask(3 + lv, 4), ALU.mult), tok, f0)
                allbanks.give(n, w)
                yield
                if lv > 0:
                    n, b, free = allbanks.take()
                    for u in range(4):
                        tok = PE.put(lambda e, u=u, b=b: e.matmul(
                            b[:, u * P:(u + 1) * P], XX[:, u, :], WW[:, u, :], start=True, stop=True),
                            free, w, x_done, mark=(u == 3))
                    y_done_ = C.put(lambda e, b=b: e.activation(YY[:, :, :], b4(b), ACT.Copy), tok)
                    allbanks.give(n, y_done_)
                else:
                    y_done_ = w
                if lv < 6:
                    n, b, free = allbanks.take()
                    for u in range(4):
                        x_ = ident[:, :] if lv == 0 else XX[:, u, :]
                        tok = PE.put(lambda e, u=u, b=b, W_=W_, x_=x_: e.matmul(
                            b[:, u * P:(u + 1) * P], W_[:, u, :], x_, start=True, stop=True),
                            free, w, x_done, mark=(u == 3))
                    x_done = C.put(lambda e, b=b: e.activation(XX[:, :, :], b4(b), ACT.Copy), tok, f0)
                    allbanks.give(n, x_done)
                yield
            b64 = lambda b, k: b[:, 0:k * HD].rearrange("p (u n) -> p u n", u=k)
            vs = lambda pr, hs: VV[:, c, pr * P + hs.start:pr * P + hs.start + HD]
            for h2 in range(2):
                n, b, free = allbanks.take()
                for u, pr, hs in un[h2::2]:
                    o_ = b[:, (u // 2) * HD:(u // 2 + 1) * HD]
                    tok = PE.put(lambda e: e.matmul(
                        o_, KR[:, u, 0, :], vs(pr, hs), start=True, stop=(c == 0)), free, kr, rkv)
                    if c == 1:
                        tok = PE.put(lambda e: e.matmul(
                            o_, TT[hs, 0, u // 2, :], S0[hs, pr, :], start=False, stop=True), s0_done[q])
                a = C.put(lambda e: e.activation(RH[:, h2:4:2, :], b64(b, 2), ACT.Copy), tok, f0)
                allbanks.give(n, a)
            yield
            n, b, free = allbanks.take()
            for u in range(4):
                tok = PE.put(lambda e: e.matmul(
                    b[:, u * HD:(u + 1) * HD], YY[:, u, :], RH[:, u, :], start=True, stop=True),
                    free, a, y_done_, mark=(u == 3))
            a = C.put(lambda e: e.activation(SA[:, :, :], b64(b, 4), ACT.Copy), tok, f0)
            allbanks.give(n, a)
            yield
            for h2 in range(2):
                n, b, free = allbanks.take()
                for u, pr, hs in un[h2::2]:
                    o_ = b[:, (u // 2) * HD:(u // 2 + 1) * HD]
                    PE.put(lambda e: e.matmul(
                        o_, KR[:, u, 1, :], vs(pr, hs), start=True, stop=False), free, mark=False)
                    if c == 1:
                        PE.put(lambda e: e.matmul(
                            o_, TT[hs, 1, u // 2, :], S0[hs, pr, :], start=False, stop=False), mark=False)
                    tok = PE.put(lambda e: e.matmul(
                        o_, MR[:, u % 2, 1, u // 2, :], SA[:, u, :], start=False, stop=True), a, rb)
                yo = R[:, c, q * 256:(q + 1) * 256].rearrange("p (u h n) -> p h u n", h=2, n=HD)[:, h2, :, :]
                y = C.put(lambda e: e.activation(yo, b64(b, 2), ACT.Copy), tok)
                allbanks.give(n, y)
            y_done[(c, q)] = y
            if c == 0:
                n, b, free = allbanks.take()
                for u, pr, hs in un:
                    o_ = b[hs, (u // 2) * HD:(u // 2) * HD + HD]
                    ch = slice(pr * P + hs.start, pr * P + hs.start + HD)
                    PE.put(lambda e, u=u, o_=o_, ch=ch: e.matmul(
                        o_, AA[:, 0, ch], SA[:, u, :], start=True, stop=False), free, mark=False)
                    tok = PE.put(lambda e, o_=o_, ch=ch: e.matmul(
                        o_, K[:, 0, ch], VV[:, 0, ch], start=False, stop=True))
                for i in range(2):
                    s0_done[q] = V.put(lambda e, i=i, b=b: e.tensor_scalar(
                        S0[:, 2 * q + i, :], b[:, i * HD:(i + 1) * HD], scl[:, 2 * q + i:2 * q + i + 1], None,
                        ALU.mult), tok, s0_free, scl_done)
                allbanks.give(n, s0_done[q])
            set_free[s_] = [tok, y, (V.sem, V.count)]

        for c in range(2):
            for q in (0, 2):
                gens = [group(c, q, 0), group(c, q + 1, 1)]
                while gens:
                    for g_ in list(gens):
                        try:
                            next(g_)
                        except StopIteration:
                            gens.remove(g_)
        for i in range(3):
            pairs.free[i] = [allbanks.free[2 * i], allbanks.free[2 * i + 1]]
        for i in range(2):
            tbanks.free[i] = allbanks.free[6 + i]
        over = [set_free[0], set_free[1]]
        for i in range(3):
            atts.free[i] = over
            bc.free[i] = over
        l0 = broadcast(A["b_lnx"][0, 0])
        l1 = broadcast(A["b_lnx"][0, 1])
        mean, var = SM[:, 128:160], SM[:, 160:192]
        x3 = fl(R[:, :, :])
        t3 = fl(TB[:, :, :])
        v = V.put(lambda e: e.tensor_reduce(mean, x3, AX, ALU.add), list(y_done.values()))
        v = V.put(lambda e: e.tensor_scalar(mean, mean, 1.0 / HD, None, ALU.mult), v)
        v = V.put(lambda e: e.tensor_tensor(x3, x3, mean.unsqueeze(2).broadcast_to([P, 32, HD]),
                                            ALU.subtract), v)
        v = V.put(lambda e: e.tensor_tensor(t3, x3, x3, ALU.mult), v, over)
        v = V.put(lambda e: e.tensor_reduce(var, t3, AX, ALU.add), v)
        g = rsqrt(var, 1.0 / HD, GN_EPS, v)
        v = V.put(lambda e: e.tensor_tensor(x3, x3, var.unsqueeze(2).broadcast_to([P, 32, HD]),
                                            ALU.mult), g)
        w = V.put(lambda e: e.tensor_tensor(t3, fl(VV[:, :, :]), bon.unsqueeze(2).broadcast_to([P, 32, HD]),
                                            ALU.mult), over)
        yd = []
        for t in range(T):
            v = V.put(lambda e, t=t: e.tensor_tensor(R[:, t, :], R[:, t, :], l0[1][:, :], ALU.mult), v, l0[2])
            v = V.put(lambda e, t=t: e.tensor_tensor(TB[:, t, :], TB[:, t, :], l1[1][:, :], ALU.add), w, l1[2])
            v = V.put(lambda e, t=t: e.tensor_tensor(R[:, t, :], R[:, t, :], TB[:, t, :], ALU.add), v)
            v = V.put(lambda e, t=t: e.tensor_tensor(R[:, t, :], R[:, t, :], GG[:, t, :], ALU.mult), v, gdone[0])
            yd.append(v)
        bc.give(l0[0], v)
        bc.give(l1[0], v)
        tmp_used[0] = v
        ready = spread(lambda k, t: R[:, t, k * P:(k + 1) * P], DK, XH, XL, None,
                       lambda k, t: yd[t], over)
        x_used[0] = project(XH, XL, DK, A["b_w_out"][0], nr[1, 3], 1.0, same(ready), (0, 1, 4))
        a_used[0] = [x_used[0], (V.sem, V.count)]

    def rope(x, nh, RP, TR, *marks):
        for t in range(T):
            x4 = x[:, t, :].rearrange("p (h n) -> p h n", n=HD)
            a, b = x4[:, :, 0:8], x4[:, :, 8:16]
            cs, sn = (RP[:, i, t, :].unsqueeze(1).broadcast_to([P, nh, 8]) for i in range(2))
            tr = [TR[:, i, t, 0:nh * 8].rearrange("p (h n) -> p h n", n=8) for i in range(4)]
            m = [V.put(lambda e, i=i, y=y, z=z: e.tensor_tensor(tr[i], y, z, ALU.mult), *marks,
                       (V.sem, V.count)) for i, (y, z) in enumerate(((a, cs), (b, sn), (b, cs), (a, sn)))]
            V.put(lambda e: e.tensor_tensor(a, tr[0], tr[1], ALU.subtract), m[3])
            v = V.put(lambda e: e.tensor_tensor(b, tr[2], tr[3], ALU.add), m[3])
        return v

    def dilated():
        QT = at("dQT", EO, [P, 12, S], F32)
        KT = at("dKT", EO + 12288, [P, 12, S], F32)
        VD = at("dVD", EO + 24576, [P, T, 3, 512], F32)
        MK = at("dMK", EO + 36864, [P, T, 3 * S], BF16)
        RP = at("dRP", EO + 39936, [P, 2, T, 8], F32)
        TR = at("dTR", EO + 40064, [P, 4, T, 64], F32)
        PS = [at(f"dPS{i}", EO + 42112 + i * 3072, [P, 3 * S], F32) for i in range(2)]
        PTs = [at(f"dPT{i}", EO + 48256 + i * 3072, [P, 6, P], F32) for i in range(2)]
        SM = at("dSM", EO + 54400, [P, 64], F32)
        QS = [TMP[:, :, i, 0:512] for i in range(2)]
        OO = at("dOO", EO + 54656, [P, T, 512], F32)
        e0 = a_used[0]
        in1 = [single(G, MK[:, :, :], A["c_dil"], e0), single(G, RP[:, :, :, :], A["c_rope"], e0)]
        rs, rs_done, ready = prenorm(1, 0, 2)
        wv = A["a_wqkv_2"][0].rearrange("(k p) n -> p k n", p=P)
        blocks = [(512, lambda k0, k1, c=c: wv[:, k0:k1, c * 512:(c + 1) * 512]) for c in range(9)]
        qs = Ring(QS)
        qs.free = [[tmp_used[0]], [tmp_used[0]]]
        kt_done, vd_done = [], []

        def consume(b, slot, pair, tok):
            if b >= 6:
                for t in range(T):
                    a = C.put(lambda e, t=t: e.activation(VD[:, t, b - 6, :], pair[t], ACT.Copy,
                                                          scale=rs[:, t:t + 1]), tok, rs_done(), e0)
                vd_done.append(a)
                pairs.give(slot, a)
                return None
            n, x, free = qs.take()
            for t in range(T):
                a = C.put(lambda e, t=t: e.activation(x[:, t, :], pair[t], ACT.Copy, scale=rs[:, t:t + 1]),
                          tok, rs_done(), free)
            pairs.give(slot, a)
            v = rope(x, 8, RP, TR, a, in1, e0)

            def later():
                dst, g = (QT, b) if b < 3 else (KT, b - 3)
                for p in range(0, 4, 2):
                    tslot, bk, tfree = tbanks.take()
                    for i in range(2):
                        for t in range(T):
                            tok = PE.put(lambda e, p=p, i=i, t=t, bk=bk: e.transpose(
                                bk[:, i * S + t * P:i * S + (t + 1) * P],
                                x[:, t, (p + i) * P:(p + i + 1) * P], ident[:, :]),
                                tfree, v, a, mark=(i == 1 and t == 1))
                    w = V.put(lambda e, p=p, bk=bk: e.tensor_copy(
                        dst[:, 4 * g + p:4 * g + p + 2, :], bk.rearrange("p (i s) -> p i s", i=2)), tok, e0)
                    tbanks.give(tslot, w)
                    kt_done.append(w)
                qs.give(n, tok)

            return later

        x_used[0] = linear(XH, XL, DK, blocks, consume, ready, head=HEAD)
        flush()
        sc = Ring([0, 1])
        sc.free = [pairs.free[0] + pairs.free[2], pairs.free[1] + pairs.free[2]]
        ob = Ring([bank(4), bank(5)])
        ob.free = [pairs.free[2], pairs.free[2]]
        pr_ring, pt_ring = Ring(PS), Ring(PTs)
        pr_ring.free = pt_ring.free = [[e0], [e0]]
        pt_ring.free = [[e0], [e0]]
        odone = {}
        steps = [(hd, t) for hd in range(8) for t in range(T)]
        state = {}

        def first(i):
            hd, t = steps[i]
            pr, hs = hd // 2, slice((hd % 2) * HD, (hd % 2) * HD + HD)
            n, s_, free = sc.take()
            for g in range(3):
                o_ = banks_t[s_][:, g * S:(g + 1) * S]
                PE.put(lambda e, g=g, o_=o_: e.matmul(
                    o_, QT[hs, 4 * g + pr, t * P:(t + 1) * P], KT[hs, 4 * g + pr, :],
                    start=True, stop=False), free, kt_done[-1], mark=False)
                tok = PE.put(lambda e, g=g, o_=o_: e.matmul(
                    o_, identb[:, :], MK[:, t, g * S:(g + 1) * S], start=False, stop=True),
                    in1, mark=(g == 2))
            c = 4 * (i % 4)
            mx, nm, den = SM[:, c:c + 1], SM[:, c + 1:c + 2], SM[:, c + 2:c + 3]
            rd = SM[:, c + 3:c + 4]
            old = state.get(i - 4)
            v = V.put(lambda e: e.tensor_reduce(mx, banks_t[s_][:, 0:3 * S], AX, ALU.max), tok, e0,
                      old[-1] if old else None)
            v = V.put(lambda e: e.tensor_scalar(nm, mx, -0.125, None, ALU.mult), v)
            m, pp, pfree = pr_ring.take()
            a = C.put(lambda e: e.activation(pp[:, :], banks_t[s_][:, 0:3 * S], ACT.Exp, bias=nm, scale=0.125,
                                             accum_out=den), v, pfree)
            sc.give(n, a)
            v = V.put(lambda e: e.reciprocal(rd, den), a)
            state[i] = [m, pp, a, rd, v]

        def second(i):
            hd, t = steps[i]
            m, pp, a, rd, rdone = state[i]
            k, pt, tfree = pt_ring.take()
            ev = []
            for h2, (j0, j1) in enumerate(((0, 4), (4, 6))):
                slot, bk, free = tbanks.take()
                for j in range(j0, j1):
                    tok = PE.put(lambda e, j=j, bk=bk: e.transpose(
                        bk[:, (j - j0) * P:(j - j0 + 1) * P], pp[:, j * P:(j + 1) * P], ident[:, :]),
                        free, a, mark=(j == j1 - 1))
                src = bk[:, 0:(j1 - j0) * P].rearrange("p (j n) -> p j n", n=P)
                if h2 == 0:
                    w = V.put(lambda e, src=src: e.tensor_copy(pt[:, 0:4, :], src), tok, tfree)
                else:
                    w = C.put(lambda e, src=src: e.activation(pt[:, 4:6, :], src, ACT.Copy), tok, tfree)
                tbanks.give(slot, w)
                ev.append(w)
            pr_ring.give(m, tok)
            n, b, free = ob.take()
            for j in range(6):
                tok = PE.put(lambda e, j=j, b=b: e.matmul(
                    b[:, 0:HD], pt[:, j, :], VD[:, j % 2, j // 2, hd * HD:(hd + 1) * HD],
                    start=(j == 0), stop=(j == 5)), free, ev, vd_done[-1], mark=(j == 5))
            pt_ring.give(k, tok)
            v = V.put(lambda e, b=b: e.tensor_scalar(OO[:, t, hd * HD:(hd + 1) * HD], b[:, 0:HD], rd, None,
                                                     ALU.mult), tok, rdone, e0)
            ob.give(n, v)
            state[i].append(v)
            odone[(hd, t)] = v

        first(0)
        for i in range(16):
            if i + 1 < 16:
                first(i + 1)
            second(i)
        pairs.free = [[sc.free[0]], [sc.free[1]], [ob.free[0], ob.free[1]]]
        ready = spread(lambda k, t: OO[:, t, k * P:(k + 1) * P], 4, XH, XL, None,
                       lambda k, t: odone[(2 * k + 1, t)], x_used[0])
        tmp_used[0] = (PE.sem, PE.count)
        x_used[0] = project(XH, XL, 4, A["a_wo_2"][0], A["norm_g_2"][0, 3], 1.0, same(ready), (1, 0, 4))
        a_used[0] = [x_used[0], (V.sem, V.count)]

    def gqa():
        QT = at("qQT", EO, [P, 8, S], F32)
        KT = at("qKT", EO + 8192, [P, 4, S], F32)
        QS = at("qQS", EO + 12288, [P, T, 1536], F32)
        KD = at("qKD", EO + 24576, [P, T, 4, P], F32)
        MK = at("qMK", EO + 28672, [P, T, S], BF16)
        RP = at("qRP", EO + 29696, [P, 2, T, 8], F32)
        TR = at("qTR", EO + 29824, [P, 4, T, 160], F32)
        OO = at("qOO", EO + 34944, [P, T, D], F32)
        PTs = [at(f"qPT{i}", EO + 43136 + 4096 * i, [P, 2, 4, P], F32) for i in range(2)]
        SK = at("qSK", EO + 51328, [P, NH], F32)
        SM = at("qSM", EO + 51392, [P, 8, 20], F32)
        PS = [at(f"qPS{i}", TO + 4096 * i, [P, 4, S], F32) for i in range(2)]
        e0 = a_used[0]
        in1 = [single(G, MK[:, :, :], A["c_gqa"], e0), single(G, RP[:, :, :, :], A["c_rope"], e0),
               single(G, SK[:, :], A["b_sink_2"][0].partition_broadcast(P), e0)]
        rs, rs_done, ready = prenorm(1, 1, 2)
        wv = A["b_wqkv_2"][0].rearrange("(k p) n -> p k n", p=P)
        blocks = [(512, lambda k0, k1, c=c: wv[:, k0:k1, c * 512:(c + 1) * 512]) for c in range(3)]
        ev = []

        def consume(b, slot, pair, tok):
            for t in range(T):
                a = C.put(lambda e, t=t: e.activation(QS[:, t, b * 512:(b + 1) * 512], pair[t], ACT.Copy,
                                                      scale=rs[:, t:t + 1]), tok, rs_done(), e0)
            ev.append(a)
            pairs.give(slot, a)

        x_used[0] = linear(XH, XL, DK, blocks, consume, ready, head=HEAD)
        v = rope(QS[:, :, 0:1280], 20, RP, TR, ev[-1], in1, e0)
        for t in range(T):
            for i in range(2):
                kd = V.put(lambda e, t=t, i=i: e.tensor_copy(
                    KD[:, t, :, i * HD:(i + 1) * HD],
                    QS[:, t, 1024:1280].rearrange("p (k n) -> p k n", n=HD)), v, e0)
        kt_done = None
        for p in range(0, 12, 2):
            slot, bk, free = tbanks.take()
            for i in range(2):
                for t in range(T):
                    src = QS[:, t, (p + i) * P:(p + i + 1) * P] if p < 8 else KD[:, t, p + i - 8, :]
                    tok = PE.put(lambda e, i=i, t=t, bk=bk, src=src: e.transpose(
                        bk[:, i * S + t * P:i * S + (t + 1) * P], src, ident[:, :]),
                        free, v if p < 8 else kd, mark=(i == 1 and t == 1))
            dst = QT[:, p:p + 2, :] if p < 8 else KT[:, p - 8:p - 6, :]
            src = bk.rearrange("p (i s) -> p i s", i=2)
            kt_done = C.put(lambda e, dst=dst, src=src: e.activation(dst, src, ACT.Copy), tok, e0)
            tbanks.give(slot, kt_done)
        sc = Ring([0, 1])
        sc.free = [pairs.free[0], pairs.free[1]]
        ob = Ring([bank(4), bank(5)])
        ob.free = [pairs.free[2], pairs.free[2]]
        pr_ring, pt_ring = Ring(PS), Ring(PTs)
        pr_ring.free = [[tmp_used[0]], [tmp_used[0]]]
        pt_ring.free = [[e0], [e0]]
        steps = [(kv, t) for kv in range(4) for t in range(T)]
        state, odone = {}, {}

        def first(i):
            kv, t = steps[i]
            n, s_, free = sc.take()
            for j in range(4):
                hd = 4 * kv + j
                hs = slice((hd % 2) * HD, (hd % 2) * HD + HD)
                at_ = (j % 2) * 2 + j // 2
                o_ = banks_t[s_][:, at_ * S:(at_ + 1) * S]
                PE.put(lambda e, hd=hd, hs=hs, o_=o_: e.matmul(
                    o_, QT[hs, hd // 2, t * P:(t + 1) * P], KT[hs, kv, :], start=True, stop=False),
                    free, kt_done, mark=False)
                tok = PE.put(lambda e, o_=o_: e.matmul(
                    o_, identb[:, :], MK[:, t, :], start=False, stop=True), in1, mark=(j == 3))
            mx, nm, den, es, rd = (SM[:, i, 4 * c:4 * c + 4] for c in range(5))
            sk = SK[:, 4 * kv:4 * kv + 4].rearrange("p (a b) -> p b a", b=2)
            ba = lambda x: x.rearrange("p (b a) -> p b a", b=2)
            v = V.put(lambda e: e.tensor_reduce(mx, banks_t[s_][:, :].rearrange("p (j s) -> p j s", j=4),
                                                AX, ALU.max), tok, e0)
            v = V.put(lambda e: e.scalar_tensor_tensor(ba(mx), ba(mx), 0.125, sk, ALU.mult, ALU.max), v, in1)
            v0 = V.put(lambda e: e.tensor_scalar(nm, mx, -1.0, None, ALU.mult), v)
            v = V.put(lambda e: e.tensor_tensor(ba(es), sk, ba(nm), ALU.add), v0)
            m, pp, pfree = pr_ring.take()
            for j in range(4):
                a = C.put(lambda e, j=j: e.activation(
                    pp[:, j, :], banks_t[s_][:, j * S:(j + 1) * S], ACT.Exp, bias=nm[:, j:j + 1], scale=0.125,
                    accum_out=den[:, j:j + 1]), v0, pfree)
            sc.give(n, a)
            a2 = C.put(lambda e: e.activation(es, es, ACT.Exp), v)
            v = V.put(lambda e: e.tensor_tensor(den, den, es, ALU.add), a2, a)
            v = V.put(lambda e: e.reciprocal(rd, den), v)
            state[i] = [m, pp, a, rd, v]

        def second(i):
            kv, t = steps[i]
            m, pp, a, rd, rdone = state[i]
            k, pt, tfree = pt_ring.take()
            ev = []
            for kt in range(2):
                slot, bk, free = tbanks.take()
                for j in range(4):
                    tok = PE.put(lambda e, j=j, bk=bk: e.transpose(
                        bk[:, j * P:(j + 1) * P], pp[:, j, kt * P:(kt + 1) * P], ident[:, :]),
                        free, a, mark=(j == 3))
                src = bk.rearrange("p (j n) -> p j n", n=P)
                if kt == 0:
                    w = V.put(lambda e, src=src: e.tensor_copy(pt[:, 0, :, :], src), tok, tfree)
                else:
                    w = C.put(lambda e, src=src: e.activation(pt[:, 1, :, :], src, ACT.Copy), tok, tfree)
                tbanks.give(slot, w)
                ev.append(w)
            pr_ring.give(m, tok)
            n, b, free = ob.take()
            for j in range(4):
                for kt in range(2):
                    tok = PE.put(lambda e, j=j, kt=kt, b=b: e.matmul(
                        b[:, j * HD:(j + 1) * HD], pt[:, kt, (j % 2) * 2 + j // 2, :],
                        QS[:, kt, 1280 + kv * HD:1280 + (kv + 1) * HD], start=(kt == 0), stop=(kt == 1)),
                        free, ev, mark=(j == 3 and kt == 1))
            pt_ring.give(k, tok)
            v = V.put(lambda e, b=b: e.tensor_tensor(
                OO[:, t, kv * 256:(kv + 1) * 256].rearrange("p (a b n) -> p a b n", n=HD, b=2),
                b[:, 0:256].rearrange("p (a b n) -> p a b n", n=HD, b=2),
                rd.rearrange("p (b a) -> p a b", b=2).unsqueeze(3).broadcast_to([P, 2, 2, HD]), ALU.mult), tok, rdone, e0)
            ob.give(n, v)
            odone[(kv, t)] = v

        first(0)
        for i in range(8):
            if i + 1 < 8:
                first(i + 1)
            second(i)
        pairs.free = [[sc.free[0]], [sc.free[1]], [ob.free[0], ob.free[1]]]
        ready = spread(lambda k, t: OO[:, t, k * P:(k + 1) * P], DK, XH, XL, None,
                       lambda k, t: odone[(k // 2, t)], x_used[0])
        tmp_used[0] = (PE.sem, PE.count)
        x_used[0] = project(XH, XL, DK, A["b_wo_2"][0], A["norm_g_2"][1, 3], 1.0, same(ready), (1, 1, 4))
        a_used[0] = [x_used[0], (V.sem, V.count)]

    todo = []
    for block, names, mixers in (
            (0, ("ffn_w13", "ffn_w2", "norm_g", "p", "ple_w_gate", "ple_w_proj"), (gmlp, rwkv)),
            (1, ("ffn_wi_2", "ffn_wo_2", "norm_g_2", "p_2", "ple_gate_2", "ple_proj_2"), (dilated, gqa))):
        w13, w2, ng, p, wg, wp = (A[n] for n in names)
        for layer in range(2):
            mixer = None if mixers[layer] is rwkv else (block, layer, 2)
            after = [(0, 1, 0), (1, 0, 0), (1, 1, 0), None][2 * block + layer]
            todo.append(lambda f=(w13[layer, 0], w2[layer, 0], ng), b=block, l=layer, n=mixer:
                        ffn(b, l, 0, *f, n))
            todo.append(mixers[layer])

            def last_ffn(b=block, l=layer, f=(w13[layer, 1], w2[layer, 1], ng), p=p):
                defer(40, ple_input(l, p))
                ffn(b, l, 1, *f, (b, l, 6))

            todo.append(last_ffn)
            todo.append(lambda b=block, l=layer, f=(p, wg, wp, ng), n=after: ple(b, l, *f, n))
    which = range(stages) if isinstance(stages, int) else stages
    if which[0] != 0:
        while deferred:
            hurry()
    for n in which:
        if n < len(todo):
            todo[n]()

    s_out = sem("d_out")
    for t in range(T):
        SP.wait(h_done[t])
        SP.ops.append(lambda e, t=t: e.dma_start(out[0, t * P:(t + 1) * P, :], H[:, t, :]).then_inc(s_out, 16))
    SP.ops.append(lambda e: e.wait_ge(s_out, 16 * T))
    return {"sp": SP, "pe": PE, "v": V, "a": C, "g": G}


_INS = ["x", "p", "norm_g", "ffn_w13", "ffn_w2", "ple_w_gate", "ple_w_proj", "a_w_in", "a_b_in", "a_v_gain",
        "a_w_s", "a_b_s", "a_w_out", "b_mu", "b_w_in", "b_w0", "b_w1", "b_w2", "b_a0", "b_a1", "b_a2", "b_g1",
        "b_g2", "b_k_k", "b_k_a", "b_r_k", "b_lnx", "b_w_out", "p_2", "norm_g_2", "ffn_wi_2", "ffn_wo_2",
        "ple_proj_2", "ple_gate_2", "a_wqkv_2", "a_wo_2", "b_wqkv_2", "b_wo_2", "b_sink_2"]


def kernel(**inputs):
    import numpy as _np
    import concourse.bacc as _bacc
    from concourse import mybir as _mybir
    from concourse.bass_utils import run_bass_kernel_spmd as _run

    nc = _bacc.Bacc("TRN2", target_bir_lowering=False, num_devices=1)
    given = {name: _np.ascontiguousarray(inputs[name]) for name in _INS}
    given.update(constants())
    arrays, args = {}, {}
    for name, a in given.items():
        arrays[f"in_{name}_dram"] = a
        args[name] = nc.dram_tensor(f"in_{name}_dram", a.shape, _mybir.dt.from_np(a.dtype),
                                    kind="ExternalInput").ap()
    out = nc.dram_tensor("out_0_dram", (1, S, D), F32, kind="ExternalOutput").ap()
    program(nc, args, out)
    r = _run(nc, [arrays], core_ids=[0])
    return r.results[0]["out_0_dram"]
```

```python
from contextlib import ExitStack

import numpy as np

import concourse.bass as bass
from concourse import mybir

F32 = mybir.dt.float32
F32R = mybir.dt.float32r
BF16 = mybir.dt.bfloat16
ALU = mybir.AluOpType
ACT = mybir.ActivationFunctionType
AX = mybir.AxisListType.X

P = 128
T = 2
S = T * P
D = 1024
DK = D // P
FF = 2816
FB = 256
PD = 256
RMS_EPS = 1e-6
LN_EPS = 1e-5
GN_EPS = 64e-5
NH = 16
HD = 64
EXP_HALF = 0.6065306597126334

BASE = 16512
CHUNK = 2048
PART = 1024
N_RAW = 3
N_W = 7
HEAD, TAIL = 6, 4
PREP = 15
LATER = 12
ROPE = 2
TURN0, TURN1, NORMS = 6, 7, 18


class Written:

    def matmul(self, *a, **k):
        return lambda e: e.matmul(*a, **k)

    def transpose(self, *a, **k):
        return lambda e: e.transpose(*a, **k)

    def activation(self, *a, **k):
        return lambda e: e.activation(*a, **k)

    def tensor_tensor(self, *a, **k):
        return lambda e: e.tensor_tensor(*a, **k)

    def tensor_scalar(self, *a, **k):
        return lambda e: e.tensor_scalar(*a, **k)

    def scalar_tensor_tensor(self, *a, **k):
        return lambda e: e.scalar_tensor_tensor(*a, **k)

    def tensor_reduce(self, *a, **k):
        return lambda e: e.tensor_reduce(*a, **k)

    def tensor_copy(self, *a, **k):
        return lambda e: e.tensor_copy(*a, **k)

    def reciprocal(self, *a, **k):
        return lambda e: e.reciprocal(*a, **k)

    def memset(self, *a, **k):
        return lambda e: e.memset(*a, **k)


class Queue:

    def __init__(self, sem):
        self.sem, self.count, self.ops, self.passed = sem, 0, [], {}

    def wait(self, *marks):
        for m in marks:
            if m is None:
                continue
            if isinstance(m, list):
                self.wait(*m)
                continue
            sem, value = m
            if self.passed.get(id(sem), 0) < value:
                self.passed[id(sem)] = value
                self.ops.append(lambda e, sem=sem, value=value: e.wait_ge(sem, value))

    def put(self, fn, *marks, mark=True):
        self.wait(*marks)
        fn = fn(Written())
        if not mark:
            self.ops.append(fn)
            return None
        self.count += 1
        self.ops.append(lambda e, sem=self.sem: fn(e).then_inc(sem, 1))
        return (self.sem, self.count)

    def run(self, e):
        for op in self.ops:
            op(e)


class Loads:

    def __init__(self, sem):
        self.sem, self.count = sem, 0

    def put(self, queue, out, in_, *marks):
        queue.wait(*marks)
        self.count += 16
        queue.ops.append(lambda e, sem=self.sem: e.dma_start(out, in_).then_inc(sem, 16))
        return (self.sem, self.count)


class Ring:

    def __init__(self, places):
        self.places, self.free, self.at, self.out = places, [[] for _ in places], 0, set()

    def take(self):
        assert len(self.out) < len(self.places)
        while self.at % len(self.places) in self.out:
            self.at += 1
        n = self.at % len(self.places)
        self.at += 1
        self.out.add(n)
        return n, self.places[n], self.free[n]

    def give(self, n, *marks):
        self.free[n] = list(marks)
        self.out.discard(n)


def constants():
    i = np.arange(S)
    rel = i[None, :] - i[:, None]
    far = np.float32(-1e30)
    dil = np.stack([np.where(np.abs(rel) <= 64, 0, far), np.where(rel % 4 == 0, 0, far),
                    np.where(rel % 16 == 0, 0, far)], axis=1)
    dil = dil.reshape(T, P, 3 * S).transpose(1, 0, 2)
    gqa = np.where(np.abs(rel) <= 128, 0, far).reshape(T, P, S).transpose(1, 0, 2)
    inv = np.float32(500000.0) ** (-np.arange(0, 16, 2, dtype=np.float32) / np.float32(16))
    ang = np.arange(S, dtype=np.float32)[:, None] * inv[None, :].astype(np.float32)
    rope = np.stack([np.cos(ang), np.sin(ang)], axis=1).astype(np.float32)
    rope = rope.reshape(T, P, 2, 8).transpose(1, 2, 0, 3)
    a = np.arange(P)
    low = a[None, :] < a[:, None]
    up = a[:, None] < a[None, :]
    upi = a[:, None] <= a[None, :]
    masks = [low, up, upi]
    for k in range(7):
        b = 1 << k
        blk = a // b
        m = (blk[:, None] % 2 == 0) & (blk[None, :] == blk[:, None] + 1)
        masks.append(m)
    masks = np.stack(masks, axis=1).astype(np.float32)
    mid = (a[:, None] <= 63).astype(np.float32) * np.ones((1, P), np.float32)
    cum = np.stack([upi - mid, up - mid], axis=1).astype(np.float32)
    ends = np.stack([a >= 64, a <= 63], axis=1).astype(np.float32)
    bf = mybir.dt.np(BF16)
    return {
        "c_ident": np.eye(P, dtype=np.float32),
        "c_identb": np.eye(P, dtype=np.float32).astype(bf),
        "c_dil": dil.astype(bf), "c_gqa": gqa.astype(bf), "c_rope": np.ascontiguousarray(rope),
        "c_masks": masks.astype(bf), "c_cum": np.concatenate([cum.reshape(P, 2 * P), ends], axis=1),
    }


def program(nc, A, out, stages=99):
    ctx = ExitStack()
    plan = []
    with ctx:
        cache = {}

        def named_sem(name):
            if name not in cache:
                cache[name] = ctx.enter_context(nc.semaphore(name))
            return cache[name]

        tensors = {}

        def at(name, offset, shape, dt):
            if name not in tensors:
                tensors[name] = nc.alloc_sbuf_tensor_at(name, shape, dt, offset=BASE + offset)
            return tensors[name]

        banks_t = [ctx.enter_context(nc.psum_tensor(f"bank{i}", [P, 1024], F32)) for i in range(4)]
        queues = emit(nc, A, out, at, banks_t, named_sem, None, plan, stages)
        queues = emit(nc, A, out, at, banks_t, named_sem, list(plan), [], stages)
        block = ctx.enter_context(nc.Block())
        for name, q in queues.items():
            on = {"sp": block.sync, "pe": block.tensor, "v": block.vector,
                  "a": block.scalar, "g": block.gpsimd}[name]
            on(q.run)


def emit(nc, A, out, at, banks_t, sem, plan, listed, stages):
    PE, V, C, G, SP = (Queue(sem(n)) for n in ("s_pe", "s_v", "s_a", "s_g", "s_sp"))

    raw = [at(f"raw{i}", i * 8192, [P, CHUNK], F32) for i in range(N_RAW)]
    o = N_RAW * 8192
    wh = [at(f"wh{i}", o + i * 4096, [P, PART], F32R) for i in range(N_W)]
    o += N_W * 4096
    wl = [at(f"wl{i}", o + i * 4096, [P, PART], F32R) for i in range(N_W)]
    o += N_W * 4096
    XO = o
    XH = at("XH", o, [P, DK, S], F32R)
    XL = at("XL", o + 8192, [P, DK, S], F32R)
    o += 16384
    H = at("H", o, [P, T, D], F32)
    o += 8192
    TO = o
    TMP = at("TMP", o, [P, T, 2, D], F32)
    o += 16384
    BO = o
    bct = [at(f"bc{i}", o + i * 4096, [P, D], F32) for i in range(3)]
    o += 12288
    AO = o
    att = [at(f"att{i}", o + i * 2048, [P, 512], F32) for i in range(3)]
    o += 6144
    JO = o
    JUNK = at("JUNK", o, [P, 1024], BF16)
    o += 2048
    ST = at("ST", o, [P, 512], F32)
    o += 2048
    ident = at("ident", o, [P, P], F32)
    identb = at("identb", o + 512, [P, P], BF16)
    o += 768
    GT = at("GT", o, [P, 2, P], F32)
    o += 1024
    MT = at("MT", o, [P, 64], F32)
    o += 256
    PO = o
    PT = at("PT", o, [P, T, PD], F32)
    PH = at("PH", o + 2048, [P, PD // P, S], F32R)
    PL = at("PL", o + 4096, [P, PD // P, S], F32R)
    o += 6144
    NEG = at("NEG", o, [P, 32], F32)
    o += 128
    EO = o
    AH = at("AH", EO, [P, FF // P, S], F32R)
    AL = at("AL", EO + FF // P * S * 4, [P, FF // P, S], F32R)

    def bank(i):
        return banks_t[i // 2][:, (i % 2) * 512:(i % 2) * 512 + 512]

    pairs = Ring([(bank(0), bank(1)), (bank(2), bank(3)), (bank(4), bank(5))])
    tbanks = Ring([bank(6), bank(7)])
    bc = Ring(bct)
    atts = Ring(att)
    bc_loads = [Loads(sem(f"d_bc{i}")) for i in range(3)]
    raw_loads = [Loads(sem(f"d_raw{i}")) for i in range(N_RAW)]
    once = Loads(sem("d_once"))
    pload = Loads(sem("d_p"))
    stat = [0]
    singles = [0]

    def single(queue, out_, in_, *marks):
        singles[0] += 1
        return Loads(sem(f"d_s{singles[0]}")).put(queue, out_, in_, *marks)


    def cols(n):
        c = stat[0]
        stat[0] += n
        assert stat[0] <= 512
        return ST[:, c:c + n]

    pending, deferred = [], []

    def flush():
        while pending:
            pending.pop(0)[0]()

    def defer(steps, fn, first=False):
        deferred.append([steps, fn, first])

    def defer_block(fn):
        item = [fn]

        def run():
            if item in pending:
                pending.remove(item)
                fn()

        pending.append(item)
        defer(LATER, run)

    def hurry():
        d = min(deferred, key=lambda d: d[0])
        deferred.remove(d)
        d[1]()

    def tick():
        for d in deferred:
            d[0] -= 1
        while deferred and min(d[0] for d in deferred) <= 0:
            hurry()

    n_used, n_ready, n_loads = [0], [0], [0]
    done, conv, landed, freed = {}, {}, {}, {}

    def load(c):
        src, shape = chunks[c]
        place = raw[c % N_RAW]
        dst = place[:, 0:shape[0] * shape[1]].rearrange("p (k n) -> p k n", k=shape[0])
        if len(src.shape) == 4:
            dst = dst.rearrange("p k (s n) -> p k s n", s=2)
            raw_loads[c % N_RAW].put(SP, dst[:, :, 0, :], src[:, :, 0, :], freed.get(c - N_RAW))
            dst, src = dst[:, :, 1, :], src[:, :, 1, :]
        landed[c] = raw_loads[c % N_RAW].put(SP, dst, src, freed.get(c - N_RAW))

    chunks, parts_left, parts_over = {}, {}, {}
    for c, src, shape, _, _ in plan or []:
        chunks[c] = (src, shape)
        parts_left[c] = parts_left.get(c, 0) + 1
        parts_over[c] = []

    def convert(j):
        c, _, _, at_, size = plan[j]
        while c not in landed:
            hurry()
        r, hi, lo = raw[c % N_RAW][:, at_:at_ + size], wh[j % N_W], wl[j % N_W]
        a = C.put(lambda e: e.activation(hi[:, 0:size], r, ACT.Copy), landed[c], done.get(j - N_W))

        def low():
            v = V.put(lambda e: e.tensor_tensor(lo[:, 0:size], r, hi[:, 0:size].bitcast(F32),
                                                ALU.subtract), a, landed[c])
            conv[j] = [a, v]
            parts_left[c] -= 1
            parts_over[c] += [a, v]
            if not parts_left[c]:
                freed[c] = parts_over[c]
                if c + N_RAW in chunks:
                    load(c + N_RAW)

        steps = [d[0] for d in deferred if d[2]]
        if steps:
            defer(max(steps) + 2, low)
        else:
            low()

    def use(src, k0, k1, r0, r1, n):
        j = n_used[0]
        n_used[0] += 1
        if k0 == r0:
            n_loads[0] += 1
        listed.append((n_loads[0] - 1, src(r0, r1), (r1 - r0, n), (k0 - r0) * n, (k1 - k0) * n))
        if plan is None:
            conv[j] = []
        else:
            if j == 0:
                for i in range(min(N_RAW, len(chunks))):
                    load(i)
                while any(d[2] for d in deferred):
                    hurry()
            while n_ready[0] < min(j + 1 if j else N_W, len(plan)):
                n_ready[0] += 1
                convert(n_ready[0] - 1)
            while j not in conv:
                hurry()
        hi = wh[j % N_W][:, 0:(k1 - k0) * n].rearrange("p (k n) -> p k n", n=n)
        lo = wl[j % N_W][:, 0:(k1 - k0) * n].rearrange("p (k n) -> p k n", n=n)
        return j, hi, lo, conv[j]

    def used(j, tok):
        done[j] = tok
        if plan is not None and n_ready[0] == j + N_W and n_ready[0] < len(plan):
            convert(n_ready[0])
            n_ready[0] += 1

    def linear(xh, xl, nk, blocks, consume, ready, kc=4, pc=2, head=1, tail=1, early=None):
        chunks = []
        for b in range(len(blocks)):
            cuts = list(range(0, nk, kc)) + [nk]
            if tail > 1 and b == len(blocks) - 1 and nk % kc:
                cuts = [0] + list(range(nk % kc, nk + 1, kc))
            chunks += [(b, k0, min(k0 + pc, r1), r0, r1) for r0, r1 in zip(cuts, cuts[1:])
                       for k0 in range(r0, r1, pc)]
        head = min(head, len(chunks))
        tail = min(tail, len(chunks) - head)
        groups = [chunks[:head]] + [[c] for c in chunks[head:len(chunks) - tail]]
        if tail:
            groups.append(chunks[len(chunks) - tail:])
        held, toks = {}, {}
        for group in groups:
            got = []
            for b, k0, k1, r0, r1 in group:
                if b not in held:
                    held[b] = pairs.take()
                    toks[b] = [None] * T
                n, src = blocks[b]
                got.append(use(src, k0, k1, r0, r1, n))
            for t in range(T):
                for (b, k0, k1, _, _), (j, hi, lo, conv_done) in zip(group, got):
                    slot, pair, free = held[b]
                    n = blocks[b][0]
                    PE.wait(conv_done, free[t] if len(free) == T else free)
                    for k in range(k0, k1):
                        tick()
                        PE.wait(ready(k, t))
                        o_ = pair[t][:, 0:n]
                        a_, b_ = xh[:, k, t * P:(t + 1) * P], xl[:, k, t * P:(t + 1) * P]
                        h_, l_ = hi[:, k - k0, :], lo[:, k - k0, :]
                        PE.put(lambda e: e.matmul(o_, a_, h_, start=(k == 0), stop=False), mark=False)
                        PE.put(lambda e: e.matmul(o_, a_, l_, start=False, stop=False), mark=False)
                        tok = PE.put(lambda e: e.matmul(o_, b_, h_, start=False, stop=(k == nk - 1)),
                                     mark=(k == k1 - 1))
                    toks[b][t] = tok
                    if k1 == nk and early is not None:
                        early(b, t, slot, pair, tok)
                    if t == T - 1:
                        used(j, tok)
                    if t == T - 1 and k1 == nk and consume is not None:
                        later = consume(b, slot, pair, toks[b])
                        if later is not None:
                            defer_block(later)
        return tok

    def same(ready):
        return lambda k, t: ready[k]

    def spread(src, nk, xh, xl, gain, src_done, free):
        ready = []
        for k in range(0, nk, 2):
            slot, b, bfree = tbanks.take()
            n = min(2, nk - k)
            for i in range(n):
                for t in range(T):
                    tok = PE.put(lambda e, i=i, t=t, k=k, b=b: e.transpose(
                        b[:, i * S + t * P:i * S + (t + 1) * P], src(k + i, t), ident[:, :]),
                        bfree, src_done(k + i, t), mark=(i == n - 1 and t == T - 1))
            v = []
            if gain is None:
                bb = b[:, 0:n * S].rearrange("p (k s) -> p k s", k=n)
                a = C.put(lambda e, k=k, n=n, bb=bb: e.activation(xh[:, k:k + n, :], bb, ACT.Copy),
                          tok, free)
                v = V.put(lambda e, k=k, n=n, bb=bb: e.tensor_tensor(
                    xl[:, k:k + n, :], bb, xh[:, k:k + n, :].bitcast(F32), ALU.subtract), a, tok, free)
                ready += [[a, v]] * n
                tbanks.give(slot, a, v)
            else:
                for i in range(n):
                    g = gain[:, k + i:k + i + 1]
                    bb = b[:, i * S:(i + 1) * S]
                    a = C.put(lambda e, k=k + i, g=g, bb=bb: e.activation(
                        xh[:, k, :], bb, ACT.Copy, scale=g), tok, free)
                for i in range(n):
                    g = gain[:, k + i:k + i + 1]
                    bb = b[:, i * S:(i + 1) * S]
                    v = V.put(lambda e, k=k + i, g=g, bb=bb: e.scalar_tensor_tensor(
                        xl[:, k, :], bb, g, xh[:, k, :].bitcast(F32), ALU.mult, ALU.subtract), a, tok, free)
                    ready.append([a, v])
                tbanks.give(slot, a, v)
        return ready

    def turn_tiles(src, xh, xl, src_done, free):
        got = {}

        def turn(t, q):
            slot, b, bfree = tbanks.take()
            for i in range(4):
                tok = PE.put(lambda e: e.transpose(b[:, i * P:(i + 1) * P], src(4 * q + i, t), ident[:, :]),
                             bfree, src_done(4 * q + i, t), mark=(i == 3))
            b4 = b.rearrange("p (k s) -> p k s", k=4)
            hi = xh[:, 4 * q:4 * q + 4, t * P:(t + 1) * P]
            lo = xl[:, 4 * q:4 * q + 4, t * P:(t + 1) * P]
            a = C.put(lambda e: e.activation(hi, b4, ACT.Copy), tok, free)
            v = V.put(lambda e: e.tensor_tensor(lo, b4, hi.bitcast(F32), ALU.subtract), a, tok, free)
            tbanks.give(slot, a, v)
            for i in range(4):
                got[(4 * q + i, t)] = [a, v]

        def ready(k, t):
            while (k, t) not in got:
                hurry()
            return got[(k, t)]

        return turn, ready

    def rsqrt(x, scale, eps, *marks):
        n = x.shape[-1]
        m = G.put(lambda e: e.tensor_scalar(x, x, scale, eps, ALU.mult, ALU.add), *marks)
        return G.put(lambda e: e.tensor_tensor(x, x, NEG[:, 0:n], ALU.pow), m, neg_done)

    def broadcast(src, n=D):
        slot, b, free = bc.take()
        tok = bc_loads[slot].put(G, b[:, 0:n], src.partition_broadcast(P), free)
        return slot, b, tok

    gs = TMP[:, 0, :, :]
    g_in = Loads(sem("d_g")).put(SP, gs[:, 0, 0:P], A["norm_g"].rearrange("l n (k p) -> (l n k) p", p=P))
    hload = [Loads(sem(f"d_h{t}")) for t in range(T)]
    h_done = [hload[t].put(SP, H[:, t, :], A["x"][0, t * P:(t + 1) * P, :]) for t in range(T)]
    i_done = Loads(sem("d_i")).put(C, ident[:, :], A["c_ident"])
    neg_done = V.put(lambda e: e.memset(NEG[:, :], -0.5))
    G.wait(neg_done)
    once.put(G, gs[:, 0, P:2 * P], A["norm_g_2"].rearrange("l n (k p) -> (l n k) p", p=P))
    once.put(G, gs[0:48, 0, 2 * P:3 * P], A["b_mu"].rearrange("l n (k p) -> (l n k) p", p=P))
    once.put(G, identb[:, :], A["c_identb"])
    late_in = once.put(G, gs[48:56, 0, 2 * P:3 * P], A["a_b_s"].rearrange("l g p -> (l g) p"))
    slot, b, free = tbanks.take()
    tok = PE.put(lambda e: e.transpose(b[:, 0:P], gs[:, 0, 0:P], ident[:, :]), g_in, i_done)
    gt_done = C.put(lambda e: e.activation(GT[:, 0, :], b[:, 0:P], ACT.Copy), tok)
    tbanks.give(slot, gt_done)
    V.wait(gt_done)
    PE.wait(i_done)
    C.wait(i_done)

    def late_constants():
        slot, b, free = tbanks.take()
        PE.put(lambda e: e.transpose(b[:, 0:P], gs[:, 0, P:2 * P], ident[:, :]), late_in, free, mark=False)
        tok = PE.put(lambda e: e.transpose(b[:, P:P + 56], gs[0:56, 0, 2 * P:3 * P], ident[0:56, 0:56]))
        C.put(lambda e: e.activation(GT[:, 1, :], b[:, 0:P], ACT.Copy), tok)
        a = C.put(lambda e: e.activation(MT[:, 0:56], b[:, P:P + 56], ACT.Copy), tok)
        tbanks.give(slot, a)
        V.wait(a)
        tmp_used[0] = tok

    defer(30, late_constants)

    x_used = [None]
    a_used = [None]
    tmp_used = [None]
    p_used, p_got = [None], [None]

    def gain_cols(block, layer, n):
        c = (layer * 8 + n) * DK
        return GT[:, block, c:c + DK]

    def prenorm(block, layer, n):
        if carry[0] is None:
            cr = carry_on((block, layer, n))
            for t in range(T):
                carry_tile(cr, t, [h_done[t], h_done[t]], x_used[0])
            carry[0] = cr
        cr, carry[0] = carry[0], None
        assert cr["next"] == (block, layer, n)
        return cr["rs"], cr["rs_done"], cr["ready"]

    carry = [None]

    def carry_on(nxt):
        got = {}

        def ready(k, t):
            while (k, t) not in got:
                hurry()
            return got[(k, t)]

        done_ = [None] * T

        def rs_done():
            while None in done_:
                hurry()
            return done_

        return {"next": nxt, "rs": cols(T), "done": done_, "rs_done": rs_done, "ready": ready, "got": got}

    def carry_tile(cr, t, halves, free):
        ss = cols(2)
        block, layer, n = cr["next"]
        x = cr["rs"][:, t:t + 1]

        def norms():
            m = [C.put(lambda e: e.activation(JUNK[:, 0:512], H[:, t, b * 512:(b + 1) * 512], ACT.Square,
                                              accum_out=ss[:, b:b + 1]), halves[b], (C.sem, C.count))
                 for b in range(2)]
            m = G.put(lambda e: e.tensor_tensor(x, ss[:, 0:1], ss[:, 1:2], ALU.add), m)
            cr["done"][t] = rsqrt(x, 1.0 / D, RMS_EPS, m)

        def turn(b):
            slot, bk, bfree = tbanks.take()
            for i in range(4):
                tok = PE.put(lambda e: e.transpose(
                    bk[:, i * P:(i + 1) * P], H[:, t, (4 * b + i) * P:(4 * b + i + 1) * P], ident[:, :]),
                    bfree, halves[b], mark=(i == 3))
            c = (layer * 8 + n) * DK + 4 * b
            g = GT[:, block, c:c + 4].unsqueeze(2).broadcast_to([P, 4, P])
            s_, tmp, tfree = atts.take()
            t4 = tmp.rearrange("p (k s) -> p k s", k=4)
            v = V.put(lambda e: e.tensor_tensor(t4, bk.rearrange("p (k s) -> p k s", k=4), g, ALU.mult),
                      tok, tfree)
            tbanks.give(slot, v)
            hi, lo = XH[:, 4 * b:4 * b + 4, t * P:(t + 1) * P], XL[:, 4 * b:4 * b + 4, t * P:(t + 1) * P]
            a = C.put(lambda e: e.activation(hi, t4, ACT.Copy), v, free)

            def low():
                w = V.put(lambda e: e.tensor_tensor(lo, t4, hi.bitcast(F32), ALU.subtract), a, free)
                atts.give(s_, w)
                for i in range(4):
                    cr["got"][(4 * b + i, t)] = [a, w]

            defer(1, low, True)

        defer(TURN0, lambda: turn(0), True)
        defer(TURN1, lambda: turn(1), True)
        defer(NORMS, norms)

    def squares(y, ss, *marks):
        return C.put(lambda e: e.activation(JUNK[:, 0:y.shape[-1]], y, ACT.Square, accum_out=ss),
                     *marks, (C.sem, C.count))

    def residual(gb, factor, pre, cr):
        slot_b, gbt, gb_done = gb
        ss, sm = cols(2 * T), cols(T)
        f2 = (pre * factor) ** 2
        half = {}

        def weigh(t, b, y, *marks):
            part, tmp = gbt[:, b * 512:(b + 1) * 512], TMP[:, t, b, 512:1024]
            return V.put(lambda e: e.tensor_tensor(tmp, y, part, ALU.mult), *marks, gb_done, tmp_used[0])

        def first(t, y, tok, sq):
            half[t] = [G.put(lambda e: e.tensor_scalar(sm[:, t:t + 1], ss[:, t:t + 1], pre * pre / D / f2,
                                                       RMS_EPS / f2, ALU.mult, ALU.add), sq),
                       weigh(t, 0, y, tok, sq)]

        def second(t, y, free, tok, sq):
            x = sm[:, t:t + 1]
            v0 = weigh(t, 1, y, tok, sq)
            m = V.put(lambda e: e.scalar_tensor_tensor(x, ss[:, T + t:T + t + 1], pre * pre / D / f2, x,
                                                       ALU.mult, ALU.add), half[t], sq)
            m = G.put(lambda e: e.tensor_tensor(x, x, NEG[:, 0:1], ALU.pow), m)
            halves = []
            for b in range(2):
                part = H[:, t, b * 512:(b + 1) * 512]
                tmp = TMP[:, t, b, 512:1024]
                v = V.put(lambda e: e.scalar_tensor_tensor(part, tmp, x, part, ALU.mult, ALU.add),
                          m, v0, h_done[t])
                halves.append(v)
            h_done[t] = v
            if cr is not None:
                carry_tile(cr, t, halves, free)
            if t == T - 1:
                bc.give(slot_b, v)
                tmp_used[0] = v
                carry[0] = cr
            return v0

        return ss, first, second

    def project(xh, xl, nk, w, gain, factor, ready, nxt, head=1, tail=TAIL):
        cr = carry_on(nxt) if nxt else None
        ss, first, second = residual(broadcast(gain), factor, 1.0, cr)
        slots = {}
        over = [None] * T

        def early(b, t, slot, pair, tok):
            slots[b] = slot
            sq = squares(pair[t], ss[:, b * T + t:b * T + t + 1], tok)
            if b == 0:
                first(t, pair[t], tok, sq)
            else:
                over[t] = second(t, pair[t], tok, tok, sq)
                if t == T - 1:
                    for s_ in slots.values():
                        pairs.give(s_, *over)

        wv = w.rearrange("(k p) n -> p k n", p=P)
        blocks = [(512, lambda k0, k1, b=b: wv[:, k0:k1, b * 512:(b + 1) * 512]) for b in range(2)]
        last = linear(xh, xl, nk, blocks, None, ready, head=head, tail=tail, early=early)
        flush()
        return last

    def ffn(block, layer, i, w13, w2, norm_g, nxt):
        rs, rs_done, ready = prenorm(block, layer, 4 * i)
        sc = cols(2 * T)
        sc_done = []
        wv = w13.rearrange("(k p) (s n) -> p k s n", p=P, s=2)
        blocks = [(512, lambda k0, k1, b=b: wv[:, k0:k1, :, b * FB:(b + 1) * FB])
                  for b in range(FF // FB)]
        aready = {}

        def consume(b, slot, pair, toks):
            if not sc_done:
                m = G.put(lambda e: e.tensor_scalar(sc[:, 0:T], rs, 0.5, None, ALU.mult), rs_done())
                sc_done.append(G.put(lambda e: e.tensor_tensor(sc[:, T:2 * T], sc[:, 0:T], rs, ALU.mult), m))
            n, th, free = atts.take()
            over = []
            for t in range(T):
                tt = th[:, t * FB:(t + 1) * FB]
                g_, u_ = pair[t][:, 0:FB], pair[t][:, FB:2 * FB]
                a = C.put(lambda e: e.activation(tt, g_, ACT.Tanh, scale=sc[:, t:t + 1]),
                          toks[t], sc_done, free)
                v = V.put(lambda e: e.scalar_tensor_tensor(tt, tt, 1.0, g_, ALU.add, ALU.mult), a)
                v = V.put(lambda e: e.scalar_tensor_tensor(
                    tt, tt, sc[:, T + t:T + t + 1], u_, ALU.mult, ALU.mult), v, sc_done)
                over.append(v)
            pairs.give(slot, *over)

            def later():
                r = spread(lambda k, t: th[:, t * FB + k * P:t * FB + (k + 1) * P], 2,
                           AH[:, 2 * b:2 * b + 2, :], AL[:, 2 * b:2 * b + 2, :], None,
                           lambda k, t: over[t], a_used[0])
                atts.give(n, (PE.sem, PE.count))
                aready[2 * b], aready[2 * b + 1] = r

            return later

        x_used[0] = linear(XH, XL, DK, blocks, consume, ready, head=HEAD)
        a_used[0] = project(AH, AL, FF // P, w2, norm_g[layer, 4 * i + 1], 0.5, same(aready), nxt)


    def ple_input(layer, p):
        p_in = pload.put(G, PT[:, :, :], p[layer, 0].rearrange("(t p) n -> p t n", p=P), p_used[0])

        def turn():
            p_got[0] = spread(lambda k, t: PT[:, t, k * P:(k + 1) * P], PD // P, PH, PL, None,
                              lambda k, t: [p_in, i_done], p_used[0])

        return turn

    def ple(block, layer, p, w_gate, w_proj, norm_g, nxt):
        if p_got[0] is None:
            ple_input(layer, p)()
        cr = carry_on(nxt) if nxt else None
        rs, rs_done, ready = prenorm(block, layer, 6)
        ss, first, second = residual(broadcast(norm_g[layer, 7]), 1.0, 0.5, cr)
        hr = cols(T)
        hr_done = []
        y = [[TMP[:, t, b, 0:512] for t in range(T)] for b in range(2)]
        wg = w_gate[layer].rearrange("(k p) n -> p k n", p=P)
        wp = w_proj[layer].rearrange("(k p) n -> p k n", p=P)
        em = {}

        def gate(b, t, slot, pair, tok):
            if not hr_done:
                hr_done.append(G.put(lambda e: e.tensor_scalar(hr, rs, 0.5, None, ALU.mult), rs_done()))
            n, th, free = atts.take()
            a = C.put(lambda e: e.activation(th[:, :], pair[t], ACT.Tanh, scale=hr[:, t:t + 1]),
                      tok, hr_done, free)
            over[t] = a
            v = V.put(lambda e: e.scalar_tensor_tensor(y[b][t], th[:, :], 1.0, y[b][t], ALU.add, ALU.mult),
                      a, em[(b, t)])
            atts.give(n, v)
            sq = squares(y[b][t], ss[:, b * T + t:b * T + t + 1], v)
            if t == T - 1:
                pairs.give(slot, *over)
            if b == 0:
                first(t, y[0][t], v, sq)
            else:
                second(t, y[1][t], tok, v, sq)

        over = [None] * T
        cut = lambda w: [(512, lambda k0, k1, b=b: w[:, k0:k1, b * 512:(b + 1) * 512]) for b in range(2)]
        def embed(b, t, slot, pair, tok):
            em[(b, t)] = C.put(lambda e: e.activation(y[b][t], pair[t], ACT.Copy), tok, tmp_used[0])
            if t == T - 1:
                pairs.give(slot, em[(b, 0)], em[(b, 1)])

        p_used[0] = linear(PH, PL, PD // P, cut(wp), None, same(p_got[0]), early=embed)
        x_used[0] = linear(XH, XL, DK, cut(wg), None, ready, head=2, tail=TAIL, early=gate)
        p_got[0] = None

    def gmlp():
        bs = MT[:, 48:56]
        U = at("gU", EO + 32768, [P, T, 2048], F32)
        W = at("gW", EO + 32768 + 16384, [P, 8, P], F32)
        yh = at("gYH", EO, [P, 16, S], F32R)
        yl = at("gYL", EO + 16384, [P, 16, S], F32R)
        e0 = a_used[0]
        w_in_done = single(G, U[:, 0, 0:1024].rearrange("p (g j) -> p g j", g=8),
                              A["a_w_s"][0].rearrange("g i j -> i g j"), a_used[0])
        rs, rs_done, ready = prenorm(0, 0, 2)
        mix = {}

        def turn_mix():
            for q in range(2):
                slot, b, free = tbanks.take()
                for i in range(4):
                    g = 4 * q + i
                    tok = PE.put(lambda e: e.transpose(
                        b[:, i * P:(i + 1) * P], U[:, 0, g * P:(g + 1) * P], ident[:, :]),
                        free, w_in_done, mark=(i == 3))
                a = C.put(lambda e: e.activation(
                    W[:, 4 * q:4 * q + 4, :], b.rearrange("p (g i) -> p g i", g=4), ACT.Copy),
                    tok, e0)
                tbanks.give(slot, a)
            mix["done"] = V.put(lambda e: e.memset(W[64:128, :, 0:64], 0.0), a)
            mix["read"] = tok

        defer(24, turn_mix)
        bsrc = A["a_b_in"][0]
        order = [4, 5, 6, 7, 0, 1, 2, 3]
        bcs = {}

        def bias(i):
            c = order[2 * i]
            bcs[i] = broadcast(bsrc[c * 512:c * 512 + 1024])

        bias(0)
        sums = cols(T * 4)
        wv = A["a_w_in"][0].rearrange("(k p) n -> p k n", p=P)
        blocks = [(512, lambda k0, k1, c=c: wv[:, k0:k1, c * 512:(c + 1) * 512]) for c in order]
        vdone, udone = [None] * T, {}
        v_norm = [None] * T

        def layer_norm():
            g0 = broadcast(A["a_v_gain"][0, 0:1024])
            mean = cols(T)
            nmean = cols(T)
            var = cols(2 * T)
            m = V.put(lambda e: e.tensor_reduce(mean, sums.rearrange("p (t b) -> p t b", t=T), AX, ALU.add),
                      vdone[0], vdone[1])
            m = V.put(lambda e: e.tensor_scalar(nmean, mean, -1.0 / 2048, None, ALU.mult), m)
            for t in range(T):
                for a_ in range(2):
                    s_ = C.put(lambda e, t=t, a_=a_: e.activation(
                        JUNK[:, :], TMP[:, t, a_, :], ACT.Square, bias=nmean[:, t:t + 1],
                        accum_out=var[:, a_ * T + t:a_ * T + t + 1]), m, (C.sem, C.count))
            r = cols(T)
            v = V.put(lambda e: e.tensor_tensor(r, var[:, 0:T], var[:, T:2 * T], ALU.add), s_)
            r_done = rsqrt(r, 1.0 / 2048, LN_EPS, v)
            for a_ in range(2):
                gg = g0 if a_ == 0 else broadcast(A["a_v_gain"][0, 1024:2048])
                for t in range(T):
                    x = TMP[:, t, a_, :]
                    v = V.put(lambda e, x=x, t=t: e.tensor_scalar(
                        x, x, nmean[:, t:t + 1], r[:, t:t + 1], ALU.add, ALU.mult), r_done, s_, m)
                    v = V.put(lambda e, x=x, gg=gg: e.tensor_tensor(x, x, gg[1][:, :], ALU.mult), v, gg[2])
                    v_norm[t] = v
                bc.give(gg[0], v)

        def consume(b, slot, pair, tok):
            c = order[b]
            i = b // 2
            bslot, bb, b_done = bcs[i]
            v = None
            for t in range(T):
                n, z, free = atts.take()
                v = V.put(lambda e, t=t, z=z: e.scalar_tensor_tensor(
                    z[:, :], pair[t], rs[:, t:t + 1], bb[:, (b % 2) * 512:(b % 2) * 512 + 512],
                    ALU.mult, ALU.add), tok, rs_done(), b_done, free)
                if c >= 4:
                    dst = TMP[:, t, (c - 4) // 2, (c % 2) * 512:(c % 2) * 512 + 512]
                    a = C.put(lambda e, z=z, dst=dst, t=t: e.activation(
                        dst, z[:, :], ACT.Gelu_apprx_tanh, accum_out=sums[:, t * 4 + c - 4:t * 4 + c - 3]),
                        v, tmp_used[0])
                    vdone[t] = a
                else:
                    dst = U[:, t, c * 512:(c + 1) * 512]
                    a = C.put(lambda e, z=z, dst=dst: e.activation(
                        dst, z[:, :], ACT.Gelu_apprx_tanh), v, mix["read"], e0)
                    udone[(t, c)] = a
                atts.give(n, a)
            pairs.give(slot, v)
            if b % 2 == 1:
                bc.give(bslot, v)
                if i < 3:
                    bias(i + 1)
            if b == 3:
                layer_norm()

        x_used[0] = linear(XH, XL, DK, blocks, consume, ready, head=HEAD)
        ydone = {}
        for g2 in range(4):
            slot, pair, free = pairs.take()
            for t in range(T):
                for i in range(2):
                    g = 2 * g2 + i
                    tok = PE.put(lambda e, t=t, g=g, i=i, pair=pair: e.matmul(
                        pair[t][:, i * 256:(i + 1) * 256], W[:, g, :],
                        TMP[:, t, g // 4, (g % 4) * 256:(g % 4) * 256 + 256], start=True, stop=True),
                        free, mix["done"], v_norm[t])
                for i in range(2):
                    g = 2 * g2 + i
                    u = U[:, t, g * 256:(g + 1) * 256]
                    v = V.put(lambda e, t=t, g=g, i=i, u=u, pair=pair: e.scalar_tensor_tensor(
                        u, pair[t][:, i * 256:(i + 1) * 256], bs[:, g:g + 1], u, ALU.add, ALU.mult),
                        tok, udone[(t, g // 2)])
                    ydone[(t, g)] = v
            pairs.give(slot, v)
        tmp_used[0] = tok
        ready = spread(lambda k, t: U[:, t, k * P:(k + 1) * P], 16, yh, yl, None,
                       lambda k, t: ydone[(t, k // 2)], a_used[0])
        a_used[0] = project(yh, yl, 16, A["a_w_out"][0], A["norm_g"][0, 3], 1.0, same(ready), (0, 0, 4))


    def rwkv():
        wide = [P, T, D]
        R = at("rR", EO, wide, F32)
        K = at("rK", EO + 8192, wide, F32)
        VV = at("rV", EO + 16384, wide, F32)
        LW = at("rLW", EO + 24576, wide, F32)
        AA = at("rAA", EO + 32768, wide, F32)
        GG = at("rGG", EO + 40960, wide, F32)
        MK = at("rMK", EO + 49152, [P, 10, P], BF16)
        CU = at("rCU", EO + 49152 + 2560, [P, 2 * P + 2], F32)
        SM = at("rSM", EO + 49152 + 2560 + 1056, [P, 256], F32)
        W2 = at("rW2", EO + 49152 + 2560 + 1056 + 1024, [P, D], F32)
        HT = at("rHT", TO, [P, DK, S], F32)
        DX = at("rDX", TO + 8192, [P, DK, S], F32)
        KK = at("rKK", TO, wide, F32)
        TB = at("rTB", TO + 8192, wide, F32)
        nr = A["norm_g"]
        e0 = a_used[0]
        mk_in = single(G, MK[:, :, :], A["c_masks"], e0)
        cu_in = single(G, CU[:, :], A["c_cum"], e0)
        ss = cols(T)
        m = [squares(H[:, t, :], ss[:, t:t + 1], h_done[t]) for t in range(T)]
        rs_done = rsqrt(ss, 1.0 / D, RMS_EPS, m[-1])
        hn = [V.put(lambda e, t=t: e.tensor_scalar(R[:, t, :], H[:, t, :], ss[:, t:t + 1], None, ALU.mult),
                    rs_done, h_done[t], e0) for t in range(T)]
        gain = gain_cols(0, 1, 2)
        hdone = []
        for k in range(0, DK, 2):
            slot, b, free = tbanks.take()
            for i in range(2):
                for t in range(T):
                    tok = PE.put(lambda e, k=k, i=i, t=t, b=b: e.transpose(
                        b[:, i * S + t * P:i * S + (t + 1) * P], R[:, t, (k + i) * P:(k + i + 1) * P],
                        ident[:, :]), free, hn[t], mark=(i == 1 and t == 1))
            for i in range(2):
                a = C.put(lambda e, k=k + i, i=i, b=b: e.activation(
                    HT[:, k, :], b[:, i * S:(i + 1) * S], ACT.Copy, scale=gain[:, k:k + 1]),
                    tok, tmp_used[0])
                hdone.append(a)
            tbanks.give(slot, a)
        ht_read = tok
        if p_got[0] is not None:
            raise AssertionError("the embedding's place is in use")
        v = V.put(lambda e: e.tensor_scalar(DX[:, :, 0:1], HT[:, :, 0:1], -1.0, None, ALU.mult),
                  hdone[-1], tmp_used[0])
        dx = V.put(lambda e: e.tensor_tensor(DX[:, :, 1:S], HT[:, :, 0:S - 1], HT[:, :, 1:S], ALU.subtract),
                   hdone[-1], v)
        LO = at("rLO", EO + 24576, [P, DK, S], F32)
        LO2 = at("rLO2", EO + 32768, [P, DK, S], F32)
        W1 = {5: at("rG1", EO + 8192, [P, DK, 160], F32), 4: at("rA1", EO + 13312, [P, DK, 64], F32),
              3: at("rD1", EO + 16384, [P, DK, 64], F32)}
        G2 = at("rG2", EO + 18432, [P, D], F32)
        w1_in = {n: single(SP, W1[n][:, :, :], A[name][0].rearrange("(k p) n -> p k n", p=P), e0)
                 for n, name in ((5, "b_g1"), (4, "b_a1"), (3, "b_w1"))}
        n3, bc3, free3 = bc.take()
        g2_in = [single(SP, G2[:, :], A["b_g2"][0][0:P, :], e0),
                 single(SP, bc3[0:32, :], A["b_g2"][0][P:160, :], free3)]
        w2_in = [single(SP, W2[0:64, :], A["b_a2"][0], e0), single(SP, W2[64:128, :], A["b_w2"][0], e0)]
        a0b = broadcast(A["b_a0"][0])
        w0b = broadcast(A["b_w0"][0])
        lora = {}

        def mix(n, dst, *marks):
            out_ = []
            for k in range(DK):
                out_.append(V.put(lambda e, k=k: e.scalar_tensor_tensor(
                    dst[:, k, :], DX[:, k, :], MT[:, n * DK + k:n * DK + k + 1], HT[:, k, :],
                    ALU.mult, ALU.add), dx, *marks))
            return out_

        lread = [e0, e0]
        TH = at("rTH", AO, [P, 4, S], F32)
        th_done = {}
        att_free = [f for f in atts.free]
        for i, (n, width) in enumerate(((5, 160), (4, 64), (3, 64))):
            lo_, w1_ = (LO, LO2)[i % 2], W1[n]
            xs = mix(n, lo_, lread[i % 2])
            slot, pair, free = pairs.take()
            for part in range((width + P - 1) // P):
                c0, c1 = part * P, min(width, part * P + P)
                for k in range(DK):
                    tok = PE.put(lambda e, k=k, c0=c0, c1=c1, part=part, pair=pair: e.matmul(
                        pair[part][0:c1 - c0, 0:S], w1_[:, k, c0:c1], lo_[:, k, :],
                        start=(k == 0), stop=(k == DK - 1)), free, w1_in[n], xs[k], mark=(k == DK - 1))
            lread[i % 2] = tok
            if n == 5:
                a = C.put(lambda e, pair=pair: e.activation(TH[:, 0, 0:S], pair[0][:, 0:S], ACT.Tanh,
                                                            scale=0.5), tok, *att_free)
                a = C.put(lambda e, pair=pair: e.activation(TH[0:32, 1, 0:S], pair[1][0:32, 0:S], ACT.Tanh,
                                                            scale=0.5), tok)
                v = V.put(lambda e: e.tensor_scalar(TH[:, 0, 0:S], TH[:, 0, 0:S], 1.0, 0.5, ALU.add,
                                                    ALU.mult), a)
                v = V.put(lambda e: e.tensor_scalar(TH[0:32, 1, 0:S], TH[0:32, 1, 0:S], 1.0, 0.5, ALU.add,
                                                    ALU.mult), a)
                th_done[n] = v
            elif n == 4:
                a = C.put(lambda e, pair=pair: e.activation(TH[0:64, 2, 0:S], pair[0][0:64, 0:S], ACT.Copy),
                          tok)
                th_done[n] = a
            else:
                a = C.put(lambda e, pair=pair: e.activation(TH[64:128, 2, 0:S], pair[0][0:64, 0:S], ACT.Tanh),
                          tok)
                th_done[n] = a
            pairs.give(slot, a)

        gdone, adone, wdone = {}, {}, {}

        def second(parts, w_ins, evac):
            for b in range(2):
                slot, pair, free = pairs.take()
                for t in range(T):
                    for i, (p0, p1, blk, w_) in enumerate(parts):
                        tok = PE.put(lambda e: e.matmul(
                            pair[t], TH[p0:p1, blk, t * P:(t + 1) * P], w_[p0:p1, b * 512:(b + 1) * 512],
                            start=(i == 0), stop=(i == len(parts) - 1)), free, w_ins, list(th_done.values()))
                evac(b, slot, pair, tok)
            return tok

        def g_evac(b, slot, pair, tok):
            for t in range(T):
                a = C.put(lambda e: e.activation(GG[:, t, b * 512:(b + 1) * 512], pair[t], ACT.Copy), tok, e0)
            pairs.give(slot, a)
            gdone[0] = a

        later = []

        def sig_evac(dst, bias, scale, done_):
            def evac(b, slot, pair, tok):
                for t in range(T):
                    d = dst[:, t, b * 512:(b + 1) * 512]
                    v = V.put(lambda e: e.tensor_tensor(
                        d, pair[t], bias[1][:, b * 512:(b + 1) * 512], ALU.add), tok, bias[2], lread)
                    a = C.put(lambda e: e.activation(d, d, ACT.Tanh, scale=0.5), v)

                    def end(d=d, a=a):
                        done_[0] = V.put(lambda e: e.tensor_scalar(d, d, 1.0, scale, ALU.add, ALU.mult), a)

                    later.append(end)
                    if len(later) > 2:
                        later.pop(0)()
                pairs.give(slot, v)
            return evac

        def mixed(n, ring):
            rdy, lows = [None] * DK, []
            for k in range(DK):
                s_, x, free = ring.take()
                v0 = V.put(lambda e: e.scalar_tensor_tensor(
                    x, DX[:, k, :], MT[:, n * DK + k:n * DK + k + 1], HT[:, k, :],
                    ALU.mult, ALU.add), dx, free)
                a = C.put(lambda e: e.activation(XH[:, k, :], x, ACT.Copy), v0, x_used[0])

                def low(k=k, x=x, s_=s_, a=a):
                    v = V.put(lambda e: e.tensor_tensor(
                        XL[:, k, :], x, XH[:, k, :].bitcast(F32), ALU.subtract), a, x_used[0])
                    ring.give(s_, v)
                    rdy[k] = [a, v]

                lows.append(low)
                if len(lows) > 1:
                    lows.pop(0)()
            lows.pop(0)()
            return rdy

        mix_ring = Ring([att[2][:, i * S:(i + 1) * S] for i in range(2)])
        mix_ring.free = [att_free[2], att_free[2]]
        first_in = mixed(0, mix_ring)
        g2read = second([(0, 128, 0, G2), (0, 32, 1, bc3)], g2_in, g_evac)
        second([(0, 64, 2, W2)], w2_in, sig_evac(AA, a0b, 0.5, adone))
        w2read = second([(64, 128, 2, W2)], w2_in, sig_evac(LW, w0b, -0.5 * EXP_HALF, wdone))
        while later:
            later.pop(0)()
        bc.give(n3, g2read)
        bc.give(a0b[0], adone[0])
        bc.give(w0b[0], wdone[0])
        for i in range(3):
            atts.free[i] = [w2read, (V.sem, V.count)]

        per_head = lambda a: a.rearrange("p (h n) -> p h n", n=HD)
        bon, scl = SM[:, 64:96], SM[:, 96:104]
        tin, tex = CU[:, 0:P], CU[:, P:2 * P]
        scan_in, early_done = {}, {}
        rk = A["b_r_k"][0].rearrange("h n -> (h n)")

        def bonus_sums(t, h, tmp, rkh, *marks):
            c, at_ = slice(h * 512, (h + 1) * 512), 64 + 16 * t + 8 * h
            v = V.put(lambda e: e.tensor_tensor(tmp, R[:, t, c], K[:, t, c], ALU.mult), *marks)
            v = V.put(lambda e: e.tensor_tensor(tmp, tmp, rkh, ALU.mult), v)
            return V.put(lambda e: e.tensor_reduce(SM[:, at_:at_ + 8], per_head(tmp), AX, ALU.add), v)

        def unit(t, m):
            inv = SM[:, 32 + 16 * t:48 + 16 * t]
            v = V.put(lambda e: e.tensor_tensor(
                per_head(KK[:, t, :]), per_head(KK[:, t, :]), inv.unsqueeze(2).broadcast_to([P, NH, HD]),
                ALU.mult), m)
            return V.put(lambda e: e.tensor_tensor(AA[:, t, :], KK[:, t, :], AA[:, t, :], ALU.mult), v)

        def decay(t, b, pair, free, es, frees, m):
            c = slice(b * 512, (b + 1) * 512)
            e1, e2, e3 = es
            tok = PE.put(lambda e: e.matmul(pair[0], tin, LW[:, t, c], start=True, stop=True),
                         free, cu_in, wdone[0])
            tok2 = PE.put(lambda e: e.matmul(pair[1], tex, LW[:, t, c], start=True, stop=True))
            a1 = C.put(lambda e: e.activation(e1, pair[0], ACT.Exp), tok, frees)
            a2 = C.put(lambda e: e.activation(e2, pair[0], ACT.Exp, scale=-1.0), tok)
            a3 = C.put(lambda e: e.activation(e3, pair[1], ACT.Exp), tok2)
            v1 = V.put(lambda e: e.tensor_tensor(R[:, t, c], R[:, t, c], e1, ALU.mult), a1, m)
            v2 = V.put(lambda e: e.tensor_tensor(K[:, t, c], K[:, t, c], e2, ALU.mult), a2)
            v3 = V.put(lambda e: e.tensor_tensor(AA[:, t, c], AA[:, t, c], e2, ALU.mult), m)
            v4 = V.put(lambda e: e.scalar_tensor_tensor(
                KK[:, t, c], KK[:, t, c], -1.0, e3, ALU.mult, ALU.mult), a3, m)
            scan_in[(t, b)] = v4
            return a3, (v1, v3, v4)

        def prepare():
            b1 = broadcast(A["b_k_k"][0])
            b2 = broadcast(A["b_k_a"][0])
            b3 = broadcast(rk)
            k_in = [rkv_done[(n, b, t)] for n in (0, 1) for b in range(2) for t in range(T)]
            sq = {}
            for t in range(T):
                v = V.put(lambda e: e.tensor_tensor(KK[:, t, :], K[:, t, :], b1[1][:, :], ALU.mult),
                          b1[2], k_in, dx, (V.sem, V.count))
                sq[t] = C.put(lambda e: e.activation(TB[:, t, :], KK[:, t, :], ACT.Square), v)
                yield
            bc.give(b1[0], v)
            for t in range(T):
                n2, inv = SM[:, 16 * t:16 + 16 * t], SM[:, 32 + 16 * t:48 + 16 * t]
                v = V.put(lambda e: e.tensor_reduce(n2, per_head(TB[:, t, :]), AX, ALU.add), sq[t])
                v = V.put(lambda e: e.tensor_scalar(n2, n2, 1e-24, None, ALU.max), v)
                early_done[t] = G.put(lambda e: e.tensor_tensor(inv, n2, NEG[:, 0:16], ALU.pow), v)
                yield
                v = V.put(lambda e: e.scalar_tensor_tensor(
                    TB[:, t, :], AA[:, t, :], -1.0, b2[1][:, :], ALU.add, ALU.mult), b2[2], adone[0], v)
                yield
                kd = V.put(lambda e: e.scalar_tensor_tensor(
                    K[:, t, :], TB[:, t, :], 1.0, K[:, t, :], ALU.add, ALU.mult), v)
                yield
                if t == 0:
                    bb = unit(0, early_done[0])
                    yield
                    for h in range(2):
                        m = bonus_sums(0, h, TB[:, 0, h * 512:(h + 1) * 512], b3[1][:, h * 512:(h + 1) * 512],
                                       b3[2], kd)
                        yield
                    for b in range(2):
                        slot, pair, free = pairs.take()
                        got = [atts.take() for _ in range(3)]
                        p_, vs_ = decay(0, b, pair, free, [g[1][:, :] for g in got], [g[2] for g in got], [m, bb])
                        pairs.give(slot, p_)
                        for g, v_ in zip(got, vs_):
                            atts.give(g[0], v_)
                        yield
            bc.give(b2[0], kd)
            bc.give(b3[0], m)
            slot, pair, free = pairs.take()
            for t in range(T):
                for p in range(8):
                    tok = PE.put(lambda e: e.matmul(
                        pair[0][:, p:p + 1], LW[:, t, p * P:(p + 1) * P], CU[:, 2 * P + t:2 * P + t + 1],
                        start=(t == 0 and p == 0), stop=(t == 1 and p == 7), skip_group_check=True), free)
            early_done["scl"] = C.put(lambda e: e.activation(scl, pair[0][:, 0:8], ACT.Exp), tok)
            pairs.give(slot, early_done["scl"])

        def complete():
            bufs = [at("rE0", PO + 4096, [P, 512], F32), at("rE1", JO, [P, 512], F32),
                    at("rE2", BO + 6144, [P, 512], F32)]
            f = [p_used[0], before]
            ins = [single(SP, bufs[h][:, :], rk[h * 512:(h + 1) * 512].partition_broadcast(P), f)
                   for h in range(2)]
            bb = unit(1, early_done[1])
            yield
            for h in range(2):
                m = bonus_sums(1, h, bufs[2][:, :], bufs[h][:, :], ins[h], bb)
                yield
            vs_ = m
            for b in range(2):
                n1, k1, f1 = allbanks.take()
                n2, k2, f2 = allbanks.take()
                p_, vs_ = decay(1, b, (k1, k2), [f1, f2], [x[:, :] for x in bufs], vs_, [m, bb])
                vs_ = list(vs_)
                allbanks.give(n1, p_)
                allbanks.give(n2, p_)
                yield

        wv = A["b_w_in"][0].rearrange("n (k p) e -> n p k e", p=P)
        rkv_done = {}
        next_in = [first_in]
        for n, dst in enumerate((R, K, VV)):
            rdy = next_in[0]

            def early(b, t, slot, pair, tok):
                if n < 2 and b == 1 and t == T - 1:
                    x_used[0] = tok
                    next_in[0] = mixed(n + 1, mix_ring)

            def consume(b, slot, pair, tok, dst=dst, n=n):
                for t in range(T):
                    a = C.put(lambda e, t=t: e.activation(dst[:, t, b * 512:(b + 1) * 512], pair[t],
                                                          ACT.Copy), tok, ht_read, e0)
                    rkv_done[(n, b, t)] = a
                pairs.give(slot, a)

            blocks = [(512, lambda k0, k1, b=b, n=n: wv[n][:, k0:k1, b * 512:(b + 1) * 512])
                      for b in range(2)]
            if n == 2:
                steps = prepare()
                for i in range(PREP):
                    defer(1 + i, lambda: next(steps, None))
            x_used[0] = linear(XH, XL, DK, blocks, consume, same(rdy), early=early)
        for _ in steps:
            pass
        rkv = rkv_done[(2, 1, 1)]

        allbanks = Ring([bank(i) for i in range(8)])
        for i in range(3):
            allbanks.free[2 * i] = list(pairs.free[i])
            allbanks.free[2 * i + 1] = list(pairs.free[i])
        for i in range(2):
            allbanks.free[6 + i] = list(tbanks.free[i])
        maps = []
        scl_done = early_done["scl"]
        before = [x_used[0], [f for f in atts.free], scl_done, scan_in[(0, 1)], bc.free[0], bc.free[1],
                  bc.free[2], p_used[0], (V.sem, V.count)]
        for s_, spots in enumerate((
                [XO, XO + 4096, XO + 8192, XO + 10240, XO + 12288, XO + 14336, AO, AO + 2048, AO + 3072],
                [TO + 8192, TO + 12288, EO + 24576, None, PO, PO + 2048, BO, BO + 2048,
                 BO + 3072])):
            TT = at(f"sTT{s_}", spots[0], [P, 4, 2, P], F32)
            KR = at(f"sKR{s_}", spots[1], [P, 4, 2, P], F32)
            MR = at(f"sMR{s_}", spots[2], [P, 2, 2, 2, P], F32)
            XX = at(f"sXX{s_}", spots[4], [P, 4, P], F32)
            YY = at(f"sYY{s_}", spots[5], [P, 4, P], F32)
            WW = at(f"sWW{s_}", spots[6], [P, 4, P], F32)
            RH = at(f"sRH{s_}", spots[7], [P, 4, HD], F32)
            SA = at(f"sSA{s_}", spots[8], [P, 4, HD], F32)
            maps.append((TT, KR, MR, XX, YY, WW, RH, SA))
        S0 = at("sS0", BO + 4096, [P, 8, HD], F32)
        set_free = [before, before]
        s0_done = {}
        s0_free = before

        def mask(i, n):
            return MK[:, i, :].unsqueeze(1).broadcast_to([P, n, P])

        def group(c, q, s_):
            TT, KR, MR, XX, YY, WW, RH, SA = maps[s_]
            f0 = set_free[s_]
            srcs = (KK, R, AA, K)
            b4 = lambda b: b.rearrange("p (u n) -> p u n", u=4)
            for half in range(2):
                n, b, free = allbanks.take()
                for i in range(2):
                    for pr in range(2):
                        x = srcs[2 * half + i][:, c, (2 * q + pr) * P:(2 * q + pr + 1) * P]
                        tok = PE.put(lambda e, i=i, pr=pr, x=x, b=b: e.transpose(
                            b[:, (2 * i + pr) * P:(2 * i + pr + 1) * P], x, ident[:, :]),
                            free, scan_in[(c, q // 2)], mark=(i == 1 and pr == 1))
                dst = TT[:, 2 * half:2 * half + 2, :, :].rearrange("p a b n -> p (a b) n")
                if half == 0:
                    tt0 = C.put(lambda e, b=b, dst=dst: e.activation(dst, b4(b), ACT.Copy), tok, f0)
                    allbanks.give(n, tt0)
                else:
                    tt1 = V.put(lambda e, b=b, dst=dst: e.tensor_copy(dst, b4(b)), tok, f0)
                    allbanks.give(n, tt1)
            begun[(c, q)] = tok
            yield
            un = [(u, 2 * q + u // 2, slice((u % 2) * HD, (u % 2) * HD + HD)) for u in range(4)]
            for h2 in range(2):
                n, b, free = allbanks.take()
                for i, (l_, r_) in enumerate(((0, 2), (2, 1))):
                    for u, pr, hs in un[h2::2]:
                        tok = PE.put(lambda e: e.matmul(
                            b[:, (2 * i + u // 2) * P:(2 * i + u // 2 + 1) * P], TT[hs, l_, u // 2, :],
                            TT[hs, r_, u // 2, :], start=True, stop=True),
                            free, tt0, tt1, mark=(i == 1 and u >= 2))
                m02 = MK[:, 0:3:2, :].unsqueeze(2).broadcast_to([P, 2, 2, P])
                ma = V.put(lambda e: e.tensor_tensor(
                    MR[:, h2, :, :, :], b.rearrange("p (i u n) -> p i u n", i=2, u=2), m02, ALU.mult),
                    tok, f0, mk_in)
                allbanks.give(n, ma)
                n, b, free = allbanks.take()
                for u, pr, hs in un[h2::2]:
                    tok = PE.put(lambda e: e.matmul(
                        b[:, (u // 2) * 256:(u // 2) * 256 + 256].rearrange("p (i n) -> p i n", i=2),
                        TT[hs, 3, u // 2, :], TT[hs, 0:2, u // 2, :], start=True, stop=True),
                        free, mark=(u >= 2))
                m12 = MK[:, 1:3, :].rearrange("p a n -> p (a n)").unsqueeze(1).broadcast_to([P, 2, 2 * P])
                kr = V.put(lambda e: e.tensor_tensor(
                    KR[:, h2:4:2, :, :].rearrange("p u a n -> p u (a n)"),
                    b.rearrange("p (u n) -> p u n", u=2), m12, ALU.mult), tok, f0)
                allbanks.give(n, kr)
            rb = ma
            yield
            x_done = y_done_ = None
            for lv in range(7):
                n, b, free = allbanks.take()
                for u in range(4):
                    m_, o_ = MR[:, u % 2, 0, u // 2, :], b[:, u * P:(u + 1) * P]
                    if lv == 0:
                        tok = PE.put(lambda e: e.transpose(o_, m_, ident[:, :]), free, ma, mark=(u == 3))
                    else:
                        tok = PE.put(lambda e: e.matmul(o_, m_, YY[:, u, :], start=True, stop=True),
                                     free, y_done_, mark=(u == 3))
                Z = YY if lv == 0 else WW
                z = V.put(lambda e: e.tensor_tensor(Z[:, :, :], b4(b), mask(3 + lv, 4), ALU.mult), tok, f0)
                allbanks.give(n, z)
                if lv == 0:
                    y_done_ = V.put(lambda e: e.tensor_tensor(
                        YY[:, :, :], YY[:, :, :], ident[:, :].unsqueeze(1).broadcast_to([P, 4, P]), ALU.add), z)
                yield
                if lv > 0:
                    n, b, free = allbanks.take()
                    for u in range(4):
                        tok = PE.put(lambda e: e.matmul(
                            b[:, u * P:(u + 1) * P], XX[:, u, :], WW[:, u, :], start=True, stop=True),
                            free, z, x_done, mark=(u == 3))
                    y_done_ = V.put(lambda e: e.tensor_tensor(YY[:, :, :], b4(b), YY[:, :, :], ALU.add), tok)
                    allbanks.give(n, y_done_)
                    yield
                if lv < 6:
                    n, b, free = allbanks.take()
                    for u in range(4):
                        tok = PE.put(lambda e: e.transpose(
                            b[:, u * P:(u + 1) * P], YY[:, u, :], ident[:, :]), free, y_done_, mark=(u == 3))
                    x_done = C.put(lambda e: e.activation(XX[:, :, :], b4(b), ACT.Copy), tok, f0)
                    allbanks.give(n, x_done)
            b64 = lambda b, k: b[:, 0:k * HD].rearrange("p (u n) -> p u n", u=k)
            vs = lambda pr, hs: VV[:, c, pr * P + hs.start:pr * P + hs.start + HD]
            for h2 in range(2):
                n, b, free = allbanks.take()
                for u, pr, hs in un[h2::2]:
                    o_ = b[:, (u // 2) * HD:(u // 2 + 1) * HD]
                    tok = PE.put(lambda e: e.matmul(
                        o_, KR[:, u, 0, :], vs(pr, hs), start=True, stop=(c == 0)), free, kr, rkv)
                    if c == 1:
                        tok = PE.put(lambda e: e.matmul(
                            o_, TT[hs, 0, u // 2, :], S0[hs, pr, :], start=False, stop=True), s0_done[q])
                a = C.put(lambda e: e.activation(RH[:, h2:4:2, :], b64(b, 2), ACT.Copy), tok, f0)
                allbanks.give(n, a)
            yield
            n, b, free = allbanks.take()
            for u in range(4):
                tok = PE.put(lambda e: e.matmul(
                    b[:, u * HD:(u + 1) * HD], YY[:, u, :], RH[:, u, :], start=True, stop=True),
                    free, a, y_done_, mark=(u == 3))
            a = C.put(lambda e: e.activation(SA[:, :, :], b64(b, 4), ACT.Copy), tok, f0)
            allbanks.give(n, a)
            yield
            for h2 in range(2):
                n, b, free = allbanks.take()
                for u, pr, hs in un[h2::2]:
                    o_ = b[:, (u // 2) * HD:(u // 2 + 1) * HD]
                    PE.put(lambda e: e.matmul(
                        o_, KR[:, u, 1, :], vs(pr, hs), start=True, stop=False), free, mark=False)
                    if c == 1:
                        PE.put(lambda e: e.matmul(
                            o_, TT[hs, 1, u // 2, :], S0[hs, pr, :], start=False, stop=False), mark=False)
                    tok = PE.put(lambda e: e.matmul(
                        o_, MR[:, u % 2, 1, u // 2, :], SA[:, u, :], start=False, stop=True), a, rb)
                yo = R[:, c, q * 256:(q + 1) * 256].rearrange("p (u h n) -> p h u n", h=2, n=HD)[:, h2, :, :]
                y = C.put(lambda e: e.activation(yo, b64(b, 2), ACT.Copy), tok)
                allbanks.give(n, y)
            if c == 0:
                n, b, free = allbanks.take()
                for u, pr, hs in un:
                    o_ = b[hs, (u // 2) * HD:(u // 2) * HD + HD]
                    ch = slice(pr * P + hs.start, pr * P + hs.start + HD)
                    PE.put(lambda e, u=u, o_=o_, ch=ch: e.matmul(
                        o_, AA[:, 0, ch], SA[:, u, :], start=True, stop=False), free, mark=False)
                    tok = PE.put(lambda e, o_=o_, ch=ch: e.matmul(
                        o_, K[:, 0, ch], VV[:, 0, ch], start=False, stop=True))
                for i in range(2):
                    s0_done[q] = V.put(lambda e, i=i, b=b: e.tensor_scalar(
                        S0[:, 2 * q + i, :], b[:, i * HD:(i + 1) * HD], scl[:, 2 * q + i:2 * q + i + 1], None,
                        ALU.mult), tok, s0_free, scl_done)
                allbanks.give(n, s0_done[q])
            set_free[s_] = [tok, y, (V.sem, V.count)]
            ended[(c, q)] = [tok, y]

        l0d = single(SP, W2[:, :], A["b_lnx"][0, 0].partition_broadcast(P), w2read)
        l1d = single(SP, bct[2][:, :], A["b_lnx"][0, 1].partition_broadcast(P), bc.free[2], w2read)
        yd, bonus_done, begun, ended = {}, {}, {}, {}
        sides = [(f, t, h, known) for t in range(T) for f, known in ((0, (ended, begun)[t]), (1, ended))
                 for h in range(2)]
        wide_ = lambda a: a.unsqueeze(2).broadcast_to([P, 8, HD])

        def bonus(t, h):
            c = slice(h * 512, (h + 1) * 512)
            bn, gg, at_ = AA[:, t, c], GG[:, t, c], 16 * t + 8 * h
            f = [(ended, begun)[t][(t, q)] for q in (2 * h, 2 * h + 1)]
            v = V.put(lambda e: e.tensor_tensor(
                per_head(bn), per_head(VV[:, t, c]), wide_(bon[:, at_:at_ + 8]), ALU.mult), f)
            yield
            v = V.put(lambda e: e.tensor_tensor(bn, bn, bct[2][:, c], ALU.add), v, l1d)
            yield
            v = V.put(lambda e: e.tensor_tensor(bn, bn, gg, ALU.mult), v, gdone[0])
            yield
            bonus_done[(t, h)] = V.put(lambda e: e.tensor_tensor(gg, gg, W2[:, c], ALU.mult), v, l0d)

        def norm(t, h):
            c = slice(h * 512, (h + 1) * 512)
            x, sq, at_ = R[:, t, c], K[:, t, c], 16 * t + 8 * h
            mean, var = SM[:, 128 + at_:136 + at_], SM[:, 160 + at_:168 + at_]
            f = [ended[(t, q)] for q in (2 * h, 2 * h + 1)]
            v = V.put(lambda e: e.tensor_reduce(mean, per_head(x), AX, ALU.add), f)
            v = V.put(lambda e: e.tensor_scalar(mean, mean, 1.0 / HD, None, ALU.mult), v)
            yield
            v0 = V.put(lambda e: e.tensor_tensor(per_head(x), per_head(x), wide_(mean), ALU.subtract), v)
            a = C.put(lambda e: e.activation(sq, x, ACT.Square), v0)
            yield
            v0 = V.put(lambda e: e.tensor_tensor(x, x, GG[:, t, c], ALU.mult), v0, a, bonus_done[(t, h)])
            yield
            v = V.put(lambda e: e.tensor_reduce(var, per_head(sq), AX, ALU.add), a)
            g = rsqrt(var, 1.0 / HD, GN_EPS, v)
            yield
            v = V.put(lambda e: e.tensor_tensor(per_head(x), per_head(x), wide_(var), ALU.mult), v0, g)
            yield
            yd[(t, h)] = V.put(lambda e: e.tensor_tensor(x, x, AA[:, t, c], ALU.add), v)

        def chain(s_):
            for c in range(2):
                for q in (s_, s_ + 2):
                    yield from group(c, q, s_)

        sets, side = [chain(0), chain(1)], [complete()]
        def step_sides():
            while True:
                if not side and sides:
                    f, t, h, known = sides[0]
                    if (t, 2 * h) in known and (t, 2 * h + 1) in known:
                        sides.pop(0)
                        side.append((bonus, norm)[f](t, h))
                if not side:
                    return False
                try:
                    next(side[0])
                    return True
                except StopIteration:
                    side.pop()

        while sets:
            for g_ in list(sets):
                try:
                    next(g_)
                except StopIteration:
                    sets.remove(g_)
            step_sides()
        for i in range(3):
            pairs.free[i] = [allbanks.free[2 * i], allbanks.free[2 * i + 1]]
        for i in range(2):
            tbanks.free[i] = allbanks.free[6 + i]
        over = [set_free[0], set_free[1]]
        for i in range(3):
            atts.free[i] = over
            bc.free[i] = over
        while (1, 0) not in yd:
            step_sides()
        turn, ready = turn_tiles(lambda k, t: R[:, t, k * P:(k + 1) * P], XH, XL,
                                 lambda k, t: yd[(t, k // 4)], over)
        for t, q in ((0, 0), (0, 1), (1, 0)):
            turn(t, q)
        while step_sides():
            pass
        defer(10, lambda: turn(1, 1))
        for i in range(3):
            bc.free[i] = [over, yd[(1, 1)]]
        tmp_used[0] = (V.sem, V.count)
        x_used[0] = project(XH, XL, DK, A["b_w_out"][0], nr[1, 3], 1.0, ready, (0, 1, 4), 4, 4)
        a_used[0] = [x_used[0], (V.sem, V.count)]

    def rope(x, nh, RP, TR, *marks):
        for t in range(T):
            before = (V.sem, V.count)
            x4 = x[:, t, :].rearrange("p (h n) -> p h n", n=HD)
            a, b = x4[:, :, 0:8], x4[:, :, 8:16]
            cs, sn = (RP[:, i, t, :].unsqueeze(1).broadcast_to([P, nh, 8]) for i in range(2))
            tr = [TR[:, i, t, 0:nh * 8].rearrange("p (h n) -> p h n", n=8) for i in range(4)]
            m = [V.put(lambda e, i=i, y=y, z=z: e.tensor_tensor(tr[i], y, z, ALU.mult), *marks,
                       before) for i, (y, z) in enumerate(((a, cs), (b, sn), (b, cs), (a, sn)))]
            V.put(lambda e: e.tensor_tensor(a, tr[0], tr[1], ALU.subtract), m[3])
            v = V.put(lambda e: e.tensor_tensor(b, tr[2], tr[3], ALU.add), m[3])
        return v

    def dilated():
        QT = at("dQT", EO, [P, 12, S], F32)
        KT = at("dKT", EO + 12288, [P, 12, S], F32)
        VD = at("dVD", EO + 24576, [P, T, 3, 512], F32)
        MK = at("dMK", EO + 36864, [P, T, 3 * S], BF16)
        RP = at("dRP", EO + 39936, [P, 2, T, 8], F32)
        TR = at("dTR", EO + 40064, [P, 4, T, 64], F32)
        PS = [at(f"dPS{i}", TO + i * 6144, [P, 2, 3 * S], F32) for i in range(2)]
        PTs = [at(f"dPT{i}", EO + 42112 + i * 6144, [P, 12, P], F32) for i in range(2)]
        SM = at("dSM", EO + 54400, [P, 8, 4, 2], F32)
        QS = [TMP[:, :, i, 0:512] for i in range(2)]
        e0 = a_used[0]
        in1 = [single(G, MK[:, :, :], A["c_dil"], e0), single(G, RP[:, :, :, :], A["c_rope"], e0)]
        rs, rs_done, ready = prenorm(1, 0, 2)
        wv = A["a_wqkv_2"][0].rearrange("(k p) n -> p k n", p=P)
        blocks = [(512, lambda k0, k1, c=c: wv[:, k0:k1, c * 512:(c + 1) * 512]) for c in range(9)]
        qs = Ring(QS)
        qs.free = [[tmp_used[0]], [tmp_used[0]]]
        kt_done, vd_done = [], []

        def consume(b, slot, pair, tok):
            if b >= 6:
                for t in range(T):
                    a = C.put(lambda e, t=t: e.activation(VD[:, t, b - 6, :], pair[t], ACT.Copy,
                                                          scale=rs[:, t:t + 1]), tok, rs_done(), e0)
                vd_done.append(a)
                pairs.give(slot, a)
                return None
            n, x, free = qs.take()
            for t in range(T):
                a = C.put(lambda e, t=t: e.activation(x[:, t, :], pair[t], ACT.Copy, scale=rs[:, t:t + 1]),
                          tok, rs_done(), free)
            pairs.give(slot, a)
            v = rope(x, 8, RP, TR, a, in1, e0)

            def later():
                dst, g = (QT, b) if b < 3 else (KT, b - 3)
                for p in range(0, 4, 2):
                    tslot, bk, tfree = tbanks.take()
                    for i in range(2):
                        for t in range(T):
                            tok = PE.put(lambda e, p=p, i=i, t=t, bk=bk: e.transpose(
                                bk[:, i * S + t * P:i * S + (t + 1) * P],
                                x[:, t, (p + i) * P:(p + i + 1) * P], ident[:, :]),
                                tfree, v, a, mark=(i == 1 and t == 1))
                    w = V.put(lambda e, p=p, bk=bk: e.tensor_copy(
                        dst[:, 4 * g + p:4 * g + p + 2, :], bk.rearrange("p (i s) -> p i s", i=2)), tok, e0)
                    tbanks.give(tslot, w)
                    kt_done.append(w)
                qs.give(n, tok)

            return later

        x_used[0] = linear(XH, XL, DK, blocks, consume, ready, head=HEAD)
        flush()
        trs = Ring([bank(4), bank(6), bank(7)])
        trs.free = [pairs.free[2], tbanks.free[0], tbanks.free[1]]
        sfree, ofree = [pairs.free[0], pairs.free[1]], pairs.free[2]
        pr_ring, pt_ring = Ring(PS), Ring(PTs)
        pr_ring.free, pt_ring.free = [[kt_done[-1]]] * 2, [[e0]] * 2
        steps = [(pr, t) for t in range(T) for pr in range(4)]
        state, odone = {}, {}

        def score(i, u):
            pr, t = steps[i]
            if u == 0:
                state[i] = [pr_ring.take(), [None, None], None]
            hs = slice(u * HD, (u + 1) * HD)
            for g in range(3):
                o_ = banks_t[u][:, g * S:(g + 1) * S]
                PE.put(lambda e: e.matmul(
                    o_, QT[hs, 4 * g + pr, t * P:(t + 1) * P], KT[hs, 4 * g + pr, :],
                    start=True, stop=False), sfree[u], kt_done[-1], mark=False)
                tok = PE.put(lambda e: e.matmul(
                    o_, identb[:, :], MK[:, t, g * S:(g + 1) * S], start=False, stop=True),
                    in1, mark=(g == 2))
            mx, nm = SM[:, i, 0, u:u + 1], SM[:, i, 1, u:u + 1]
            v = V.put(lambda e: e.tensor_reduce(mx, banks_t[u][:, 0:3 * S], AX, ALU.max), tok, e0)
            state[i][1][u] = V.put(lambda e: e.tensor_scalar(nm, mx, -0.125, None, ALU.mult), v)

        def exp(i, u):
            (_, pp, pfree), maxed, _ = state[i]
            nm, den = SM[:, i, 1, u:u + 1], SM[:, i, 2, u:u + 1]
            sfree[u] = C.put(lambda e: e.activation(
                pp[:, u, :], banks_t[u][:, 0:3 * S], ACT.Exp, bias=nm, scale=0.125, accum_out=den),
                maxed[u], pfree)

        def scale(i):
            (_, pp, _), _, _ = state[i]
            done_ = []
            for u in range(2):
                den, rd, x = SM[:, i, 2, u:u + 1], SM[:, i, 3, u:u + 1], pp[:, u, :]
                v = V.put(lambda e: e.reciprocal(rd, den), sfree[u])
                done_.append(V.put(lambda e: e.tensor_scalar(x, x, rd, None, ALU.mult), v))
            state[i][2] = done_

        def turn(i):
            (m, pp, _), _, scaled = state[i]
            k, pt, tfree = pt_ring.take()
            ev = []
            for q in range(3):
                slot, bk, free = trs.take()
                for j in range(4 * q, 4 * q + 4):
                    u, jj = j // 6, j % 6
                    tok = PE.put(lambda e: e.transpose(
                        bk[:, (j % 4) * P:(j % 4 + 1) * P], pp[:, u, jj * P:(jj + 1) * P], ident[:, :]),
                        free, scaled[u], mark=(j % 4 == 3))
                src, dst = bk.rearrange("p (j n) -> p j n", n=P), pt[:, 4 * q:4 * q + 4, :]
                if q == 0:
                    w = V.put(lambda e: e.tensor_copy(dst, src), tok, tfree)
                else:
                    w = C.put(lambda e: e.activation(dst, src, ACT.Copy), tok, tfree)
                trs.give(slot, w)
                ev.append(w)
            pr_ring.give(m, tok)
            state[i] = [k, pt, ev]

        def output(i):
            nonlocal ofree
            pr, t = steps[i]
            k, pt, ev = state[i]
            for j in range(6):
                for u in range(2):
                    hd = 2 * pr + u
                    tok = PE.put(lambda e: e.matmul(
                        bank(5)[u * HD:(u + 1) * HD, 0:P], VD[:, j % 2, j // 2, hd * HD:(hd + 1) * HD],
                        pt[:, 6 * u + j, :], start=(j == 0), stop=(j == 5)), ofree, ev, vd_done[-1],
                        mark=(j == 5 and u == 1))
            pt_ring.give(k, tok)
            hi, lo = XH[:, pr, t * P:(t + 1) * P], XL[:, pr, t * P:(t + 1) * P]
            a = C.put(lambda e: e.activation(hi, bank(5)[:, 0:P], ACT.Copy), tok, x_used[0])
            v = V.put(lambda e: e.tensor_tensor(lo, bank(5)[:, 0:P], hi.bitcast(F32), ALU.subtract),
                      a, tok, x_used[0])
            ofree = [a, v]
            odone[(pr, t)] = [a, v]

        for n in range(10):
            if 1 <= n <= 8:
                scale(n - 1)
            if n < 8:
                score(n, 0)
                exp(n, 0)
                score(n, 1)
            if 1 <= n <= 8:
                turn(n - 1)
            if n < 8:
                exp(n, 1)
            if n >= 2:
                output(n - 2)
        pairs.free = [[sfree[0]], [sfree[1]], [[ofree, trs.free[0]]]]
        tbanks.free = [trs.free[1], trs.free[2]]
        tmp_used[0] = (PE.sem, PE.count)
        x_used[0] = project(XH, XL, 4, A["a_wo_2"][0], A["norm_g_2"][0, 3], 1.0, lambda k, t: odone[(k, t)],
                            (1, 0, 4), 2, 2)
        a_used[0] = [x_used[0], (V.sem, V.count)]

    def gqa():
        QT = at("qQT", EO, [P, 8, S], F32)
        KT = at("qKT", EO + 8192, [P, 4, S], F32)
        QS = at("qQS", EO + 12288, [P, T, 1536], F32)
        KD = at("qKD", EO + 24576, [P, T, 4, P], F32)
        MK = at("qMK", EO + 28672, [P, T, S], BF16)
        RP = at("qRP", EO + 29696, [P, 2, T, 8], F32)
        TR = at("qTR", EO + 29824, [P, 4, T, 160], F32)
        PTs = [at(f"qPT{i}", EO + 43136 + 4096 * i, [P, 2, 4, P], F32) for i in range(2)]
        SK = at("qSK", EO + 51328, [P, NH], F32)
        SM = at("qSM", EO + 51392, [P, 8, 20], F32)
        PS = [at(f"qPS{i}", TO + 4096 * i, [P, 4, S], F32) for i in range(2)]
        e0 = a_used[0]
        in1 = [single(G, MK[:, :, :], A["c_gqa"], e0), single(G, RP[:, :, :, :], A["c_rope"], e0),
               single(G, SK[:, :], A["b_sink_2"][0].partition_broadcast(P), e0)]
        rs, rs_done, ready = prenorm(1, 1, 2)
        wv = A["b_wqkv_2"][0].rearrange("(k p) n -> p k n", p=P)
        cols_ = (2, 0, 1)
        blocks = [(512, lambda k0, k1, c=c: wv[:, k0:k1, c * 512:(c + 1) * 512]) for c in cols_]
        turned, spots = [], [tbanks]

        def consume(b, slot, pair, tok):
            c = cols_[b]
            for t in range(T):
                a = C.put(lambda e: e.activation(QS[:, t, c * 512:(c + 1) * 512], pair[t], ACT.Copy,
                                                 scale=rs[:, t:t + 1]), tok[t], rs_done(), e0)
            pairs.give(slot, a)
            n = 4 if c == 2 else 8
            roped = []

            def turn_places():
                v = rope(QS[:, :, c * 512:c * 512 + n * HD], n, RP, TR, a, in1, e0)
                if c == 2:
                    for t in range(T):
                        for i in range(2):
                            v = C.put(lambda e: e.activation(
                                KD[:, t, :, i * HD:(i + 1) * HD],
                                QS[:, t, 1024:1280].rearrange("p (k n) -> p k n", n=HD), ACT.Copy), v, e0)
                roped.append(v)

            if b < 2:
                defer(ROPE, turn_places)
            else:
                turn_places()

            def later():
                while not roped:
                    hurry()
                v = roped[0]
                for p in range(0, 4, 2):
                    ring = spots[0]
                    slot, bk, free = ring.take()
                    for i in range(2):
                        for t in range(T):
                            src = KD[:, t, p + i, :] if c == 2 else QS[:, t, (4 * c + p + i) * P:(4 * c + p + i + 1) * P]
                            tok = PE.put(lambda e: e.transpose(
                                bk[:, i * S + t * P:i * S + (t + 1) * P], src, ident[:, :]),
                                free, v, mark=(i == 1 and t == 1))
                    dst = KT[:, p:p + 2, :] if c == 2 else QT[:, 4 * c + p:4 * c + p + 2, :]
                    w = C.put(lambda e: e.activation(dst, bk.rearrange("p (i s) -> p i s", i=2), ACT.Copy),
                              tok, e0)
                    ring.give(slot, w)
                    turned.append(w)

            return later

        x_used[0] = linear(XH, XL, DK, blocks, consume, ready, head=HEAD)
        sc = Ring([0, 1])
        sc.free = [pairs.free[0], pairs.free[1]]
        trs = Ring([bank(4), bank(6), bank(7)])
        trs.free = [pairs.free[2], tbanks.free[0], tbanks.free[1]]
        spots[0] = trs
        ofree = pairs.free[2]
        pr_ring, pt_ring = Ring(PS), Ring(PTs)
        pr_ring.free = [[tmp_used[0]], [tmp_used[0]]]
        pt_ring.free = [[e0], [e0]]
        steps = [(kv, t) for t in range(T) for kv in range(4)]
        state, odone = {}, {}

        def small(i):
            return (SM[:, i, 4 * c:4 * c + 4] for c in range(5))

        def score(i):
            kv, t = steps[i]
            n, s_, free = sc.take()
            for j in range(4):
                hd = 4 * kv + j
                hs = slice((hd % 2) * HD, (hd % 2) * HD + HD)
                at_ = (j % 2) * 2 + j // 2
                o_ = banks_t[s_][:, at_ * S:(at_ + 1) * S]
                PE.put(lambda e: e.matmul(
                    o_, QT[hs, hd // 2, t * P:(t + 1) * P], KT[hs, kv, :], start=True, stop=False),
                    free, turned[-1], mark=False)
                tok = PE.put(lambda e: e.matmul(
                    o_, identb[:, :], MK[:, t, :], start=False, stop=True), in1, mark=(j == 3))
            mx, nm, den, es, rd = small(i)
            sk = SK[:, 4 * kv:4 * kv + 4].rearrange("p (a b) -> p b a", b=2)
            ba = lambda x: x.rearrange("p (b a) -> p b a", b=2)
            v = V.put(lambda e: e.tensor_reduce(mx, banks_t[s_][:, :].rearrange("p (j s) -> p j s", j=4),
                                                AX, ALU.max), tok, e0)
            v = V.put(lambda e: e.scalar_tensor_tensor(ba(mx), ba(mx), 0.125, sk, ALU.mult, ALU.max), v, in1)
            v0 = V.put(lambda e: e.tensor_scalar(nm, mx, -1.0, None, ALU.mult), v)
            v = V.put(lambda e: e.tensor_tensor(ba(es), sk, ba(nm), ALU.add), v0)
            state[i] = [n, s_, v0, v]

        def exp(i):
            n, s_, v0, v = state[i]
            mx, nm, den, es, rd = small(i)
            m, pp, pfree = pr_ring.take()
            for j in range(4):
                a = C.put(lambda e: e.activation(
                    pp[:, j, :], banks_t[s_][:, j * S:(j + 1) * S], ACT.Exp, bias=nm[:, j:j + 1], scale=0.125,
                    accum_out=den[:, j:j + 1]), v0, pfree)
            sc.give(n, a)
            a2 = C.put(lambda e: e.activation(es, es, ACT.Exp), v)
            state[i] = [m, pp, a, a2]

        def scale(i):
            m, pp, a, a2 = state[i]
            mx, nm, den, es, rd = small(i)
            v = V.put(lambda e: e.tensor_tensor(den, den, es, ALU.add), a2, a)
            v = V.put(lambda e: e.reciprocal(rd, den), v)
            v = V.put(lambda e: e.tensor_tensor(
                pp[:, :, :], pp[:, :, :], rd.unsqueeze(2).broadcast_to([P, 4, S]), ALU.mult), v)
            state[i] = [m, pp, v]

        def turn(i):
            m, pp, scaled = state[i]
            k, pt, tfree = pt_ring.take()
            ev = []
            for kt in range(2):
                slot, bk, free = trs.take()
                for j in range(4):
                    tok = PE.put(lambda e: e.transpose(
                        bk[:, j * P:(j + 1) * P], pp[:, j, kt * P:(kt + 1) * P], ident[:, :]),
                        free, scaled, mark=(j == 3))
                src = bk.rearrange("p (j n) -> p j n", n=P)
                if kt == 0:
                    w = V.put(lambda e: e.tensor_copy(pt[:, 0, :, :], src), tok, tfree)
                else:
                    w = C.put(lambda e: e.activation(pt[:, 1, :, :], src, ACT.Copy), tok, tfree)
                trs.give(slot, w)
                ev.append(w)
            pr_ring.give(m, tok)
            state[i] = [k, pt, ev]

        def output(i):
            nonlocal ofree
            kv, t = steps[i]
            k, pt, ev = state[i]
            for kt in range(2):
                for u in range(2):
                    tok = PE.put(lambda e: e.matmul(
                        bank(5)[u * HD:(u + 1) * HD, 0:S], QS[:, kt, 1280 + kv * HD:1280 + (kv + 1) * HD],
                        pt[:, kt, 2 * u:2 * u + 2, :], start=(kt == 0), stop=(kt == 1)), ofree, ev,
                        mark=(kt == 1 and u == 1))
            pt_ring.give(k, tok)
            hi, lo = (x[:, 2 * kv:2 * kv + 2, t * P:(t + 1) * P] for x in (XH, XL))
            b2 = bank(5)[:, 0:S].rearrange("p (a s) -> p a s", a=2)
            a = C.put(lambda e: e.activation(hi, b2, ACT.Copy), tok, x_used[0])
            v = V.put(lambda e: e.tensor_tensor(lo, b2, hi.bitcast(F32), ALU.subtract), a, tok, x_used[0])
            ofree = [a, v]
            for a_ in range(2):
                odone[(2 * kv + a_, t)] = [a, v]

        for n in range(10):
            if 1 <= n <= 8:
                scale(n - 1)
            if n == 2:
                flush()
            if n < 8:
                score(n)
            if 1 <= n <= 8:
                turn(n - 1)
            if n < 8:
                exp(n)
            if n >= 2:
                output(n - 2)
        pairs.free = [[sc.free[0]], [sc.free[1]], [[ofree, trs.free[0]]]]
        tbanks.free = [trs.free[1], trs.free[2]]
        tmp_used[0] = (PE.sem, PE.count)
        x_used[0] = project(XH, XL, DK, A["b_wo_2"][0], A["norm_g_2"][1, 3], 1.0, lambda k, t: odone[(k, t)],
                            (1, 1, 4), 4, 4)
        a_used[0] = [x_used[0], (V.sem, V.count)]

    todo = []
    for block, names, mixers in (
            (0, ("ffn_w13", "ffn_w2", "norm_g", "p", "ple_w_gate", "ple_w_proj"), (gmlp, rwkv)),
            (1, ("ffn_wi_2", "ffn_wo_2", "norm_g_2", "p_2", "ple_gate_2", "ple_proj_2"), (dilated, gqa))):
        w13, w2, ng, p, wg, wp = (A[n] for n in names)
        for layer in range(2):
            mixer = None if mixers[layer] is rwkv else (block, layer, 2)
            after = [(0, 1, 0), (1, 0, 0), (1, 1, 0), None][2 * block + layer]
            todo.append(lambda f=(w13[layer, 0], w2[layer, 0], ng), b=block, l=layer, n=mixer:
                        ffn(b, l, 0, *f, n))
            todo.append(mixers[layer])

            def last_ffn(b=block, l=layer, f=(w13[layer, 1], w2[layer, 1], ng), p=p):
                defer(40, ple_input(l, p))
                ffn(b, l, 1, *f, (b, l, 6))

            todo.append(last_ffn)
            todo.append(lambda b=block, l=layer, f=(p, wg, wp, ng), n=after: ple(b, l, *f, n))
    which = range(stages) if isinstance(stages, int) else stages
    if which[0] != 0:
        while deferred:
            hurry()
    for n in which:
        if n < len(todo):
            todo[n]()

    s_out = sem("d_out")
    for t in range(T):
        SP.wait(h_done[t])
        SP.ops.append(lambda e, t=t: e.dma_start(out[0, t * P:(t + 1) * P, :], H[:, t, :]).then_inc(s_out, 16))
    SP.ops.append(lambda e: e.wait_ge(s_out, 16 * T))
    return {"sp": SP, "pe": PE, "v": V, "a": C, "g": G}


_INS = ["x", "p", "norm_g", "ffn_w13", "ffn_w2", "ple_w_gate", "ple_w_proj", "a_w_in", "a_b_in", "a_v_gain",
        "a_w_s", "a_b_s", "a_w_out", "b_mu", "b_w_in", "b_w0", "b_w1", "b_w2", "b_a0", "b_a1", "b_a2", "b_g1",
        "b_g2", "b_k_k", "b_k_a", "b_r_k", "b_lnx", "b_w_out", "p_2", "norm_g_2", "ffn_wi_2", "ffn_wo_2",
        "ple_proj_2", "ple_gate_2", "a_wqkv_2", "a_wo_2", "b_wqkv_2", "b_wo_2", "b_sink_2"]


def kernel(**inputs):
    import numpy as _np
    import concourse.bacc as _bacc
    from concourse import mybir as _mybir
    from concourse.bass_utils import run_bass_kernel_spmd as _run

    nc = _bacc.Bacc("TRN2", target_bir_lowering=False, num_devices=1)
    given = {name: _np.ascontiguousarray(inputs[name]) for name in _INS}
    given.update(constants())
    arrays, args = {}, {}
    for name, a in given.items():
        arrays[f"in_{name}_dram"] = a
        args[name] = nc.dram_tensor(f"in_{name}_dram", a.shape, _mybir.dt.from_np(a.dtype),
                                    kind="ExternalInput").ap()
    out = nc.dram_tensor("out_0_dram", (1, S, D), F32, kind="ExternalOutput").ap()
    program(nc, args, out)
    r = _run(nc, [arrays], core_ids=[0])
    return r.results[0]["out_0_dram"]
```
